# Optimizing a Trainium2 kernel written in Bass

```python
import jax, jax.numpy as jnp
from jax import lax
import numpy as np
import jax
import jax.numpy as jnp

D_MODEL = 1024
BATCH = 1
SEQ = 512
DEPTH = 1

GRID_W = 64
CTX_LEN = 256
MIX_WIDTH = D_MODEL // 2
HEAD_DIM = 64
GQA_HEADS = MIX_WIDTH // HEAD_DIM
GQA_KV_HEADS = GQA_HEADS // 4
NA_HEADS = MIX_WIDTH // HEAD_DIM
NA_WIN_ROWS = 8
NA_WIN_COLS = 16
FOURIER_WIDTH = MIX_WIDTH
FOURIER_GROUPS = 4
FOURIER_GROUP_DIM = FOURIER_WIDTH // FOURIER_GROUPS
CONV_WIDTH = MIX_WIDTH
CONV_KERNEL = 31
N_BRANCHES = 4
N_EXPERTS = 16
N_EXPERT_GROUPS = 4
EXPERTS_PER_GROUP = N_EXPERTS // N_EXPERT_GROUPS
TOP_K = 2
EXPERT_FF = D_MODEL // 2
Q_BLOCK = 128
ROPE_THETA = 10000.0
EPS = 1e-6
ATTN_SCALE = HEAD_DIM ** -0.5

GQA_Q_WIDTH = GQA_HEADS * HEAD_DIM
GQA_KV_WIDTH = GQA_KV_HEADS * HEAD_DIM
NA_WIDTH = NA_HEADS * HEAD_DIM
PROJ_SIZES = (GQA_Q_WIDTH, GQA_KV_WIDTH, GQA_KV_WIDTH, NA_WIDTH, NA_WIDTH, NA_WIDTH,
              FOURIER_WIDTH, 2 * CONV_WIDTH, N_BRANCHES * D_MODEL)
PROJ_SPLITS = tuple(int(v) for v in np.cumsum(PROJ_SIZES)[:-1])
IN_WIDTH = sum(PROJ_SIZES)


def rms_norm(x, g):
    xf = x.astype(jnp.float32)
    y = xf * lax.rsqrt(jnp.mean(xf * xf, axis=-1, keepdims=True) + EPS)
    return (y * g.astype(jnp.float32)).astype(x.dtype)

def axial_rope(n_tokens):
    t = jnp.arange(n_tokens, dtype=jnp.int32)
    row = (t // GRID_W).astype(jnp.float32)
    col = (t % GRID_W).astype(jnp.float32)
    n_pairs = HEAD_DIM // 4
    inv_freq = ROPE_THETA ** (-jnp.arange(n_pairs, dtype=jnp.float32) / n_pairs)
    ang = jnp.concatenate([row[:, None] * inv_freq, col[:, None] * inv_freq], axis=-1)
    return jnp.cos(ang), jnp.sin(ang)

def apply_rope(x, cos, sin):
    xf = x.astype(jnp.float32).reshape(*x.shape[:-1], HEAD_DIM // 2, 2)
    x1, x2 = xf[..., 0], xf[..., 1]
    c = cos[None, :, None, :]
    s = sin[None, :, None, :]
    return jnp.stack([x1 * c - x2 * s, x1 * s + x2 * c], axis=-1).reshape(x.shape).astype(x.dtype)

def attend(qg, k, v):
    s = jnp.einsum('bqhgd,bkhd->bhgqk', qg, k, preferred_element_type=jnp.float32) * ATTN_SCALE
    p = jax.nn.softmax(s, axis=-1).astype(v.dtype)
    return jnp.einsum('bhgqk,bkhd->bqhgd', p, v)

def dense_attention(q, k, v):
    B, L, hq, _ = q.shape
    hkv = k.shape[2]
    out = attend(q.reshape(B, L, hkv, hq // hkv, HEAD_DIM), k, v)
    return out.reshape(B, L, hq * HEAD_DIM)

def gqa_latent(q, k, v, k_ctx, v_ctx):
    B, S = q.shape[:2]
    g = GQA_HEADS // GQA_KV_HEADS
    k_all = jnp.concatenate([k, k_ctx], axis=1)
    v_all = jnp.concatenate([v, v_ctx], axis=1)
    nb = S // Q_BLOCK
    qb = q.reshape(B, nb, Q_BLOCK, GQA_KV_HEADS, g, HEAD_DIM).transpose(1, 0, 2, 3, 4, 5)
    out = lax.map(lambda qblk: attend(qblk, k_all, v_all), qb)
    return out.transpose(1, 0, 2, 3, 4, 5).reshape(B, S, GQA_Q_WIDTH)

def neighbourhood_latent(q, k, v, k_ctx, v_ctx, rpb):
    B, S = q.shape[:2]
    rows = S // GRID_W
    wr = min(NA_WIN_ROWS, rows)
    qg = q.reshape(B, rows, GRID_W, NA_HEADS, HEAD_DIM)
    kg = k.reshape(B, rows, GRID_W, NA_HEADS, HEAD_DIM)
    vg = v.reshape(B, rows, GRID_W, NA_HEADS, HEAD_DIM)
    cols = np.arange(GRID_W)
    col_start = np.clip(cols - NA_WIN_COLS // 2, 0, GRID_W - NA_WIN_COLS)
    col_idx = col_start[:, None] + np.arange(NA_WIN_COLS)[None, :]
    col_bias_idx = col_idx - cols[:, None] + (NA_WIN_COLS - 1)
    row_starts = jnp.clip(jnp.arange(rows) - NA_WIN_ROWS // 2, 0, rows - wr)
    rpb_f = rpb.astype(jnp.float32)
    n_win = wr * NA_WIN_COLS

    def row_block(args):
        r, r0, q_row = args
        k_band = lax.dynamic_slice_in_dim(kg, r0, wr, axis=1)
        v_band = lax.dynamic_slice_in_dim(vg, r0, wr, axis=1)
        k_win = k_band[:, :, col_idx]
        v_win = v_band[:, :, col_idx]
        s_win = jnp.einsum('bqhd,bwqjhd->bhqwj', q_row, k_win,
                           preferred_element_type=jnp.float32) * ATTN_SCALE
        row_bias_idx = r0 + jnp.arange(wr) - r + (NA_WIN_ROWS - 1)
        bias = rpb_f[:, row_bias_idx][:, :, col_bias_idx]
        s_win = s_win + bias.transpose(0, 2, 1, 3)[None]
        s_ctx = jnp.einsum('bqhd,bkhd->bhqk', q_row, k_ctx,
                           preferred_element_type=jnp.float32) * ATTN_SCALE
        s = jnp.concatenate([s_win.reshape(B, NA_HEADS, GRID_W, n_win), s_ctx], axis=-1)
        p = jax.nn.softmax(s, axis=-1).astype(v.dtype)
        p_win = p[..., :n_win].reshape(B, NA_HEADS, GRID_W, wr, NA_WIN_COLS)
        p_ctx = p[..., n_win:]
        return (jnp.einsum('bhqwj,bwqjhd->bqhd', p_win, v_win)
                + jnp.einsum('bhqk,bkhd->bqhd', p_ctx, v_ctx))

    out = lax.map(row_block, (jnp.arange(rows), row_starts, qg.transpose(1, 0, 2, 3, 4)))
    return out.transpose(1, 0, 2, 3, 4).reshape(B, S, NA_WIDTH)

def fourier_mix(u):
    B, L = u.shape[:2]
    ug = u.astype(jnp.float32).reshape(B, L, FOURIER_GROUPS, FOURIER_GROUP_DIM)
    y = jnp.fft.fft2(ug, axes=(1, 3), norm='ortho').real
    return y.reshape(B, L, FOURIER_WIDTH).astype(u.dtype)

def conformer_conv(u, conv_w, conv_b, conv_g):
    a, b = jnp.split(u, 2, axis=-1)
    z = a * jax.nn.sigmoid(b)
    z = lax.conv_general_dilated(z, conv_w[:, None, :], window_strides=(1,),
                                 padding=[(CONV_KERNEL // 2, CONV_KERNEL // 2)],
                                 dimension_numbers=('NWC', 'WIO', 'NWC'),
                                 feature_group_count=CONV_WIDTH) + conv_b
    return jax.nn.silu(rms_norm(z, conv_g))

def merge_branches(branches, gate_logits, w_branch, w_out):
    y = jnp.stack(branches, axis=-2)
    z = jnp.einsum('blnc,ncd->blnd', y, w_branch)
    g = jax.nn.sigmoid(gate_logits.reshape(*gate_logits.shape[:-1], N_BRANCHES, D_MODEL)
                       .astype(jnp.float32)).astype(z.dtype)
    return jnp.sum(g * z, axis=-2) @ w_out

def token_mixer(h, hc, w_in, q_g, k_g, rpb, conv_w, conv_b, conv_g, w_branch, w_out, cos, sin, update_ctx):
    B, S, _ = h.shape
    C = hc.shape[1]
    gq, gk, gv, nq, nk, nv, fu, cu, gl = jnp.split(h @ w_in, PROJ_SPLITS, axis=-1)
    cgq, cgk, cgv, cnq, cnk, cnv, cfu, ccu, cgl = jnp.split(hc @ w_in, PROJ_SPLITS, axis=-1)
    q = apply_rope(rms_norm(gq.reshape(B, S, GQA_HEADS, HEAD_DIM), q_g), cos, sin)
    k = apply_rope(rms_norm(gk.reshape(B, S, GQA_KV_HEADS, HEAD_DIM), k_g), cos, sin)
    v = gv.reshape(B, S, GQA_KV_HEADS, HEAD_DIM)
    kc = rms_norm(cgk.reshape(B, C, GQA_KV_HEADS, HEAD_DIM), k_g)
    vc = cgv.reshape(B, C, GQA_KV_HEADS, HEAD_DIM)
    y_gqa = gqa_latent(q, k, v, kc, vc)
    nkc = cnk.reshape(B, C, NA_HEADS, HEAD_DIM)
    nvc = cnv.reshape(B, C, NA_HEADS, HEAD_DIM)
    y_na = neighbourhood_latent(nq.reshape(B, S, NA_HEADS, HEAD_DIM), nk.reshape(B, S, NA_HEADS, HEAD_DIM),
                                nv.reshape(B, S, NA_HEADS, HEAD_DIM), nkc, nvc, rpb)
    y_fn = fourier_mix(fu)
    y_cv = conformer_conv(cu, conv_w, conv_b, conv_g)
    out = merge_branches((y_gqa, y_na, y_fn, y_cv), gl, w_branch, w_out)
    if not update_ctx:
        return out, None
    qc = rms_norm(cgq.reshape(B, C, GQA_HEADS, HEAD_DIM), q_g)
    yc_gqa = dense_attention(qc, kc, vc)
    yc_na = dense_attention(cnq.reshape(B, C, NA_HEADS, HEAD_DIM), nkc, nvc)
    yc_fn = fourier_mix(cfu)
    yc_cv = conformer_conv(ccu, conv_w, conv_b, conv_g)
    out_c = merge_branches((yc_gqa, yc_na, yc_fn, yc_cv), cgl, w_branch, w_out)
    return out, out_c

def moe(h, w_router, router_bias, w_gu, w_down):
    lead = h.shape[:-1]
    t = h.reshape(-1, D_MODEL)
    scores = jax.nn.sigmoid((t @ w_router).astype(jnp.float32))
    sel = scores + router_bias.astype(jnp.float32)
    group_score = lax.top_k(sel.reshape(-1, N_EXPERT_GROUPS, EXPERTS_PER_GROUP), TOP_K)[0].sum(-1)
    g_idx = jnp.argmax(group_score, axis=-1)
    in_group = (jnp.arange(N_EXPERTS) // EXPERTS_PER_GROUP)[None, :] == g_idx[:, None]
    _, top_idx = lax.top_k(jnp.where(in_group, sel, -jnp.inf), TOP_K)
    w = jnp.take_along_axis(scores, top_idx, axis=-1)
    w = w / jnp.sum(w, axis=-1, keepdims=True)
    gate = jnp.sum(jax.nn.one_hot(top_idx, N_EXPERTS, dtype=jnp.float32) * w[..., None], axis=1).astype(t.dtype)
    out = jnp.zeros_like(t)
    for e in range(N_EXPERTS):
        a, b = jnp.split(t @ w_gu[e], 2, axis=-1)
        out = out + gate[:, e:e + 1] * ((jax.nn.silu(a) * b) @ w_down[e])
    return out.reshape(*lead, D_MODEL)

def first_inputs(seed: int = 0) -> dict:
    key = jax.random.key(seed)
    ks = jax.random.split(key, 22)
    D = D_MODEL

    def nrm(k, shape, std):
        return jax.random.normal(k, shape, jnp.float32) * std

    return {
        "x": nrm(ks[0], (BATCH, SEQ, D), 1.0),
        "c": nrm(ks[1], (BATCH, D), 1.0),
        "ctx": nrm(ks[2], (BATCH, CTX_LEN, D), 1.0),
        "c_ctx": nrm(ks[3], (D,), 1.0),
        "w_mod": nrm(ks[4], (DEPTH, D, 6 * D), 0.5 * D ** -0.5),
        "b_mod": nrm(ks[5], (DEPTH, 6 * D), 0.02),
        "norm1_g": 1.0 + nrm(ks[6], (DEPTH, D), 0.02),
        "norm2_g": 1.0 + nrm(ks[7], (DEPTH, D), 0.02),
        "w_in": nrm(ks[8], (DEPTH, D, IN_WIDTH), D ** -0.5),
        "q_norm_g": 1.0 + nrm(ks[9], (DEPTH, HEAD_DIM), 0.02),
        "k_norm_g": 1.0 + nrm(ks[10], (DEPTH, HEAD_DIM), 0.02),
        "na_rpb": nrm(ks[11], (DEPTH, NA_HEADS, 2 * NA_WIN_ROWS - 1, 2 * NA_WIN_COLS - 1), 0.02),
        "conv_w": nrm(ks[12], (DEPTH, CONV_KERNEL, CONV_WIDTH), CONV_KERNEL ** -0.5),
        "conv_b": nrm(ks[13], (DEPTH, CONV_WIDTH), 0.01),
        "conv_norm_g": 1.0 + nrm(ks[14], (DEPTH, CONV_WIDTH), 0.02),
        "w_branch": nrm(ks[15], (DEPTH, N_BRANCHES, MIX_WIDTH, D), MIX_WIDTH ** -0.5),
        "w_out": nrm(ks[16], (DEPTH, D, D), D ** -0.5),
        "w_router": nrm(ks[17], (D, N_EXPERTS), D ** -0.5),
        "router_bias": nrm(ks[18], (N_EXPERTS,), 0.01),
        "w_expert_gu": nrm(ks[19], (DEPTH, N_EXPERTS, D, 2 * EXPERT_FF), D ** -0.5),
        "w_expert_down": nrm(ks[20], (DEPTH, N_EXPERTS, EXPERT_FF, D), EXPERT_FF ** -0.5),
        "final_norm_g": 1.0 + nrm(ks[21], (D,), 0.02),
    }

def first_block(x, c, ctx, c_ctx, w_mod, b_mod, norm1_g, norm2_g, w_in, q_norm_g, k_norm_g, na_rpb,
              conv_w, conv_b, conv_norm_g, w_branch, w_out, w_router, router_bias,
              w_expert_gu, w_expert_down, final_norm_g):
    S = x.shape[1]
    cos, sin = axial_rope(S)
    xc = ctx
    for l in range(DEPTH):
        update_ctx = l < DEPTH - 1
        m = jax.nn.silu(c) @ w_mod[l] + b_mod[l]
        sh1, sc1, g1, sh2, sc2, g2 = [t[:, None, :] for t in jnp.split(m, 6, axis=-1)]
        mc = jax.nn.silu(c_ctx) @ w_mod[l] + b_mod[l]
        csh1, csc1, cg1, csh2, csc2, cg2 = jnp.split(mc, 6, axis=-1)
        h = rms_norm(x, norm1_g[l]) * (1.0 + sc1) + sh1
        hc = rms_norm(xc, norm1_g[l]) * (1.0 + csc1) + csh1
        y, yc = token_mixer(h, hc, w_in[l], q_norm_g[l], k_norm_g[l], na_rpb[l], conv_w[l], conv_b[l],
                            conv_norm_g[l], w_branch[l], w_out[l], cos, sin, update_ctx)
        x = x + g1 * y
        h2 = rms_norm(x, norm2_g[l]) * (1.0 + sc2) + sh2
        if update_ctx:
            xc = xc + cg1 * yc
            h2c = rms_norm(xc, norm2_g[l]) * (1.0 + csc2) + csh2
            z = moe(jnp.concatenate([h2, h2c], axis=1), w_router, router_bias, w_expert_gu[l], w_expert_down[l])
            x = x + g2 * z[:, :S]
            xc = xc + cg2 * z[:, S:]
        else:
            x = x + g2 * moe(h2, w_router, router_bias, w_expert_gu[l], w_expert_down[l])
    return rms_norm(x, final_norm_g)


DEPTH_2 = 2

RET_HEADS = 4
DSA_HEADS = 4
DIL_HEADS = 8
RET_W = RET_HEADS * HEAD_DIM
DSA_W = DSA_HEADS * HEAD_DIM
DIL_W = DIL_HEADS * HEAD_DIM
D_MIX = RET_W + DSA_W + DIL_W
RET_CHUNK = 128
RET_ROPE_BASE = 10000.0
KV_LATENT = 128
IDX_HEADS = 8
IDX_DIM = 64
TOPK_MAX = 256
QUERY_BLOCK = 128
DIL_PATTERNS = ((128, 1), (512, 4), (2048, 16))
D_FF = 4 * D_MODEL
NORM_EPS = 1e-6
RET_COLS = 4 * RET_W
DSA_SIZES = (DSA_W, KV_LATENT, IDX_HEADS * IDX_DIM, IDX_DIM, IDX_HEADS)
DSA_COLS = sum(DSA_SIZES)
DIL_COLS = 3 * DIL_W
N_IN = RET_COLS + DSA_COLS + DIL_COLS


def _offsets(sizes):
    return [int(o) for o in np.cumsum(sizes)[:-1]]

def rms_norm_2(x, w):
    xf = x.astype(jnp.float32)
    y = xf * lax.rsqrt(jnp.mean(xf * xf, axis=-1, keepdims=True) + NORM_EPS)
    return (y * w.astype(jnp.float32)).astype(x.dtype)

def rotary(x, pos):
    half = x.shape[-1] // 2
    inv = RET_ROPE_BASE ** (-jnp.arange(half, dtype=jnp.float32) / half)
    ang = pos.astype(jnp.float32)[:, None] * inv[None, :]
    cos = jnp.cos(ang)[None, :, None, :]
    sin = jnp.sin(ang)[None, :, None, :]
    xf = x.astype(jnp.float32)
    x1, x2 = xf[..., :half], xf[..., half:]
    return jnp.concatenate([x1 * cos - x2 * sin, x2 * cos + x1 * sin], axis=-1)

def retention_chunkwise(q, k, v):
    B, S, H, d = q.shape
    C = RET_CHUNK
    N = S // C
    log_g = jnp.log(1.0 - 2.0 ** (-5.0 - jnp.arange(H, dtype=jnp.float32)))

    def chunks(t):
        return t.reshape(B, N, C, H, d).transpose(0, 3, 1, 2, 4)

    qc, kc, vc = chunks(q), chunks(k * (d ** -0.5)), chunks(v)
    i = jnp.arange(C, dtype=jnp.float32)
    diff = i[:, None] - i[None, :]
    decay = jnp.exp(jnp.maximum(diff, 0.0)[None] * log_g[:, None, None]) * (diff >= 0)[None]
    inner = jnp.einsum('bhncd,bhnmd->bhncm', qc, kc) * decay[None, :, None]
    inner = jnp.einsum('bhncm,bhnme->bhnce', inner, vc)
    zeta = jnp.exp((C - 1.0 - i)[None, :] * log_g[:, None])
    xi = jnp.exp((i + 1.0)[None, :] * log_g[:, None])
    kv = jnp.einsum('bhnmd,bhnme->nbhde', kc * zeta[None, :, None, :, None], vc)
    g_chunk = jnp.exp(C * log_g)[None, :, None, None]

    def step(state, kv_n):
        return g_chunk * state + kv_n, state

    _, state_prev = lax.scan(step, jnp.zeros((B, H, d, d), jnp.float32), kv)
    cross = jnp.einsum('bhncd,nbhde->bhnce', qc, state_prev) * xi[None, :, None, :, None]
    o = inner + cross
    return o.transpose(0, 2, 3, 1, 4).reshape(B, S, H, d)

def retention_mixer(cols, norm_w, pos):
    B, S, _ = cols.shape
    q, k, v, g = jnp.split(cols, 4, axis=-1)
    shp = (B, S, RET_HEADS, HEAD_DIM)
    o = retention_chunkwise(rotary(q.reshape(shp), pos), rotary(k.reshape(shp), pos),
                            v.reshape(shp).astype(jnp.float32))
    mu = jnp.mean(o, axis=-1, keepdims=True)
    var = jnp.mean(jnp.square(o - mu), axis=-1, keepdims=True)
    o = (o - mu) * lax.rsqrt(var + NORM_EPS) * norm_w.astype(jnp.float32)
    o = o.reshape(B, S, RET_W)
    return (jax.nn.silu(g.astype(jnp.float32)) * o).astype(cols.dtype)

def dsa_mixer(cols, kv_norm_w, w_uk, w_uv):
    B, S, _ = cols.shape
    q, c_kv, q_idx, k_idx, w_idx = jnp.split(cols, _offsets(DSA_SIZES), axis=-1)
    q = q.reshape(B, S, DSA_HEADS, HEAD_DIM)
    c_kv = rms_norm_2(c_kv, kv_norm_w)
    k = (c_kv @ w_uk).reshape(B, S, DSA_HEADS, HEAD_DIM)
    v = (c_kv @ w_uv).reshape(B, S, DSA_HEADS, HEAD_DIM)
    q_idx = q_idx.reshape(B, S, IDX_HEADS, IDX_DIM)
    w_idx = w_idx * (IDX_HEADS ** -0.5 * IDX_DIM ** -0.5)
    n_sel = min(TOPK_MAX, S // 4)
    nblk = S // QUERY_BLOCK
    key_pos = jnp.arange(S)

    def to_blocks(t):
        return jnp.moveaxis(t.reshape((B, nblk, QUERY_BLOCK) + t.shape[2:]), 1, 0)

    def block(args):
        qb, qib, wb, start = args
        qpos = start + jnp.arange(QUERY_BLOCK)
        logits = jnp.einsum('bqhd,bsd->bqhs', qib, k_idx)
        score = jnp.einsum('bqhs,bqh->bqs', jax.nn.relu(logits), wb).astype(jnp.float32)
        causal = key_pos[None, :] <= qpos[:, None]
        score = jnp.where(causal[None], score, -jnp.inf)
        _, idx = lax.top_k(score, n_sel)
        k_sel = jax.vmap(lambda kb, ib: kb[ib])(k, idx)
        v_sel = jax.vmap(lambda vb, ib: vb[ib])(v, idx)
        s = jnp.einsum('bqhd,bqnhd->bhqn', qb, k_sel).astype(jnp.float32) * (HEAD_DIM ** -0.5)
        valid = (idx <= qpos[None, :, None])[:, None]
        p = jax.nn.softmax(jnp.where(valid, s, -jnp.inf), axis=-1).astype(v.dtype)
        return jnp.einsum('bhqn,bqnhd->bqhd', p, v_sel)

    starts = jnp.arange(nblk) * QUERY_BLOCK
    o = lax.map(block, (to_blocks(q), to_blocks(q_idx), to_blocks(w_idx), starts))
    return jnp.moveaxis(o, 0, 1).reshape(B, S, DSA_W).astype(cols.dtype)

def dilated_branch(q, k, v, window, dilation):
    B, S, H, d = q.shape
    steps = window // dilation
    n = S // dilation
    lb = min(steps, n)
    nb = -(-n // lb)
    pad = nb * lb - n

    def to_sub(t):
        t = t.reshape(B, n, dilation, H, d).transpose(0, 2, 3, 1, 4)
        t = jnp.pad(t, ((0, 0), (0, 0), (0, 0), (0, pad), (0, 0)))
        return t.reshape(B, dilation, H, nb, lb, d)

    def with_prev(t):
        prev = jnp.pad(t, ((0, 0), (0, 0), (0, 0), (1, 0), (0, 0), (0, 0)))[:, :, :, :-1]
        return jnp.concatenate([prev, t], axis=4)

    qs = to_sub(q)
    kk = with_prev(to_sub(k))
    vv = with_prev(to_sub(v)).astype(jnp.float32)
    qi = jnp.arange(lb)[:, None]
    kj = jnp.arange(2 * lb)[None, :]
    dist = lb + qi - kj
    key_idx = jnp.arange(nb)[:, None, None] * lb - lb + kj[None]
    mask = (dist >= 0) & (dist <= steps) & (key_idx >= 0)
    s = jnp.einsum('brhnqd,brhnkd->brhnqk', qs, kk).astype(jnp.float32) * (d ** -0.5)
    s = jnp.where(mask, s, -jnp.inf)
    m = jnp.max(s, axis=-1, keepdims=True)
    p = jnp.exp(s - m)
    den = jnp.sum(p, axis=-1, keepdims=True)
    o = jnp.einsum('brhnqk,brhnkd->brhnqd', p, vv) / den
    lse = (m + jnp.log(den))[..., 0]
    o = o.reshape(B, dilation, H, nb * lb, d)[:, :, :, :n].transpose(0, 3, 1, 2, 4).reshape(B, S, H, d)
    lse = lse.reshape(B, dilation, H, nb * lb)[:, :, :, :n].transpose(0, 3, 1, 2).reshape(B, S, H)
    return o, lse

def dilated_mixer(cols):
    B, S, _ = cols.shape
    q, k, v = jnp.split(cols, 3, axis=-1)
    shp = (B, S, DIL_HEADS, HEAD_DIM)
    q, k, v = q.reshape(shp), k.reshape(shp), v.reshape(shp)
    outs = []
    lses = []
    for window, dilation in DIL_PATTERNS:
        o, lse = dilated_branch(q, k, v, window, dilation)
        outs.append(o)
        lses.append(lse)
    alpha = jax.nn.softmax(jnp.stack(lses, axis=0), axis=0)
    o = jnp.sum(alpha[..., None] * jnp.stack(outs, axis=0), axis=0)
    return o.reshape(B, S, DIL_W).astype(cols.dtype)

def hybrid_layer(x, attn_norm_w, w_in, ret_norm_w, kv_norm_w, w_uk, w_uv, w_out, mlp_norm_w, w_up, w_down, pos):
    h = rms_norm_2(x, attn_norm_w)
    proj = h @ w_in
    ret_cols, dsa_cols, dil_cols = jnp.split(proj, _offsets((RET_COLS, DSA_COLS, DIL_COLS)), axis=-1)
    mixed = jnp.concatenate([retention_mixer(ret_cols, ret_norm_w, pos),
                             dsa_mixer(dsa_cols, kv_norm_w, w_uk, w_uv),
                             dilated_mixer(dil_cols)], axis=-1)
    x = x + mixed @ w_out
    h = rms_norm_2(x, mlp_norm_w)
    return x + jnp.square(jax.nn.relu(h @ w_up)) @ w_down

def second_inputs(seed: int = 0) -> dict:
    key = jax.random.key(seed)
    ks = jax.random.split(key, 12)
    f32 = jnp.float32

    def nrm(k, shape, scale):
        return jax.random.normal(k, shape, f32) * scale

    return {
        'x': nrm(ks[0], (BATCH, SEQ, D_MODEL), 1.0),
        'attn_norm_w': 1.0 + nrm(ks[1], (DEPTH_2, D_MODEL), 0.02),
        'w_in': nrm(ks[2], (DEPTH_2, D_MODEL, N_IN), D_MODEL ** -0.5),
        'ret_norm_w': 1.0 + nrm(ks[3], (DEPTH_2, RET_HEADS, HEAD_DIM), 0.02),
        'dsa_kv_norm_w': 1.0 + nrm(ks[4], (DEPTH_2, KV_LATENT), 0.02),
        'dsa_w_uk': nrm(ks[5], (DEPTH_2, KV_LATENT, DSA_W), KV_LATENT ** -0.5),
        'dsa_w_uv': nrm(ks[6], (DEPTH_2, KV_LATENT, DSA_W), KV_LATENT ** -0.5),
        'w_out': nrm(ks[7], (DEPTH_2, D_MIX, D_MODEL), D_MIX ** -0.5),
        'mlp_norm_w': 1.0 + nrm(ks[8], (DEPTH_2, D_MODEL), 0.02),
        'w_up': nrm(ks[9], (DEPTH_2, D_MODEL, D_FF), D_MODEL ** -0.5),
        'w_down': nrm(ks[10], (DEPTH_2, D_FF, D_MODEL), D_FF ** -0.5),
        'final_norm_w': 1.0 + nrm(ks[11], (D_MODEL,), 0.02),
    }

def second_block(x, attn_norm_w, w_in, ret_norm_w, dsa_kv_norm_w, dsa_w_uk, dsa_w_uv, w_out, mlp_norm_w, w_up, w_down, final_norm_w):
    pos = jnp.arange(x.shape[1])
    for layer in range(DEPTH_2):
        x = hybrid_layer(x, attn_norm_w[layer], w_in[layer], ret_norm_w[layer], dsa_kv_norm_w[layer],
                         dsa_w_uk[layer], dsa_w_uv[layer], w_out[layer], mlp_norm_w[layer],
                         w_up[layer], w_down[layer], pos)
    return rms_norm_2(x, final_norm_w)


def setup_inputs(seed=0):
    out = dict(first_inputs(seed))
    for name, value in second_inputs(seed + 1).items():
        if name != "x":
            out[name + "_2"] = value
    return out


def reference(
    x, c, ctx, c_ctx, w_mod, b_mod, norm1_g, norm2_g, w_in, q_norm_g, k_norm_g, na_rpb, conv_w,
    conv_b, conv_norm_g, w_branch, w_out, w_router, router_bias, w_expert_gu, w_expert_down,
    final_norm_g, attn_norm_w_2, w_in_2, ret_norm_w_2, dsa_kv_norm_w_2, dsa_w_uk_2, dsa_w_uv_2,
    w_out_2, mlp_norm_w_2, w_up_2, w_down_2, final_norm_w_2,
):
    x = first_block(
        x, c, ctx, c_ctx, w_mod, b_mod, norm1_g, norm2_g, w_in, q_norm_g, k_norm_g, na_rpb,
        conv_w, conv_b, conv_norm_g, w_branch, w_out, w_router, router_bias, w_expert_gu,
        w_expert_down, final_norm_g,
    )
    return second_block(
        x, attn_norm_w_2, w_in_2, ret_norm_w_2, dsa_kv_norm_w_2, dsa_w_uk_2, dsa_w_uv_2,
        w_out_2, mlp_norm_w_2, w_up_2, w_down_2, final_norm_w_2,
    )


_drawn_inputs = setup_inputs


def setup_inputs(seed=0):
    import zlib

    import numpy as np

    out = dict(_drawn_inputs(seed))
    spreads = {}
    factors = {'norm1_g': 3.274,
     'q_norm_g': 8.0,
     'k_norm_g': 8.0,
     'na_rpb': 8.0,
     'conv_b': 3.572,
     'conv_norm_g': 5.69,
     'attn_norm_w_2': 2.677,
     'ret_norm_w_2': 6.888,
     'dsa_kv_norm_w_2': 8.0,
     'final_norm_w_2': 2.669}
    for name, (base, spread) in spreads.items():
        noise = np.random.default_rng([zlib.crc32(name.encode()), seed]).standard_normal(out[name].shape)
        drawn = base * np.exp(spread * noise) if base else spread * noise
        out[name] = jnp.asarray(drawn.astype(out[name].dtype))
    for name, factor in factors.items():
        out[name] = (out[name] * factor).astype(out[name].dtype)
    return out
```

```python
from contextlib import ExitStack

import concourse.bass as bass
from concourse import mybir
import numpy as np

F32 = mybir.dt.float32
F32R = mybir.dt.float32r
I32 = mybir.dt.int32
ALU = mybir.AluOpType
ACT = mybir.ActivationFunctionType
AX = mybir.AxisListType

P = 128
D = 1024
S = 512
C = 256
HD = 64
NK = D // P
NT = S // P
NC = C // P
UN = 512
UK = UN // P
SCALE = HD ** -0.5
EPS = 1e-6
NEG = -1.0e30
NTAP = 31
PADT = NTAP // 2
NEXP = 16
FF = 4096
NHEADS = 16
KEYS = S + C
NSEL = 128
TAKEN = -3.0e38
BIG_E = 1.0e30
WIN = 127
V_BMOD, V_N1, V_N2, V_ATT, V_MLP, V_CB, V_CG, V_C, V_CC, V_ALL = 0, 48, 56, 64, 80, 96, 100, 104, 112, 120


class Tally:

    def __init__(self, eng, turns, key, start):
        self.eng, self.turns, self.key = eng, turns, key
        self.n, self.frames, self.loops = dict(start), [], 0

    def at(self, name, k=1):
        v = self.n.get(name, 0) + k
        for i, adds in self.frames:
            if adds.get(name, 0):
                v = i * adds[name] + v
        return v

    def next(self, name, k=1):
        v = self.at(name, k)
        self.skip(name, k)
        return v

    def skip(self, name, k=1):
        self.n[name] = self.n.get(name, 0) + k

    def loop(self, count, body):
        key = (self.key, self.loops)
        self.loops += 1
        before = dict(self.n)
        with self.eng.Fori(0, count) as i:
            self.frames.append((i, self.turns.get(key, {})))
            body(i)
            self.frames.pop()
        got = {s: v - before.get(s, 0) for s, v in self.n.items() if v != before.get(s, 0)}
        self.turns[key] = got
        for s, v in got.items():
            self.n[s] += (count - 1) * v


class Sems(dict):
    def __init__(self, nc, ctx):
        super().__init__()
        self.nc, self.ctx = nc, ctx

    def __missing__(self, name):
        self[name] = self.ctx.enter_context(self.nc.semaphore(name))
        return self[name]


STORES_1 = [("ctx_kv", 0, 2 + 2 * NC), ("ctx_nk", 1, 4), ("ctx_nv", 0, NC), ("q", 1, 4), ("kv", 0, 2 + 2 * NT),
            ("nq", 1, 4), ("nk", 0, 4), ("nv", 1, NT), ("fourier", 0, 1), ("gqa", 1, 1), ("na", 0, 1)]
STORES_2 = [("rqk", 0, 4), ("rv", 1, NT), ("sqk", 0, 4), ("sv", 1, NT), ("dq", 0, 4), ("dk", 1, 4), ("dv", 0, NT)]


def stored(seq, s, upto=None):
    n = 0
    for name, b, k in seq:
        n += 16 * k if b == s else 0
        if name == upto:
            break
    return n


def program(nc, t, out, turns, only_first=False):
    ctx = ExitStack()
    with ctx:
        def sb(name, shape, dt=F32):
            return ctx.enter_context(nc.sbuf_tensor(name, shape, dt))

        def flat(ap):
            return ap.rearrange("p a b -> p (a b)")

        sems = Sems(nc, ctx)

        X = sb("X", [P, NT, D])
        BIG = sb("BIG", [P, NT * D])
        hH, hL = sb("hH", [P, NK, S], F32R), sb("hL", [P, NK, S], F32R)
        aH, aL = sb("aH", [P, UK, S], F32R), sb("aL", [P, UK, S], F32R)
        W = [sb(f"W{i}", [P, UK, UN]) for i in range(2)]
        WH = [sb(f"WH{i}", [P, UK, UN], F32R) for i in range(2)]
        WL = [sb(f"WL{i}", [P, UK, UN], F32R) for i in range(2)]
        ST = [sb(f"ST{i}", [P, UK, S]) for i in range(2)]
        G = sb("G", [P, NK, S])
        Z = sb("Z", [P, 4, S + 2 * PADT])
        F = sb("F", [P, 2, 512])
        AT = sb("AT", [P, 3 * KEYS])
        QS = [sb(f"QS{i}", [HD, S]) for i in range(2)]
        KS = [sb(f"KS{i}", [HD, KEYS]) for i in range(2)]
        VS = [sb(f"VS{i}", [P, KEYS // P, HD]) for i in range(2)]
        ES = [sb(f"ES{i}", [P, 14, 64]) for i in range(2)]
        VT = sb("VT", [P, V_ALL])
        MOD = sb("MOD", [P, 48, 2])
        CSH, CSL = sb("CSH", [P, NK, 2], F32R), sb("CSL", [P, NK, 2], F32R)
        CF = sb("CF", [P, 2, NK, 2])
        CW = sb("CW", [P, 4, 32])
        AF = sb("AF", [P, 4, NK])
        IDN = sb("IDN", [P, P])
        MSK = sb("MSK", [P, 64])
        CM = sb("CM", [P, P])
        RNW = sb("RNW", [P, 256])
        RB = sb("RB", [P, NEXP])
        WRH, WRL = sb("WRH", [P, NK, NEXP], F32R), sb("WRL", [P, NK, NEXP], F32R)
        GATE = sb("GATE", [P, NT, NEXP])
        SM = sb("SM", [P, 4, 32])
        MX, NM, DEN, RD = (sb(n, [P, 2]) for n in ("MX", "NM", "DEN", "RD"))
        TOP = sb("TOP", [P, 8])
        WIX = sb("WIX", [P, NT, 8])

        BK = [ctx.enter_context(nc.psum_tensor(f"BK{i}", [P, 512], F32)) for i in range(4)]
        SC = ctx.enter_context(nc.psum_tensor("SCP", [P, 1024], F32))
        TP = ctx.enter_context(nc.psum_tensor("TPP", [P, 1024], F32))
        OB = [BK[0][:, 0:HD], BK[1][:, 0:HD]]

        qT_d = nc.dram_tensor("qT_scratch", (NHEADS, HD, S), F32).ap()
        kT_d = nc.dram_tensor("kT_scratch", (NHEADS, HD, KEYS), F32).ap()
        v_d = nc.dram_tensor("v_scratch", (NHEADS, KEYS, HD), F32).ap()
        yT_d = nc.dram_tensor("yT_scratch", (4, 512, S), F32).ap()
        rpb_d = nc.dram_tensor("rpb_scratch", (8 * 15, 64, WIN), F32).ap()

        XN = BIG[:].rearrange("p (t d) -> p t d", t=NT)
        BV = BIG[:].rearrange("p (k s) -> p k s", k=NK)
        cH = flat(aH[:]).rearrange("p (k s) -> p k s", k=NK)
        cL = flat(aL[:]).rearrange("p (k s) -> p k s", k=NK)
        CTX = [flat(ST[i][:])[:, 0:D] for i in range(2)]
        CTN = flat(G[:])[:, 0:2 * D].rearrange("p (t d) -> p t d", t=2)
        TM = AT[:, 0:NT * 512].rearrange("p (t c) -> p t c", t=NT)
        T1, T2 = G[:, 0:4, :], G[:, 4:8, :]
        PR = AT[:, 0:KEYS]
        PT = AT[:, KEYS:2 * KEYS].rearrange("p (k q) -> p k q", q=P)
        SB = AT[:, 2 * KEYS:3 * KEYS]
        GB = AT[:, 0:D]
        DG = AT[:, 2048:2304]
        VR = F[0:V_ALL, 0, 0:P]
        CWR = F[0:NTAP, 1, :]
        WR = Z[:, 0, 0:NK * NEXP].rearrange("p (k e) -> p k e", k=NK)
        RPB = Z[0:120, 1, 0:WIN]
        RC = flat(ES[1][:])[:, 0:256].rearrange("p (t d) -> p t d", t=NT)
        RS = flat(ES[1][:])[:, 256:512].rearrange("p (t d) -> p t d", t=NT)
        GQ, GK = flat(ES[1][:])[:, 512:576], flat(ES[1][:])[:, 576:640]
        KNW = flat(ES[1][:])[:, 512:640]
        ONE = AT[:, 1024:1152]
        TC = flat(ES[1][:])[:, 0:128].rearrange("p (t d) -> p t d", t=NT)
        TS = flat(ES[1][:])[:, 128:256].rearrange("p (t d) -> p t d", t=NT)
        XB = flat(ES[0][:])[:, 0:S]
        UKW, UVW = flat(ES[0][:])[:, 0:256], flat(ES[0][:])[:, 256:512]
        CU, CT = G[:, 0:4, :], G[:, 4:8, :]
        ZF = flat(Z[:])
        CKT, KIT = ZF[:, 0:512], ZF[:, 512:1024]
        SG = ZF[:, 1024:2048].rearrange("p (t c) -> p t c", t=NT)
        SEL, QI = G[:, 0:4, :], G[:, 4:8, :]
        IXA, IXW = AT[:, 0:512], AT[:, 512:1024]
        RP = TM
        RT = lambda n: F[:, 0, n * 64:(n + 1) * 64].rearrange("p (t e) -> p t e", t=NT)
        RT2 = lambda n, w: F[:, 1, n * 64:n * 64 + NT * w].rearrange("p (t e) -> p t e", t=NT)

        block = ctx.enter_context(nc.Block())
        BANKS = [f"bank_free{j}" for j in range(4)]

        @block.sync
        def _(sp):
            T = Tally(sp, turns, "sp", {})
            slot = [0]

            def unit(src, n=UN):
                s = slot[0]
                slot[0] ^= 1
                sp.wait_ge(sems["w_lo"], T.next("w_lo"))
                sp.dma_start(W[s][:, :, 0:n], src.rearrange("(k p) n -> p k n", p=P)).then_inc(sems[f"w_landed{s}"], 16)

            def blk(w, col, n=UN):
                for r in range(2):
                    unit(w[r * UN:(r + 1) * UN, bass.ds(col, n)], n)

            def load(dst, src, name):
                sp.dma_start(dst, src).then_inc(sems[name], 16)

            def row(ap, n):
                return ap.rearrange("(o n) -> o n", o=1).to_broadcast([P, n])

            def pick(ap, l):
                return ap[bass.ds(l, 1)].rearrange("a k n -> (a k) n")

            rows = lambda ap: ap.rearrange("(r p) -> r p", p=P)
            load(VR[V_BMOD:V_N1, :], rows(t["b_mod"][0]), "vec_landed")
            load(VR[V_N1:V_N2, :], rows(t["norm1_g"][0]), "vec_landed")
            load(VR[V_N2:V_ATT, :], rows(t["norm2_g"][0]), "vec_landed")
            load(VR[V_ATT:V_MLP, :], t["attn_norm_w_2"].rearrange("l (r p) -> (l r) p", p=P), "vec_landed")
            load(VR[V_MLP:V_CB, :], t["mlp_norm_w_2"].rearrange("l (r p) -> (l r) p", p=P), "vec_landed")
            load(VR[V_CB:V_CG, :], rows(t["conv_b"][0]), "vec_landed")
            load(VR[V_CG:V_C, :], rows(t["conv_norm_g"][0]), "vec_landed")
            load(VR[V_C:V_CC, :], rows(t["c"][0]), "vec_landed")
            load(VR[V_CC:V_ALL, :], rows(t["c_ctx"]), "vec_landed")
            load(CWR, t["conv_w"][0], "vec_landed")
            load(IDN[:], t["k_ident"], "vec_landed")
            load(WR, t["w_router"].rearrange("(k p) e -> p k e", p=P), "wr_landed")
            for i in range(NT):
                load(X[:, i, :], t["x"][0, i * P:(i + 1) * P, :], "x_landed")
            for i in range(NC):
                load(CTX[i], t["ctx"][0, i * P:(i + 1) * P, :], "x_landed")
            sp.wait_ge(sems["rpb_zero"], T.next("rpb_zero"))
            load(RPB[:, 48:79], t["na_rpb"][0].rearrange("h m c -> (h m) c"), "rpb_landed")
            sp.wait_ge(sems["rpb_landed"], T.next("rpb_landed", 16))
            load(rpb_d, RPB.unsqueeze(1).to_broadcast([120, 64, WIN]), "rpb_stored")
            load(RC, t["k_ropec"], "tab_landed")
            load(RS, t["k_ropes"], "tab_landed")
            load(GQ, row(t["q_norm_g"][0], HD), "tab_landed")
            load(GK, row(t["k_norm_g"][0], HD), "tab_landed")
            load(MSK[:], t["k_colmask"], "tab_landed")
            load(CM[:], t["k_causal"], "tab_landed")
            load(RB[:], row(t["router_bias"], NEXP), "tab_landed")

            T.loop(12, lambda i: blk(t["w_mod"][0], i * UN))
            w = t["w_in"][0]
            blk(w, 512, 256)
            blk(w, 1280)
            blk(w, 1792)
            blk(w, 0)
            blk(w, 512, 256)
            blk(w, 768)
            blk(w, 1280)
            blk(w, 1792)
            blk(w, 2304)
            sp.wait_ge(sems["norm_tr"], T.next("norm_tr", NK))
            load(BV[:, 0:4, :], t["k_dftc"].rearrange("(k p) s -> p k s", p=P), "fou_landed")
            load(BV[:, 4:8, :], t["k_dfts"].rearrange("(k p) s -> p k s", p=P), "fou_landed")
            sp.wait_ge(sems["nv_out"], T.next("nv_out"))
            load(DG, t["k_dftg"], "fou_landed")
            blk(w, 3328)
            blk(w, 2816)

            def heads(name, count, base, nk, bias=None):
                def head(h, s):
                    sem = f"head_landed{s}"
                    load(QS[s][:], pick(qT_d, h), sem)
                    load(KS[s][:, 0:nk], pick(kT_d, h)[:, 0:nk], sem)
                    load(VS[s][:, 0:nk // P, :], pick(v_d, h)[0:nk, :].rearrange("(t p) d -> p t d", p=P), sem)
                    if bias is not None:
                        bias(h - base, s, sem)
                for s in range(2):
                    head(base + s, s)

                def later(i):
                    for s in range(2):
                        sp.wait_ge(sems[name + "_oe"], T.next(name + "_oe", NT))
                        head(i * 2 + (base + 2 + s), s)
                T.loop(count // 2 - 1, later)
                sp.wait_ge(sems[name + "_oe"], T.next(name + "_oe", 2 * NT))
                sp.sem_inc(sems["sp_paused"], 1)

            for s in range(2):
                sp.wait_ge(sems[f"st_written{s}"], T.at(f"st_written{s}", stored(STORES_1, s, "nv" if s else "nk")))

            heads("head", 8, 0, KEYS)
            sp.wait_ge(sems["rpb_stored"], T.at("rpb_stored", 16))

            def na_bias(h, s, sem):
                for rr in range(2):
                    src = bass.AP(rpb_d.tensor, h * (15 * 64 * WIN) + ((1 - rr) * 64 * WIN + 63),
                                  [[WIN - 1, 64], [64 * WIN, 14], [1, 64]])
                    load(ES[s][rr * 64:(rr + 1) * 64, :, :], src, sem)
            heads("head", 8, 8, KEYS, na_bias)

            for s in range(2):
                sp.wait_ge(sems[f"st_written{s}"], T.next(f"st_written{s}", stored(STORES_1, s)))
            sp.wait_ge(sems["cv_written"], T.next("cv_written", 16))

            def branch(i):
                sp.wait_ge(sems["yb_used"], T.next("yb_used"))
                load(ST[1][:], pick(yT_d, i).rearrange("(k p) s -> p k s", p=P), "yb_landed")
                blk(w, i * D + 3840)
                blk(w, i * D + (3840 + UN))
                for hf in range(2):
                    unit(pick(t["w_branch"][0], i)[:, hf * UN:(hf + 1) * UN])
            T.loop(4, branch)
            blk(t["w_out"][0], 0)
            blk(t["w_out"][0], UN)

            def expert(e):
                gu = pick(t["w_expert_gu"][0], e)
                blk(gu, 0)
                blk(gu, UN)
                for hf in range(2):
                    unit(pick(t["w_expert_down"][0], e)[:, hf * UN:(hf + 1) * UN])
            T.loop(NEXP, expert)
            sp.wait_ge(sems["moe_done"], T.next("moe_done"))
            load(flat(G[:])[:, 0:D], row(t["final_norm_g"], D), "gf_landed")

            def layer(l):
                w2 = pick(t["w_in_2"], l)
                sp.wait_ge(sems["es_free"], T.next("es_free"))
                load(TC, t["k_retc"], "lay_landed")
                load(TS, t["k_rets"], "lay_landed")
                load(UKW, pick(t["dsa_w_uk_2"], l), "lay_landed")
                load(UVW, pick(t["dsa_w_uv_2"], l), "lay_landed")
                load(KNW, t["dsa_kv_norm_w_2"][bass.ds(l, 1), :].to_broadcast([P, P]), "lay_landed")
                load(RNW[:], t["ret_norm_w_2"].rearrange("l h d -> l (h d)")[bass.ds(l, 1), :].to_broadcast([P, 256]), "lay_landed")
                blk(w2, 0)
                blk(w2, UN)
                blk(w2, 1024, 384)
                blk(w2, 1408)
                blk(w2, 1920, 72)
                for b in range(3):
                    blk(w2, 1992 + b * UN)
                for s in range(2):
                    sp.wait_ge(sems[f"st_written{s}"], T.next(f"st_written{s}", stored(STORES_2, s)))
                heads("ret", 4, 0, S, lambda h, s, sem: load(flat(ES[s][:])[:, 0:S], pick(t["k_decay"], h), sem))
                load(XB, t["k_dilbias"], "xb_landed")
                heads("head", 4, 4, S)
                heads("head", 8, 8, S)
                wo = pick(t["w_out_2"], l)
                blk(wo, 0)
                blk(wo, UN)

                def chunk(c):
                    blk(pick(t["w_up_2"], l), c * UN)
                    for hf in range(2):
                        unit(t["w_down_2"][bass.ds(l, 1), bass.ds(c * UN, UN), hf * UN:(hf + 1) * UN]
                             .rearrange("a k n -> (a k) n"))
                sp.sem_inc(sems["sp_paused"], 1)
                T.loop(FF // UN, chunk)
            if not only_first:
                T.loop(2, layer)
                sp.wait_ge(sems["mlp_done"], T.next("mlp_done", 2))
                load(flat(G[:])[:, 0:D], row(t["final_norm_w_2"], D), "gf_landed")
            for i in range(NT):
                sp.wait_ge(sems["out_ready"], T.next("out_ready"))
                sp.dma_start(out[0, i * P:(i + 1) * P, :], XN[:, i, :]).then_inc(sems["out_written"], 16)
            sp.wait_ge(sems["out_written"], T.next("out_written", 16 * NT))

        @block.gpsimd
        def _(pool):
            T = Tally(pool, turns, "pool", {})
            pool.memset(RPB, 0.0).then_inc(sems["rpb_zero"], 1)

            def store(seq, name, dmas):
                s = [b for n, b, _ in seq if n == name][0]
                assert len(dmas) == [k for n, _, k in seq if n == name][0], name
                pool.wait_ge(sems[name + "_out"], T.next(name + "_out"))
                pool.sem_inc(sems["pool_paused"], 1)
                for dst, src in dmas:
                    pool.dma_start(dst, src).then_inc(sems[f"st_written{s}"], 16)

            def qk(dst, s, b0=0, nb=4):
                return [(dst[2 * b:2 * b + 2].rearrange("h d s -> (h d) s"), ST[s][:, b0 + b, 0:dst.shape[2]])
                        for b in range(nb)]

            def vv(dst, s, nt):
                nh = dst.shape[0]
                return [(dst[:, i * P:(i + 1) * P, :].rearrange("h p d -> p h d"),
                         ST[s][:, i, 0:nh * HD].rearrange("p (h d) -> p h d", h=nh)) for i in range(nt)]

            def kv(s, c0, nt):
                dm = []
                vt = flat(ST[s][:, 2:4, :]).rearrange("p (t c) -> p t c", t=8)
                for g in range(2):
                    dm.append((kT_d[4 * g:4 * g + 4, :, c0:c0 + nt * P].rearrange("r d s -> d r s"),
                               ST[s][g * HD:(g + 1) * HD, 0, 0:nt * P].unsqueeze(1).to_broadcast([HD, 4, nt * P])))
                    for i in range(nt):
                        dm.append((v_d[4 * g:4 * g + 4, c0 + i * P:c0 + (i + 1) * P, :].rearrange("r p d -> p r d"),
                                   vt[:, i, g * HD:(g + 1) * HD].unsqueeze(1).to_broadcast([P, 4, HD])))
                return dm

            store(STORES_1, "ctx_kv", kv(0, S, NC))
            store(STORES_1, "ctx_nk", qk(kT_d[8:16, :, S:KEYS], 1))
            store(STORES_1, "ctx_nv", vv(v_d[8:16, S:KEYS, :], 0, NC))
            store(STORES_1, "q", qk(qT_d[0:8], 1))
            store(STORES_1, "kv", kv(0, 0, NT))
            store(STORES_1, "nq", qk(qT_d[8:16], 1))
            store(STORES_1, "nk", qk(kT_d[8:16, :, 0:S], 0))
            store(STORES_1, "nv", vv(v_d[8:16, 0:S, :], 1, NT))
            store(STORES_1, "fourier", [(yT_d[2].rearrange("(k p) s -> p k s", p=P), ST[0][:])])

            pool.wait_ge(sems["z_ready"], T.next("z_ready"))
            pool.memset(CU, 0.0).then_inc(sems["pool_self"], 1)
            pool.wait_ge(sems["pool_self"], T.next("pool_self"))

            def tap(k):
                pool.tensor_tensor(CT, Z[:, :, bass.ds(k, S)], CW[:, :, bass.ds(k, 1)].to_broadcast([P, 4, S]),
                                   ALU.mult).then_inc(sems["pool_self"], 1)
                pool.wait_ge(sems["pool_self"], T.next("pool_self"))
                pool.tensor_tensor(CU, CU, CT, ALU.add).then_inc(sems["pool_self"], 1)
                pool.wait_ge(sems["pool_self"], T.next("pool_self"))
            T.loop(NTAP, tap)
            pool.sem_inc(sems["conv_done"], 1)
            store(STORES_1, "gqa", [(yT_d[0].rearrange("(k p) s -> p k s", p=P), ST[1][:])])
            store(STORES_1, "na", [(yT_d[1].rearrange("(k p) s -> p k s", p=P), ST[0][:])])
            pool.wait_ge(sems["cv_out"], T.next("cv_out"))
            pool.dma_start(yT_d[3].rearrange("(k p) s -> p k s", p=P), CU).then_inc(sems["cv_written"], 16)

            def layer(l):
                store(STORES_2, "rqk", qk(qT_d[0:4], 0, 0, 2) + qk(kT_d[0:4, :, 0:S], 0, 2, 2))
                store(STORES_2, "rv", vv(v_d[0:4, 0:S, :], 1, NT))
                store(STORES_2, "sqk", qk(qT_d[4:8], 0, 0, 2) + qk(kT_d[4:8, :, 0:S], 0, 2, 2))
                store(STORES_2, "sv", vv(v_d[4:8, 0:S, :], 1, NT))
                store(STORES_2, "dq", qk(qT_d[8:16], 0))
                store(STORES_2, "dk", qk(kT_d[8:16, :, 0:S], 1))
                store(STORES_2, "dv", vv(v_d[8:16, 0:S, :], 0, NT))
            if not only_first:
                T.loop(2, layer)
            for s in range(2):
                pool.wait_ge(sems[f"st_written{s}"],
                             stored(STORES_1, s) + (0 if only_first else 2 * stored(STORES_2, s)))
            pool.wait_ge(sems["cv_written"], 16)

        @block.tensor
        def _(pe):
            T = Tally(pe, turns, "pe", {"w_lo": 2, "yb_used": 1})
            slot = [0]
            h, cx, aa, cs = (hH[:], hL[:]), (cH, cL), (aH[:], aL[:]), (CSH[:], CSL[:])

            def unit(act, k0, form, n, start, stop, nj=4):
                s = slot[0]
                slot[0] ^= 1
                pe.wait_ge(sems["w_lo"], T.next("w_lo"))
                ah, al = act
                cols = n if form == "T" else ah.shape[2]
                for j in range(nj):
                    if start:
                        pe.wait_ge(sems[BANKS[j]], T.at(BANKS[j]))
                    q = []
                    for k in range(UK):
                        for wp, ap in ((WH, ah), (WL, ah), (WH, al)):
                            if form == "F":
                                q.append((wp[s][:, k, j * P:(j + 1) * P], ap[:, k0 + k, :]))
                            else:
                                q.append((ap[:, k0 + k, j * P:(j + 1) * P], wp[s][:, k, 0:n]))
                    for a, (lt, rh) in enumerate(q):
                        mm = pe.matmul(BK[j][:, 0:cols], lt, rh, start=start and a == 0,
                                       stop=stop and a == len(q) - 1, skip_group_check=True)
                    mm.then_inc(sems["gemm_done"], 4 // nj)
                if start:
                    for b in BANKS:
                        T.skip(b)

            def blk(act, form, n=UN, nj=4):
                unit(act, 0, form, n, True, False, nj)
                unit(act, 4, form, n, False, True, nj)

            def turn(name, src, nt, nk):
                for k in range(nk):
                    if k >= 2:
                        pe.wait_ge(sems[name + "_free"], T.next(name + "_free"))
                    for i in range(nt):
                        c0 = (k % 2) * 512 + i * P
                        mm = pe.transpose(TP[:, c0:c0 + P], src(i, k), IDN[:])
                    mm.then_inc(sems[name + "_tr"], 1)
                pe.wait_ge(sems[name + "_free"], T.next(name + "_free", min(2, nk)))

            cols_of = lambda v: (lambda i, k: v[:, i, k * P:(k + 1) * P])

            pe.wait_ge(sems["vec_landed"], T.next("vec_landed", 16 * 11))
            pe.transpose(TP[:, 0:V_ALL], VR, IDN[0:V_ALL, 0:V_ALL])
            for j in range(4):
                mm = pe.transpose(TP[:, 128 + j * 32:128 + j * 32 + NTAP], CWR[:, j * P:(j + 1) * P],
                                  IDN[0:NTAP, 0:NTAP])
            mm.then_inc(sems["vec_tr"], 1)
            pe.wait_ge(sems["cs_lo"], T.next("cs_lo"))
            T.loop(12, lambda i: blk(cs, "F"))
            pe.wait_ge(sems["norm_xn"], T.next("norm_xn", NC))
            turn("norm", cols_of(CTN), NC, NK)
            pe.wait_ge(sems["norm_xn"], T.next("norm_xn", NT))
            turn("norm", cols_of(XN), NT, NK)
            pe.wait_ge(sems["norm_lo"], T.next("norm_lo", NK))
            blk(cx, "T", 256, 2)
            blk(cx, "F")
            pe.wait_ge(sems["ck_rms"], T.next("ck_rms"))
            turn("sink", cols_of(TM), NC, 1)
            blk(cx, "T", UN, 2)
            pe.wait_ge(sems["norm_lo"], T.next("norm_lo", NK))
            blk(h, "T")
            pe.wait_ge(sems["q_rope"], T.next("q_rope"))
            turn("sink", cols_of(TM), NT, 4)
            blk(h, "T", 256)
            blk(h, "F")
            pe.wait_ge(sems["k_rope"], T.next("k_rope"))
            turn("sink", cols_of(TM), NT, 1)
            blk(h, "F")
            blk(h, "T")
            blk(h, "T")
            pe.wait_ge(sems["fou_landed"], T.next("fou_landed", 48))
            pe.wait_ge(sems["fou_in"], T.next("fou_in"))
            for g in range(4):
                for part in range(2):
                    for k in range(4):
                        mm = pe.matmul(SC[:, part * 512:(part + 1) * 512], TM[:, k, g * P:(g + 1) * P],
                                       BV[:, part * 4 + k, :], start=k == 0, stop=k == 3)
                mm.then_inc(sems["fo_a"], 1)
                pe.wait_ge(sems["fo_cp"], T.next("fo_cp"))
                if g:
                    pe.wait_ge(sems["fo_o"], T.next("fo_o"))
                for part in range(2):
                    mm = pe.matmul(TP[:, 0:512], DG[:, part * P:(part + 1) * P], F[:, part, :],
                                   start=part == 0, stop=part == 1)
                mm.then_inc(sems["fo_b"], 1)
            pe.wait_ge(sems["fo_o"], T.next("fo_o"))
            blk(h, "F")
            blk(h, "F")

            def scores(name, s, tt, nk):
                for c0 in range(0, nk, 512):
                    c1 = min(nk, c0 + 512)
                    mm = pe.matmul(SC[:, c0:c1], QS[s][:, tt * P:(tt + 1) * P], KS[s][:, c0:c1], start=True,
                                   stop=True, skip_group_check=True)
                mm.then_inc(sems[name + "_s"], 1)

            def values(name, n, s, nk):
                for kt in range(nk // P):
                    mm = pe.transpose(TP[:, kt * P:(kt + 1) * P], PR[:, kt * P:(kt + 1) * P], IDN[:])
                mm.then_inc(sems[name + "_pt"], 1)
                pe.wait_ge(sems[name + "_ptc"], T.next(name + "_ptc"))
                if n:
                    pe.wait_ge(sems[name + "_oe"], T.next(name + "_oe"))
                for kt in range(nk // P):
                    mm = pe.matmul(OB[n % 2], PT[:, kt, :], VS[s][:, kt, :], start=kt == 0,
                                   stop=kt == nk // P - 1, skip_group_check=True)
                mm.then_inc(sems[name + "_o"], 1)

            def attend(name, count, loads, keys):
                def body(i):
                    seq = [(s, tt) for s in range(2) for tt in range(NT)]
                    pe.wait_ge(sems["head_landed0"], T.next("head_landed0", 16 * loads))
                    scores(name, 0, 0, keys(0))
                    for n, (s, tt) in enumerate(seq):
                        pe.wait_ge(sems[name + "_exp"], T.next(name + "_exp"))
                        if n + 1 < len(seq):
                            s2, t2 = seq[n + 1]
                            if t2 == 0:
                                pe.wait_ge(sems["head_landed1"], T.next("head_landed1", 16 * loads))
                            scores(name, s2, t2, keys(t2))
                        values(name, n, s, keys(tt))
                    pe.wait_ge(sems[name + "_oe"], T.next(name + "_oe"))
                for b in BANKS[:2]:
                    pe.wait_ge(sems[b], T.at(b))
                pe.sem_inc(sems["pe_paused"], 1)
                T.loop(count // 2, body)

            attend("head", 8, 3, lambda tt: KEYS)
            turn("sink", cols_of(BIG[:, 0:2048].rearrange("p (t c) -> p t c", t=NT)), NT, 4)
            attend("head", 8, 5, lambda tt: KEYS)
            turn("sink", cols_of(BIG[:, 2048:4096].rearrange("p (t c) -> p t c", t=NT)), NT, 4)
            pe.wait_ge(sems["cv_sq"], T.next("cv_sq"))
            for j in range(4):
                mm = pe.matmul(SC[:, 0:512], ONE, CT[:, j, :], start=j == 0, stop=j == 3)
            mm.then_inc(sems["cv_pe"], 1)
            pe.wait_ge(sems["cv_r"], T.next("cv_r"))

            def branch(i):
                blk(h, "F")
                blk(h, "F")
                pe.wait_ge(sems["yb_used"], T.next("yb_used"))
                unit(aa, 0, "F", UN, True, True)
                unit(aa, 0, "F", UN, True, True)
            T.loop(4, branch)

            def spread(name):
                pe.wait_ge(sems[name + "_in"], T.next(name + "_in"))
                for k in range(NK):
                    mm = pe.matmul(SC[:, k * P:(k + 1) * P], flat(ST[0][:])[:, k * P:(k + 1) * P], IDN[:],
                                   start=True, stop=True, skip_group_check=True)
                mm.then_inc(sems[name + "_pe"], 1)
                pe.wait_ge(sems[name + "_gb"], T.next(name + "_gb"))
            spread("g1")
            pe.wait_ge(sems["norm_lo"], T.next("norm_lo", NK))
            blk(h, "T")
            blk(h, "T")
            pe.wait_ge(sems["norm_xn"], T.next("norm_xn", NT))
            turn("norm", cols_of(XN), NT, NK)
            pe.wait_ge(sems["norm_lo"], T.next("norm_lo", NK))
            pe.wait_ge(sems["wr_lo"], T.next("wr_lo"))
            for i in range(NT):
                q = [(a, b, k) for k in range(NK) for a, b in ((hH, WRH), (hH, WRL), (hL, WRH), (hL, WRL))]
                for n, (a, b, k) in enumerate(q):
                    mm = pe.matmul(TP[:, i * NEXP:(i + 1) * NEXP], a[:, k, i * P:(i + 1) * P], b[:, k, :],
                                   start=n == 0, stop=n == len(q) - 1, skip_group_check=True)
            mm.then_inc(sems["rt_pe"], 1)

            def expert(e):
                blk(h, "F")
                blk(h, "F")
                pe.wait_ge(sems["hid_lo"], T.next("hid_lo", 4))
                unit(aa, 0, "T", UN, True, True)
                unit(aa, 0, "T", UN, True, True)
            T.loop(NEXP, expert)
            spread("g2")

            def layer(l):
                pe.wait_ge(sems["norm_xn"], T.next("norm_xn", NT))
                turn("norm", cols_of(XN), NT, NK)
                pe.wait_ge(sems["norm_lo"], T.next("norm_lo", NK))
                blk(h, "T")
                blk(h, "T")
                pe.wait_ge(sems["rqk_rope"], T.next("rqk_rope"))
                turn("sink", cols_of(TM), NT, 4)
                blk(h, "T", 384)
                blk(h, "F")
                pe.wait_ge(sems["lat_rms"], T.next("lat_rms"))
                turn("sink", cols_of(TM), NT, 3)
                blk(h, "T", 72)
                pe.wait_ge(sems["lay_landed"], T.next("lay_landed", 16 * 6))
                for b in range(2):
                    mm = pe.matmul(SC[:, b * 512:(b + 1) * 512], UKW[:, b * P:(b + 1) * P], CKT, start=True, stop=True)
                for i in range(NT):
                    mm = pe.matmul(TP[:, i * 256:(i + 1) * 256], CKT[:, i * P:(i + 1) * P], UVW,
                                   start=True, stop=True, skip_group_check=True)
                mm.then_inc(sems["uk_pe"], 1)
                pe.wait_ge(sems["uk_cp"], T.next("uk_cp"))
                pe.wait_ge(sems["ki_out"], T.next("ki_out"))
                turn("sink", cols_of(TM), NT, 1)
                blk(h, "F")
                blk(h, "F")
                blk(h, "T")
                n = 0
                for tt in range(1, NT):
                    nk = (tt + 1) * P
                    for ih in range(8):
                        if n >= 2:
                            pe.wait_ge(sems["ix_act"], T.next("ix_act"))
                        p0 = (ih % 2) * HD
                        pe.matmul(SC[:, (n % 2) * 512:(n % 2) * 512 + nk],
                                  QI[p0:p0 + HD, ih // 2, tt * P:(tt + 1) * P], KIT[p0:p0 + HD, 0:nk],
                                  start=True, stop=True).then_inc(sems["ix_pe"], 1)
                        n += 1
                pe.wait_ge(sems["ix_act"], T.next("ix_act", 2))
                pe.wait_ge(sems["sel_done"], T.next("sel_done"))

                def ret(i):
                    for s in range(2):
                        pe.wait_ge(sems[f"head_landed{s}"], T.next(f"head_landed{s}", 64))
                        for kt in range(NT):
                            if kt >= 2:
                                pe.wait_ge(sems["ret_d"], T.next("ret_d"))
                            bank = SC if kt % 2 == 0 else TP
                            pe.matmul(bank[:, 0:S - kt * P], KS[s][:, kt * P:(kt + 1) * P], QS[s][:, kt * P:S],
                                      start=True, stop=True, skip_group_check=True).then_inc(sems["ret_s"], 1)
                        pe.wait_ge(sems["ret_d"], T.next("ret_d", 2))
                        for tt in range(NT):
                            if tt:
                                pe.wait_ge(sems["ret_oe"], T.next("ret_oe"))
                            for kt in range(tt + 1):
                                mm = pe.matmul(OB[tt % 2], RP[:, kt, (tt - kt) * P:(tt - kt + 1) * P],
                                               VS[s][:, kt, :], start=kt == 0, stop=kt == tt, skip_group_check=True)
                            mm.then_inc(sems["ret_o"], 1)
                        pe.wait_ge(sems["ret_oe"], T.next("ret_oe"))
                for b in BANKS[:2]:
                    pe.wait_ge(sems[b], T.at(b))
                pe.sem_inc(sems["pe_paused"], 1)
                T.loop(2, ret)
                attend("head", 4, 3, lambda tt: (tt + 1) * P)
                attend("head", 8, 3, lambda tt: (tt + 1) * P)
                pe.wait_ge(sems["mix_ready"], T.next("mix_ready"))
                turn("norm", cols_of(XN), NT, NK)
                pe.wait_ge(sems["norm_lo"], T.next("norm_lo", NK))
                blk(h, "T")
                blk(h, "T")
                pe.wait_ge(sems["norm_xn"], T.next("norm_xn", NT))
                turn("norm", cols_of(XN), NT, NK)
                pe.wait_ge(sems["norm_lo"], T.next("norm_lo", NK))

                def chunk(c):
                    blk(h, "F")
                    pe.wait_ge(sems["mlp_lo"], T.next("mlp_lo", 4))
                    unit(aa, 0, "T", UN, True, True)
                    unit(aa, 0, "T", UN, True, True)
                pe.sem_inc(sems["pe_paused"], 1)
                T.loop(FF // UN, chunk)
            if not only_first:
                T.loop(2, layer)

        @block.scalar
        def _(act):
            T = Tally(act, turns, "act", {b: 1 for b in BANKS})
            T.n["gemm_done:out"] = 8
            slot = [0]

            def hi():
                s = slot[0]
                slot[0] ^= 1
                act.wait_ge(sems[f"w_landed{s}"], T.next(f"w_landed{s}", 16))
                act.wait_ge(sems["gemm_done"], T.next("gemm_done:w", 4))
                act.activation(WH[s][:], W[s][:], ACT.Copy).then_inc(sems["w_hi"], 1)

            def unit(evac=None, more=True):
                if more:
                    hi()
                T.skip("gemm_done:out", 4)
                if evac is not None:
                    T.skip("gemm_done:out", -4)
                    evac()
                    T.skip("gemm_done:out", 4)

            def blk(evac=None, more=True):
                unit()
                unit(evac, more)
                for b in BANKS:
                    T.skip(b)

            def out(j, nj=4):
                act.wait_ge(sems["gemm_done"], T.at("gemm_done:out", (j + 1) * (4 // nj)))

            def copies(dst, cols=UN, nj=4, ready=None):
                def go():
                    for j in range(nj):
                        out(j, nj)
                        act.activation(dst(j), BK[j][:, 0:cols], ACT.Copy).then_inc(sems[BANKS[j]], 1)
                    for j in range(nj, 4):
                        act.sem_inc(sems[BANKS[j]], 1)
                    if ready:
                        act.wait_ge(sems[BANKS[nj - 1]], T.at(BANKS[nj - 1]))
                        act.sem_inc(sems[ready], 1)
                return go

            held = {0: 0, 1: 0}

            def begin(seq, name):
                s = [b for n, b, _ in seq if n == name][0]
                if held[s]:
                    act.wait_ge(sems[f"st_written{s}"], T.next(f"st_written{s}", held[s]))
                held[s] = 16 * [k for n, _, k in seq if n == name][0]
                return s

            def sink(name, nk, dst, w=S):
                for k in range(nk):
                    act.wait_ge(sems[name + "_tr"], T.next(name + "_tr"))
                    act.activation(dst(k), TP[:, (k % 2) * 512:(k % 2) * 512 + w], ACT.Copy).then_inc(
                        sems[name + "_free"], 1)
                act.wait_ge(sems[name + "_free"], T.next(name + "_free", nk))

            def split(name, nk, dst, w=S):
                for k in range(nk):
                    act.wait_ge(sems[name + "_free"], T.next(name + "_free"))
                    act.activation(dst[:, k, :], F[:, k % 2, 0:w], ACT.Copy).then_inc(sems[name + "_hi"], 1)

            def squares(name, src, nt):
                for i in range(nt):
                    act.activation(flat(F[:]), src(i), ACT.Square, accum_out=SM[:, 0, i:i + 1]).then_inc(
                        sems[name + "_ss"], 1)
                    act.wait_ge(sems[name + "_ss"], T.next(name + "_ss"))

            hi()
            act.wait_ge(sems["vec_cp"], T.next("vec_cp"))
            act.activation(CF[:, 0, :, :], CF[:, 1, :, :], ACT.Sigmoid).then_inc(sems["cs_sig"], 1)
            act.wait_ge(sems["cs_val"], T.next("cs_val"))
            act.activation(CSH[:], CF[:, 0, :, :], ACT.Copy).then_inc(sems["cs_hi"], 1)
            act.wait_ge(sems["wr_landed"], T.next("wr_landed", 16))
            act.activation(WRH[:], WR, ACT.Copy).then_inc(sems["wr_hi"], 1)
            T.loop(12, lambda i: blk())
            act.wait_ge(sems["x_landed"], T.next("x_landed", 16 * (NT + NC)))
            squares("norm", lambda i: CTX[i], NC)
            act.wait_ge(sems["norm_rd"], T.next("norm_rd"))
            squares("norm", lambda i: X[:, i, :], NT)
            act.wait_ge(sems["norm_rd"], T.next("norm_rd"))
            split("norm", NK, cH, C)
            split("norm", NK, hH[:])
            s = begin(STORES_1, "ctx_kv")
            blk(copies(lambda j: TM[:, j, 0:256], 256, 2, "ck_in"))
            s1 = begin(STORES_1, "ctx_nk")
            blk(copies(lambda j: ST[s1][:, j, 0:C], C, 4, "ctx_nk_out"))

            def kv_sink(nt, ready):
                vt = flat(ST[0][:, 2:4, :]).rearrange("p (t c) -> p t c", t=8)
                sink("sink", 1, lambda k: ST[0][:, 0, 0:nt * P], nt * P)
                act.activation(vt[:, 0:nt, :], TM[:, 0:nt, P:256], ACT.Copy).then_inc(sems["act_self"], 1)
                act.wait_ge(sems["act_self"], T.next("act_self"))
                act.sem_inc(sems[ready], 1)
            kv_sink(NC, "ctx_kv_out")
            s = begin(STORES_1, "ctx_nv")
            blk(copies(lambda j: ST[0][:, j, :], UN, 2, "ctx_nv_out"))
            blk(copies(lambda j: TM[:, j, :], UN, 4, "q_in"))
            s = begin(STORES_1, "q")
            sink("sink", 4, lambda k: ST[1][:, k, :])
            act.sem_inc(sems["q_out"], 1)
            blk(copies(lambda j: TM[:, j, 0:256], 256, 4, "k_in"))
            begin(STORES_1, "kv")
            nq = lambda: begin(STORES_1, "nq")
            nq()
            blk(copies(lambda j: ST[1][:, j, :], UN, 4, "nq_out"))
            kv_sink(NT, "kv_out")
            begin(STORES_1, "nk")
            blk(copies(lambda j: ST[0][:, j, :], UN, 4, "nk_out"))
            begin(STORES_1, "nv")
            blk(copies(lambda j: ST[1][:, j, :], UN, 4, "nv_out"))
            blk(copies(lambda j: TM[:, j, :], UN, 4, "fou_in"))
            begin(STORES_1, "fourier")
            for g in range(4):
                act.wait_ge(sems["fo_a"], T.next("fo_a"))
                act.activation(flat(F[:]), SC[:], ACT.Copy).then_inc(sems["fo_cp"], 1)
                act.wait_ge(sems["fo_b"], T.next("fo_b"))
                act.activation(ST[0][:, g, :], TP[:, 0:512], ACT.Copy).then_inc(sems["fo_o"], 1)
            act.wait_ge(sems["fo_o"], T.next("fo_o", 4))
            act.sem_inc(sems["fourier_out"], 1)

            def conv_gate():
                for j in range(4):
                    out(j)
                    act.activation(CT[:, j, :], BK[j][:], ACT.Sigmoid).then_inc(sems[BANKS[j]], 1)
            blk(conv_gate)
            blk(None, False)

            def attend(name, count, keys, biased):
                def body(i):
                    for n in range(2 * NT):
                        nk = keys(n % NT)
                        act.wait_ge(sems[name + "_nm"], T.next(name + "_nm"))
                        act.activation(PR[:, 0:nk], SB[:, 0:nk] if biased else SC[:, 0:nk], ACT.Exp,
                                       bias=NM[:, n % 2:n % 2 + 1], scale=1.0 if biased else SCALE,
                                       accum_out=DEN[:, n % 2:n % 2 + 1]).then_inc(sems[name + "_exp"], 1)
                        if n:
                            act.wait_ge(sems[name + "_o"], T.next(name + "_o"))
                        act.wait_ge(sems[name + "_pt"], T.next(name + "_pt"))
                        act.activation(flat(PT[:, 0:nk // P, :]), TP[:, 0:nk], ACT.Copy).then_inc(
                            sems[name + "_ptc"], 1)
                    act.wait_ge(sems[name + "_o"], T.next(name + "_o"))
                act.sem_inc(sems["act_paused"], 1)
                T.loop(count // 2, body)

            attend("head", 8, lambda tt: KEYS, False)
            begin(STORES_1, "gqa")
            sink("sink", 4, lambda k: ST[1][:, k, :])
            act.sem_inc(sems["gqa_out"], 1)
            attend("head", 8, lambda tt: KEYS, True)
            begin(STORES_1, "na")
            sink("sink", 4, lambda k: ST[0][:, k, :])
            act.sem_inc(sems["na_out"], 1)
            act.sem_inc(sems["y_turned"], 1)
            act.wait_ge(sems["cv_n"], T.next("cv_n"))
            act.activation(CT, CU, ACT.Sigmoid).then_inc(sems["cv_sig"], 1)

            def gates(hb):
                def go():
                    for j in range(4):
                        out(j)
                        act.activation(G[:, hb * 4 + j, :], BK[j][:], ACT.Sigmoid).then_inc(sems[BANKS[j]], 1)
                return go

            def skip_banks():
                for b in BANKS:
                    T.skip(b)

            act.wait_ge(sems["g_free"], T.next("g_free"))
            hi()

            def branch(i):
                blk(gates(0))
                act.wait_ge(sems["yb_landed"], T.next("yb_landed", 16))
                act.activation(aH[:], ST[1][:], ACT.Copy).then_inc(sems["yb_hi"], 1)
                blk(gates(1))
                for _ in range(2):
                    unit()
                    skip_banks()
            T.loop(4, branch)

            def spread(name):
                act.wait_ge(sems[name + "_pe"], T.next(name + "_pe"))
                act.activation(GB, SC[:], ACT.Copy).then_inc(sems[name + "_gb"], 1)
            spread("g1")
            for k in range(NK):
                act.wait_ge(sems["m_go"], T.next("m_go")) if k == 0 else None
                act.activation(hH[:, k, :], BV[:, k, :], ACT.Copy).then_inc(sems["norm_hi"], 1)
            blk()
            blk()
            act.wait_ge(sems["x2"], T.next("x2"))
            squares("norm", lambda i: X[:, i, :], NT)
            act.wait_ge(sems["norm_rd"], T.next("norm_rd"))
            split("norm", NK, hH[:])
            act.wait_ge(sems["rt_pe"], T.next("rt_pe"))
            act.activation(RT(0), TP[:, 0:64].rearrange("p (t e) -> p t e", t=NT), ACT.Sigmoid).then_inc(sems["rt_sig"], 1)
            act.wait_ge(sems["rt_done"], T.next("rt_done"))

            def hid_hi(name):
                def go():
                    for j in range(4):
                        act.wait_ge(sems[BANKS[j]], T.at(BANKS[j]))
                        act.activation(aH[:, j, :], F[:, j % 2, :], ACT.Copy).then_inc(sems[name], 1)
                return go

            def expert(e, more=True):
                def sig():
                    for j in range(4):
                        out(j)
                        act.activation(G[:, j, :], BK[j][:], ACT.Sigmoid).then_inc(sems["e_sig"], 1)
                blk(sig)
                blk(hid_hi("hid_hi"))
                unit()
                skip_banks()
                unit(None, more)
                skip_banks()
            T.loop(NEXP - 1, expert)
            expert(NEXP - 1, False)
            spread("g2")
            act.wait_ge(sems["x3"], T.next("x3"))
            squares("norm", lambda i: X[:, i, :], NT)
            act.wait_ge(sems["norm_rd"], T.next("norm_rd"))

            def layer(l):
                hi()
                act.wait_ge(sems["x4"], T.next("x4"))
                squares("norm", lambda i: X[:, i, :], NT)
                act.wait_ge(sems["norm_rd"], T.next("norm_rd"))
                split("norm", NK, hH[:])
                blk(copies(lambda j: TM[:, j, :], UN, 4, "rqk_in"))
                begin2("rv")

                def ret_vg():
                    for j in range(4):
                        out(j)
                        act.activation(ST[1][:, j, 0:256], BK[j][:, 0:256], ACT.Copy)
                        act.activation(SG[:, j, :], BK[j][:, 256:512], ACT.Sigmoid).then_inc(sems["sg_sig"], 1)
                    act.wait_ge(sems["sg_sig"], T.next("sg_sig", 4))
                    act.sem_inc(sems["rv_out"], 1)
                blk(ret_vg)
                begin2("rqk")
                sink("sink", 4, lambda k: ST[0][:, k, :])
                act.sem_inc(sems["rqk_out"], 1)
                blk(copies(lambda j: TM[:, j, 0:384], 384, 4, "lat_in"))
                blk(copies(lambda j: QI[:, j, :]))
                begin2("sqk")
                sink("sink", 3, lambda k: ST[0][:, k, :] if k < 2 else CKT)

                def index_kw():
                    for j in range(4):
                        out(j)
                        act.activation(TM[:, j, 0:64], BK[j][:, 0:64], ACT.Copy)
                        act.activation(TM[:, j, 64:128], BK[j][:, 0:64], ACT.Copy)
                        act.activation(WIX[:, j, :], BK[j][:, 64:72], ACT.Copy,
                                       scale=8 ** -0.5 * 64 ** -0.5).then_inc(sems[BANKS[j]], 1)
                    act.wait_ge(sems[BANKS[3]], T.at(BANKS[3]))
                    act.sem_inc(sems["ki_out"], 1)
                blk(index_kw)
                begin2("sv")
                act.wait_ge(sems["uk_pe"], T.next("uk_pe"))
                act.activation(ST[0][:, 2:4, :], SC[:].rearrange("p (k s) -> p k s", k=2), ACT.Copy)
                act.activation(ST[1][:, :, 0:256], TP[:].rearrange("p (t c) -> p t c", t=NT), ACT.Copy).then_inc(
                    sems["uk_cp"], 1)
                act.wait_ge(sems["uk_cp"], T.next("uk_cp"))
                act.sem_inc(sems["sqk_out"], 1)
                act.sem_inc(sems["sv_out"], 1)
                sink("sink", 1, lambda k: KIT)
                begin2("dq")
                blk(copies(lambda j: ST[0][:, j, :], UN, 4, "dq_out"))
                begin2("dk")
                blk(copies(lambda j: ST[1][:, j, :], UN, 4, "dk_out"))
                begin2("dv")
                blk(copies(lambda j: ST[0][:, j, :], UN, 4, "dv_out"), False)
                n = 0
                for tt in range(1, NT):
                    nk = (tt + 1) * P
                    for ih in range(8):
                        act.wait_ge(sems["ix_pe"], T.next("ix_pe"))
                        if n >= 2:
                            act.wait_ge(sems["ix_dve"], T.next("ix_dve"))
                        act.activation(F[:, n % 2, 0:nk], SC[:, (n % 2) * 512:(n % 2) * 512 + nk], ACT.Relu).then_inc(
                            sems["ix_act"], 1)
                        n += 1
                act.wait_ge(sems["ix_dve"], T.next("ix_dve", 2))
                act.wait_ge(sems["sel_done"], T.next("sel_done"))
                attend("head", 4, lambda tt: (tt + 1) * P, True)
                attend("head", 8, lambda tt: (tt + 1) * P, True)
                hi()
                split("norm", NK, hH[:])
                blk()
                blk()
                act.wait_ge(sems["x5"], T.next("x5"))
                squares("norm", lambda i: X[:, i, :], NT)
                act.wait_ge(sems["norm_rd"], T.next("norm_rd"))
                split("norm", NK, hH[:])

                def chunk(c, more=True):
                    def relu():
                        for j in range(4):
                            out(j)
                            if j >= 2:
                                act.wait_ge(sems["mlp_lo"], T.next("mlp_lo"))
                            act.activation(F[:, j % 2, :], BK[j][:], ACT.Relu).then_inc(sems[BANKS[j]], 1)
                            act.wait_ge(sems["mlp_sq"], T.next("mlp_sq"))
                            act.activation(aH[:, j, :], F[:, j % 2, :], ACT.Copy).then_inc(sems["mlp_hi"], 1)
                        act.wait_ge(sems["mlp_lo"], T.next("mlp_lo", 2))
                    blk(relu)
                    unit()
                    skip_banks()
                    unit(None, more)
                    skip_banks()
                act.sem_inc(sems["act_paused"], 1)
                T.loop(FF // UN - 1, chunk)
                chunk(FF // UN - 1, False)
            ring2 = {}

            def begin2(name):
                s = [b for n, b, _ in STORES_2 if n == name][0]
                act.wait_ge(sems[f"st_written{s}"], T.next(f"st_written{s}", held[s]))
                held[s] = 16 * [k for n, _, k in STORES_2 if n == name][0]
            if not only_first:
                for s in range(2):
                    act.wait_ge(sems[f"st_written{s}"], T.next(f"st_written{s}", held[s]))
                    T.skip(f"st_written{s}", -16 * [k for n, b, k in STORES_2 if b == s][-1])
                    held[s] = 16 * [k for n, b, k in STORES_2 if b == s][-1]
                T.loop(2, layer)
                act.wait_ge(sems["x4"], T.next("x4"))
                squares("norm", lambda i: X[:, i, :], NT)

        @block.vector
        def _(v):
            T = Tally(v, turns, "dve", {b: 1 for b in BANKS})
            T.n["gemm_done:out"] = 8
            slot = [0]
            link_sem = "dve_self"

            def link(ins):
                ins.then_inc(sems[link_sem], 1)
                v.wait_ge(sems[link_sem], T.next(link_sem))

            def lo():
                s = slot[0]
                slot[0] ^= 1
                v.wait_ge(sems["w_hi"], T.next("w_hi"))
                v.tensor_tensor(WL[s][:], W[s][:], WH[s][:].bitcast(F32), ALU.subtract).then_inc(sems["w_lo"], 1)

            def unit(evac=None, more=True):
                if more:
                    lo()
                if evac is not None:
                    evac()
                T.skip("gemm_done:out", 4)

            def blk(evac=None, more=True):
                unit()
                unit(evac, more)
                skip_banks()

            def skip_banks():
                for b in BANKS:
                    T.skip(b)

            def out(j):
                v.wait_ge(sems["gemm_done"], T.at("gemm_done:out", j + 1))

            def rsqrt(y, m, work):
                link(v.tensor_scalar(y.bitcast(I32), m.bitcast(I32), -0.5, float(0x5F3759DF), ALU.mult, ALU.add))
                for _ in range(3):
                    link(v.scalar_tensor_tensor(work, m, -0.5, y, ALU.mult, ALU.mult))
                    link(v.tensor_tensor(work, work, y, ALU.mult))
                    link(v.scalar_tensor_tensor(y, work, 1.5, y, ALU.add, ALU.mult))

            def stats(src_n, name, nt, dim):
                v.wait_ge(sems[name + "_ss"], T.next(name + "_ss", nt))
                link(v.tensor_scalar(SM[:, 1, 0:nt], SM[:, 0, 0:nt], 1.0 / dim, EPS, ALU.mult, ALU.add))
                rsqrt(SM[:, 2, 0:nt], SM[:, 1, 0:nt], SM[:, 3, 0:nt])
                v.sem_inc(sems[name + "_rd"], 1)

            def normed(name, src, dst, nt):
                stats(src, name, nt, D)
                for i in range(nt):
                    v.tensor_scalar(dst[:, i, :], src(i), SM[:, 2, i:i + 1], None, ALU.mult).then_inc(sems[name + "_xn"], 1)
                v.wait_ge(sems[name + "_xn"], T.next(name + "_xn", nt))

            def split(name, nk, H, L, scale, bias=None, w=S):
                def rest(k):
                    v.wait_ge(sems[name + "_hi"], T.next(name + "_hi"))
                    v.tensor_tensor(L[:, k, :], F[:, k % 2, 0:w], H[:, k, :].bitcast(F32), ALU.subtract).then_inc(
                        sems[name + "_lo"], 1)
                for k in range(nk):
                    v.wait_ge(sems[name + "_tr"], T.next(name + "_tr"))
                    if k >= 2:
                        v.wait_ge(sems[name + "_lo"], T.next(name + "_lo"))
                    src = TP[:, (k % 2) * 512:(k % 2) * 512 + w]
                    if scale is None:
                        ins = v.tensor_copy(F[:, k % 2, 0:w], src)
                    elif bias is None:
                        ins = v.tensor_scalar(F[:, k % 2, 0:w], src, scale(k), None, ALU.mult)
                    else:
                        ins = v.tensor_scalar(F[:, k % 2, 0:w], src, scale(k), bias(k), ALU.mult, ALU.add)
                    ins.then_inc(sems[name + "_free"], 1)
                    if k:
                        rest(k - 1)
                rest(nk - 1)
                v.wait_ge(sems[name + "_lo"], T.next(name + "_lo", 2))

            def rms(x4, nt, nh, gain, hd=HD):
                n = nt * nh
                sq = flat(T1)[:, 0:n * hd].rearrange("p (t h d) -> p t h d", t=nt, h=nh)
                ss = lambda r: SM[:, r, 0:n].rearrange("p (t h) -> p t h", t=nt)
                link(v.tensor_tensor(sq, x4, x4, ALU.mult))
                link(v.tensor_reduce(ss(0), sq, AX.X, ALU.add))
                link(v.tensor_scalar(SM[:, 1, 0:n], SM[:, 0, 0:n], 1.0 / hd, EPS, ALU.mult, ALU.add))
                rsqrt(SM[:, 2, 0:n], SM[:, 1, 0:n], SM[:, 3, 0:n])
                link(v.tensor_tensor(x4, x4, ss(2).unsqueeze(3).to_broadcast([P, nt, nh, hd]), ALU.mult))
                link(v.tensor_tensor(x4, x4, gain.unsqueeze(1).unsqueeze(1).to_broadcast([P, nt, nh, hd]), ALU.mult))

            def rope(x4, nt, nh):
                shp = [P, nt, nh, HD // 2]
                a = flat(T1)[:, 0:nt * nh * HD].rearrange("p (t h d) -> p t h d", t=nt, h=nh)
                b = flat(T2)[:, 0:nt * nh * HD].rearrange("p (t h d) -> p t h d", t=nt, h=nh)
                v.tensor_tensor(a, x4, RC.unsqueeze(2).to_broadcast([P, nt, nh, HD]), ALU.mult)
                v.tensor_tensor(b[:, :, :, 0:HD:2], x4[:, :, :, 1:HD:2], RS[:, :, 0:HD:2].unsqueeze(2).to_broadcast(shp), ALU.mult)
                link(v.tensor_tensor(b[:, :, :, 1:HD:2], x4[:, :, :, 0:HD:2], RS[:, :, 1:HD:2].unsqueeze(2).to_broadcast(shp), ALU.mult))
                link(v.tensor_tensor(x4, a, b, ALU.add))

            heads4 = lambda ap: ap.rearrange("p t (h d) -> p t h d", d=HD)

            v.sem_inc(sems["w_lo"], 2)
            v.sem_inc(sems["gemm_done"], 8)
            for b in BANKS:
                v.sem_inc(sems[b], 1)
            v.sem_inc(sems["yb_used"], 1)
            T.n["yb_used"] = 1
            v.wait_ge(sems["vec_tr"], T.next("vec_tr"))
            v.tensor_copy(VT[:], TP[:, 0:V_ALL])
            v.tensor_copy(CW[:, :, 0:NTAP], TP[:, 128:256].rearrange("p (j k) -> p j k", j=4)[:, :, 0:NTAP])
            for m in range(2):
                ins = v.tensor_copy(CF[:, 1, :, m], TP[:, V_C + 8 * m:V_C + 8 * m + 8])
            link(ins)
            v.sem_inc(sems["vec_cp"], 1)
            v.wait_ge(sems["cs_sig"], T.next("cs_sig"))
            link(v.tensor_tensor(CF[:, 0, :, :], CF[:, 0, :, :], CF[:, 1, :, :], ALU.mult))
            v.sem_inc(sems["cs_val"], 1)
            v.wait_ge(sems["cs_hi"], T.next("cs_hi"))
            v.tensor_tensor(CSL[:], CF[:, 0, :, :], CSH[:].bitcast(F32), ALU.subtract).then_inc(sems["cs_lo"], 1)
            v.wait_ge(sems["wr_hi"], T.next("wr_hi"))
            v.tensor_tensor(WRL[:], WR, WRH[:].bitcast(F32), ALU.subtract).then_inc(sems["wr_lo"], 1)
            lo()

            def mod(i):
                def go():
                    for j in range(4):
                        out(j)
                        v.tensor_copy(MOD[:, bass.ds(i * 4 + j, 1), :].rearrange("p a b -> p (a b)"), BK[j][:, 0:2]).then_inc(sems[BANKS[j]], 1)
                blk(go)
            T.loop(12, mod)
            for b in BANKS:
                v.wait_ge(sems[b], T.at(b, 0))
            link(v.tensor_tensor(MOD[:], MOD[:], VT[:, V_BMOD:V_N1].unsqueeze(2).to_broadcast([P, 48, 2]), ALU.add))
            for r, c0, m, g in ((0, 8, 0, V_N1), (1, 8, 1, V_N1), (2, 32, 0, V_N2)):
                ins = v.scalar_tensor_tensor(AF[:, r, :], MOD[:, c0:c0 + 8, m], 1.0, VT[:, g:g + 8], ALU.add, ALU.mult)
            link(ins)
            normed("norm", lambda i: CTX[i], CTN, NC)
            normed("norm", lambda i: X[:, i, :], XN, NT)
            split("norm", NK, cH, cL, lambda k: AF[:, 1, k:k + 1], lambda k: MOD[:, k, 1:2], C)
            split("norm", NK, hH[:], hL[:], lambda k: AF[:, 0, k:k + 1], lambda k: MOD[:, k, 0:1])
            v.wait_ge(sems["tab_landed"], T.next("tab_landed", 16 * 7))
            blk()
            v.wait_ge(sems["ck_in"], T.next("ck_in"))
            rms(heads4(TM[:, 0:NC, 0:P]), NC, 2, GK)
            v.sem_inc(sems["ck_rms"], 1)
            blk()
            blk()
            blk()
            v.wait_ge(sems["q_in"], T.next("q_in"))
            rms(heads4(TM), NT, 8, GQ)
            rope(heads4(TM), NT, 8)
            v.sem_inc(sems["q_rope"], 1)
            blk()
            v.wait_ge(sems["k_in"], T.next("k_in"))
            rms(heads4(TM[:, :, 0:P]), NT, 2, GK)
            rope(heads4(TM[:, :, 0:P]), NT, 2)
            v.sem_inc(sems["k_rope"], 1)
            for _ in range(5):
                blk()

            def conv_in():
                for j in range(4):
                    out(j)
                    v.tensor_tensor(Z[:, j, PADT:PADT + S], BK[j][:], CT[:, j, :], ALU.mult).then_inc(sems[BANKS[j]], 1)
                v.wait_ge(sems[BANKS[3]], T.at(BANKS[3]))
                v.sem_inc(sems["z_ready"], 1)
            v.wait_ge(sems["rpb_stored"], T.at("rpb_stored", 16))
            link(v.memset(Z[:], 0.0))
            blk(conv_in, False)

            def attend(name, count, keys, bias, dst):
                def body(i):
                    def top(n):
                        nk = keys(n % NT)
                        v.wait_ge(sems[name + "_s"], T.next(name + "_s"))
                        src = SC[:, 0:nk]
                        if bias is not None:
                            bias(n // NT, n % NT)
                            src = SB[:, 0:nk]
                        c = n % 2
                        link(v.tensor_reduce(MX[:, c:c + 1], src, AX.X, ALU.max))
                        v.tensor_scalar(NM[:, c:c + 1], MX[:, c:c + 1], -1.0 if bias is not None else -SCALE, None,
                                        ALU.mult).then_inc(sems[name + "_nm"], 1)

                    def put(n):
                        c = n % 2
                        v.wait_ge(sems[name + "_exp"], T.next(name + "_exp"))
                        link(v.reciprocal(RD[:, c:c + 1], DEN[:, c:c + 1]))
                        v.wait_ge(sems[name + "_o"], T.next(name + "_o"))
                        v.tensor_scalar(dst(n % NT, i * (2 * HD) + (n // NT) * HD), OB[c], RD[:, c:c + 1], None,
                                        ALU.mult).then_inc(sems[name + "_oe"], 1)
                    top(0)
                    for n in range(2 * NT):
                        if n + 1 < 2 * NT:
                            top(n + 1)
                        put(n)
                v.sem_inc(sems["v_paused"], 1)
                T.loop(count // 2, body)
                T.skip(name + "_oe", count * NT)

            def settle(name):
                v.wait_ge(sems[name], T.next(name))

            YG = BIG[:, 0:2048].rearrange("p (t c) -> p t c", t=NT)
            YN = BIG[:, 2048:4096].rearrange("p (t c) -> p t c", t=NT)
            v.wait_ge(sems["fo_b"], T.next("fo_b", 4))
            attend("head", 8, lambda tt: KEYS, None, lambda tt, c: YG[:, tt, bass.ds(c, HD)])

            def na_bias(s, tt):
                if tt == 0:
                    link(v.tensor_tensor(ES[s][:], ES[s][:], MSK[:].unsqueeze(1).to_broadcast([P, 14, 64]), ALU.add))
                j0 = 2 * (NT - 1 - tt)
                v.scalar_tensor_tensor(SB[:, 0:S], SC[:, 0:S], SCALE, flat(ES[s][:, j0:j0 + 8, :]), ALU.mult, ALU.add)
                link(v.tensor_scalar(SB[:, S:KEYS], SC[:, S:KEYS], SCALE, None, ALU.mult))
            attend("head", 8, lambda tt: KEYS, na_bias, lambda tt, c: YN[:, tt, bass.ds(c, HD)])
            v.wait_ge(sems["y_turned"], T.next("y_turned"))
            v.memset(BIG[:], 0.0)
            v.memset(ONE, 1.0)
            v.wait_ge(sems["conv_done"], T.next("conv_done"))
            for j in range(4):
                ins = v.tensor_scalar(CU[:, j, :], CU[:, j, :], VT[:, V_CB + j:V_CB + j + 1], None, ALU.add)
            link(ins)
            v.tensor_tensor(CT, CU, CU, ALU.mult).then_inc(sems["cv_sq"], 1)
            v.wait_ge(sems["cv_pe"], T.next("cv_pe"))
            link(v.tensor_scalar(F[:, 0, :], SC[:, 0:512], 1.0 / 512, EPS, ALU.mult, ALU.add))
            v.sem_inc(sems["cv_r"], 1)
            rsqrt(F[:, 1, :], F[:, 0, :], AT[:, 0:512])
            for j in range(4):
                ins = v.scalar_tensor_tensor(CU[:, j, :], CU[:, j, :], VT[:, V_CG + j:V_CG + j + 1], F[:, 1, :],
                                             ALU.mult, ALU.mult)
            link(ins)
            v.sem_inc(sems["cv_n"], 1)
            v.wait_ge(sems["cv_sig"], T.next("cv_sig"))
            link(v.tensor_tensor(CU, CU, CT, ALU.mult))
            v.sem_inc(sems["cv_out"], 1)
            v.wait_ge(sems["cv_written"], T.next("cv_written", 16))
            v.sem_inc(sems["g_free"], 1)
            lo()

            def branch(i):
                blk()
                v.wait_ge(sems["yb_hi"], T.next("yb_hi"))
                v.tensor_tensor(aL[:], ST[1][:], aH[:].bitcast(F32), ALU.subtract).then_inc(sems["yb_used"], 1)
                blk()
                for hb in range(2):
                    def go():
                        for j in range(4):
                            out(j)
                            v.tensor_tensor(F[:, j % 2, :], BK[j][:], G[:, hb * 4 + j, :], ALU.mult).then_inc(
                                sems[BANKS[j]], 1)
                            v.wait_ge(sems[BANKS[j]], T.at(BANKS[j]))
                            link(v.tensor_tensor(BV[:, hb * 4 + j, :], BV[:, hb * 4 + j, :], F[:, j % 2, :], ALU.add))
                    unit(go)
                    skip_banks()
            T.loop(4, branch)
            v.sem_inc(sems["m_go"], 1)

            def spread(name, c0):
                link(v.tensor_copy(flat(ST[0][:])[:, 0:D].rearrange("p (k c) -> p k c", k=NK),
                                   MOD[:, c0:c0 + NK, 0].unsqueeze(2).to_broadcast([P, NK, P])))
                v.sem_inc(sems[name + "_in"], 1)
            spread("g1", 16)
            for k in range(NK):
                v.wait_ge(sems["norm_hi"], T.next("norm_hi"))
                v.tensor_tensor(hL[:, k, :], BV[:, k, :], hH[:, k, :].bitcast(F32), ALU.subtract).then_inc(sems["norm_lo"], 1)
            v.wait_ge(sems["g1_gb"], T.next("g1_gb"))

            def add_x(hb, gain):
                def go():
                    for j in range(4):
                        xs = X[:, j, hb * UN:(hb + 1) * UN]
                        out(j)
                        if gain:
                            v.tensor_tensor(F[:, j % 2, :], BK[j][:], GB[:, hb * UN:(hb + 1) * UN], ALU.mult).then_inc(
                                sems[BANKS[j]], 1)
                            v.wait_ge(sems[BANKS[j]], T.at(BANKS[j]))
                            link(v.tensor_tensor(xs, xs, F[:, j % 2, :], ALU.add))
                        else:
                            v.tensor_tensor(xs, xs, BK[j][:], ALU.add).then_inc(sems[BANKS[j]], 1)
                return go
            blk(add_x(0, True))
            blk(add_x(1, True))
            v.sem_inc(sems["x2"], 1)
            v.wait_ge(sems["norm_lo"], T.next("norm_lo", NK))
            normed("norm", lambda i: X[:, i, :], XN, NT)
            split("norm", NK, hH[:], hL[:], lambda k: AF[:, 2, k:k + 1], lambda k: MOD[:, 24 + k, 0:1])
            v.memset(BIG[:], 0.0)

            v.wait_ge(sems["rt_sig"], T.next("rt_sig"))
            s_, sel, tmp, eq, onehot, ing = RT(0), RT(1), RT(2), RT(3), RT(4), RT(5)
            link(v.tensor_tensor(sel, s_, RB[:].unsqueeze(1).to_broadcast([P, NT, NEXP]), ALU.add))
            g5 = sel.rearrange("p t (g x y) -> p (t g) x y", g=4, x=2)
            mx2, mn2 = RT2(0, 8).rearrange("p t (g x) -> p (t g) x", x=2), RT2(1, 8).rearrange("p t (g x) -> p (t g) x", x=2)
            v.tensor_tensor(mx2, g5[:, :, :, 0], g5[:, :, :, 1], ALU.max)
            link(v.tensor_tensor(mn2, g5[:, :, :, 0], g5[:, :, :, 1], ALU.min))
            ga, gb2, gs = (RT2(n, 4).rearrange("p t g -> p (t g)") for n in (2, 3, 4))
            v.tensor_tensor(ga, mx2[:, :, 0], mx2[:, :, 1], ALU.max)
            link(v.tensor_tensor(gb2, mx2[:, :, 0], mx2[:, :, 1], ALU.min))
            link(v.tensor_tensor(gs, mn2[:, :, 0], mn2[:, :, 1], ALU.max))
            link(v.tensor_tensor(gb2, gb2, gs, ALU.max))
            link(v.tensor_tensor(ga, ga, gb2, ALU.add))

            def first_max(vals, n, hot, work, mxt):
                bc = mxt.unsqueeze(2).to_broadcast([P, NT, n])
                link(v.tensor_reduce(mxt, vals, AX.X, ALU.max))
                link(v.tensor_tensor(work, vals, bc, ALU.is_ge))
                link(v.tensor_tensor(work, work, DESC[:, 0:n].unsqueeze(1).to_broadcast([P, NT, n]), ALU.mult))
                link(v.tensor_reduce(mxt, work, AX.X, ALU.max))
                link(v.tensor_tensor(hot, work, bc, ALU.is_ge))
            DESC = SM[:, 3, 0:NEXP]
            for e in range(NEXP):
                ins = v.memset(SM[:, 3, e:e + 1], float(NEXP - e))
            link(ins)
            mxt = SM[:, 3, NEXP:NEXP + NT]
            gv = RT2(2, 4)
            first_max(gv, 4, RT2(4, 4), RT2(3, 4), mxt)
            link(v.tensor_copy(ing.rearrange("p t (g x) -> p (t g) x", x=4),
                               RT2(4, 4).rearrange("p t g -> p (t g)").unsqueeze(2).to_broadcast([P, 16, 4])))
            link(v.tensor_tensor(sel, sel, ing, ALU.mult))
            link(v.tensor_scalar(ing, ing, -1.0, BIG_E, ALU.add, ALU.mult))
            link(v.tensor_tensor(sel, sel, ing, ALU.add))
            first_max(sel, NEXP, onehot, tmp, mxt)
            link(v.scalar_tensor_tensor(sel, onehot, -3.0e30, sel, ALU.mult, ALU.add))
            first_max(sel, NEXP, eq, tmp, mxt)
            link(v.tensor_tensor(onehot, onehot, eq, ALU.add))
            link(v.tensor_tensor(s_, s_, onehot, ALU.mult))
            link(v.tensor_reduce(mxt, s_, AX.X, ALU.add))
            link(v.reciprocal(SM[:, 3, 20:24], mxt))
            link(v.tensor_tensor(GATE[:], s_, SM[:, 3, 20:24].unsqueeze(2).to_broadcast([P, NT, NEXP]), ALU.mult))
            v.sem_inc(sems["rt_done"], 1)

            def expert(e, more=True):
                def gate_half():
                    for j in range(4):
                        v.wait_ge(sems["e_sig"], T.next("e_sig"))
                        v.tensor_tensor(G[:, 4 + j, :], BK[j][:], G[:, j, :], ALU.mult).then_inc(sems[BANKS[j]], 1)
                blk(gate_half)

                def hidden():
                    def rest(j):
                        v.wait_ge(sems["hid_hi"], T.next("hid_hi"))
                        v.tensor_tensor(aL[:, j, :], F[:, j % 2, :], aH[:, j, :].bitcast(F32), ALU.subtract).then_inc(
                            sems["hid_lo"], 1)
                    for j in range(4):
                        out(j)
                        if j >= 2:
                            v.wait_ge(sems["hid_lo"], T.next("hid_lo"))
                        v.tensor_tensor(F[:, j % 2, :], BK[j][:], G[:, 4 + j, :], ALU.mult).then_inc(sems[BANKS[j]], 1)
                        if j:
                            rest(j - 1)
                    rest(3)
                    v.wait_ge(sems["hid_lo"], T.next("hid_lo", 2))
                blk(hidden)
                for hf in range(2):
                    def down():
                        for j in range(4):
                            out(j)
                            acc = XN[:, j, hf * UN:(hf + 1) * UN]
                            v.scalar_tensor_tensor(acc, BK[j][:], GATE[:, j, bass.ds(e, 1)], acc, ALU.mult,
                                                   ALU.add).then_inc(sems[BANKS[j]], 1)
                    unit(down, more or hf == 0)
                    skip_banks()
            T.loop(NEXP - 1, expert)
            expert(NEXP - 1, False)
            for b in BANKS:
                v.wait_ge(sems[b], T.at(b, 0))
            v.sem_inc(sems["moe_done"], 1)
            spread("g2", 40)
            v.wait_ge(sems["g2_gb"], T.next("g2_gb"))
            for i in range(NT):
                link(v.tensor_tensor(XN[:, i, :], XN[:, i, :], GB, ALU.mult))
                link(v.tensor_tensor(X[:, i, :], X[:, i, :], XN[:, i, :], ALU.add))
            v.sem_inc(sems["x3"], 1)

            def final(name, dst):
                stats(None, name, NT, D)
                v.wait_ge(sems["gf_landed"], T.next("gf_landed", 16))
                for i in range(NT):
                    ins = v.scalar_tensor_tensor(dst(i), X[:, i, :], SM[:, 2, i:i + 1], flat(G[:])[:, 0:D], ALU.mult,
                                                 ALU.mult)
                    link(ins)

            final("norm", (lambda i: XN[:, i, :]) if only_first else (lambda i: X[:, i, :]))
            if only_first:
                v.sem_inc(sems["out_ready"], NT)
                return
            v.sem_inc(sems["x4"], 1)
            v.sem_inc(sems["es_free"], 1)

            def layer(l):
                lo()
                link(v.tensor_copy(AF[:, 3, :], VT[:, bass.ds(l * 8 + V_ATT, 8)]))
                normed("norm", lambda i: X[:, i, :], XN, NT)
                split("norm", NK, hH[:], hL[:], lambda k: AF[:, 3, k:k + 1])
                v.wait_ge(sems["lay_landed"], T.next("lay_landed", 16 * 6))
                blk()
                v.wait_ge(sems["rqk_in"], T.next("rqk_in"))
                x16 = TM.rearrange("p t (h d) -> p t h d", d=32)
                a16 = T1.rearrange("p t (h d) -> p t h d", d=32)
                x4, a4, b4 = (q.rearrange("p t (h x d) -> p t h x d", x=2, d=32) for q in (TM, T1, T2))
                shp = [P, NT, 8, 32]
                ts = TS.unsqueeze(2).to_broadcast(shp)
                v.tensor_tensor(a16, x16, TC.unsqueeze(2).to_broadcast([P, NT, 16, 32]), ALU.mult)
                v.tensor_tensor(b4[:, :, :, 0, :], x4[:, :, :, 1, :], ts, ALU.mult)
                link(v.tensor_tensor(b4[:, :, :, 1, :], x4[:, :, :, 0, :], ts, ALU.mult))
                v.tensor_tensor(x4[:, :, :, 0, :], a4[:, :, :, 0, :], b4[:, :, :, 0, :], ALU.subtract)
                link(v.tensor_tensor(x4[:, :, :, 1, :], a4[:, :, :, 1, :], b4[:, :, :, 1, :], ALU.add))
                v.sem_inc(sems["rqk_rope"], 1)

                def ret_gate():
                    for j in range(4):
                        v.wait_ge(sems["sg_sig"], T.next("sg_sig"))
                        v.tensor_tensor(SG[:, j, :], BK[j][:, 256:512], SG[:, j, :], ALU.mult).then_inc(sems[BANKS[j]], 1)
                blk(ret_gate)
                blk()
                v.wait_ge(sems["lat_in"], T.next("lat_in"))
                rms(TM[:, :, 256:384].unsqueeze(2), NT, 1, KNW, P)
                v.sem_inc(sems["lat_rms"], 1)
                for n in range(5):
                    blk(None, n < 4)
                n = 0
                for tt in range(NT):
                    nk = (tt + 1) * P
                    if tt == 0:
                        v.tensor_copy(SEL[:, 0, 0:P], CM[:])
                        continue
                    for ih in range(8):
                        v.wait_ge(sems["ix_act"], T.next("ix_act"))
                        w = WIX[:, tt, ih:ih + 1]
                        if ih == 0:
                            ins = v.tensor_scalar(IXA[:, 0:nk], F[:, n % 2, 0:nk], w, None, ALU.mult)
                        else:
                            ins = v.scalar_tensor_tensor(IXA[:, 0:nk], F[:, n % 2, 0:nk], w, IXA[:, 0:nk], ALU.mult, ALU.add)
                        ins.then_inc(sems["ix_dve"], 1)
                        v.wait_ge(sems["ix_dve"], T.next("ix_dve"))
                        n += 1
                    link(v.tensor_tensor(IXA[:, nk - P:nk], IXA[:, nk - P:nk], CM[:], ALU.add))
                    for r in range(NSEL // 8):
                        src = IXA if r == 0 else IXW
                        v.sem_inc(sems["v_paused"], 1)
                        link(v.max(TOP[:], src[:, 0:nk]))
                        v.sem_inc(sems["v_paused"], 1)
                        link(v.match_replace(IXW[:, 0:nk], TOP[:], src[:, 0:nk], TAKEN))
                    link(v.tensor_scalar(SEL[:, tt, 0:nk], IXW[:, 0:nk], 0.5 * TAKEN, NEG, ALU.is_gt, ALU.mult))
                v.sem_inc(sems["sel_done"], 1)

                def ret(i):
                    for s in range(2):
                        for kt in range(NT):
                            n = S - kt * P
                            v.wait_ge(sems["ret_s"], T.next("ret_s"))
                            bank = SC if kt % 2 == 0 else TP
                            v.tensor_tensor(RP[:, kt, 0:n], bank[:, 0:n], flat(ES[s][:])[:, 0:n], ALU.mult).then_inc(
                                sems["ret_d"], 1)
                        for tt in range(NT):
                            v.wait_ge(sems["ret_o"], T.next("ret_o"))
                            v.tensor_copy(XN[:, tt, bass.ds(i * (2 * HD) + s * HD, HD)], OB[tt % 2]).then_inc(
                                sems["ret_oe"], 1)
                v.sem_inc(sems["v_paused"], 1)
                T.loop(2, ret)
                T.skip("ret_oe", 4 * NT)
                v.wait_ge(sems["ret_oe"], T.at("ret_oe", 0))
                o4 = XN[:, :, 0:256].rearrange("p t (h d) -> p t h d", h=4)
                sq = flat(T2)[:, 0:NT * 256].rearrange("p (t h d) -> p t h d", t=NT, h=4)
                st = lambda r: SM[:, r, 0:16].rearrange("p (t h) -> p t h", t=NT)
                bc = lambda r: st(r).unsqueeze(3).to_broadcast([P, NT, 4, HD])
                link(v.tensor_reduce(st(0), o4, AX.X, ALU.add))
                link(v.tensor_scalar(SM[:, 1, 0:16], SM[:, 0, 0:16], 1.0 / HD, None, ALU.mult))
                link(v.tensor_tensor(o4, o4, bc(1), ALU.subtract))
                link(v.tensor_tensor(sq, o4, o4, ALU.mult))
                link(v.tensor_reduce(st(0), sq, AX.X, ALU.add))
                link(v.tensor_scalar(SM[:, 1, 0:16], SM[:, 0, 0:16], 1.0 / HD, EPS, ALU.mult, ALU.add))
                rsqrt(SM[:, 2, 0:16], SM[:, 1, 0:16], SM[:, 3, 0:16])
                link(v.tensor_tensor(o4, o4, bc(2), ALU.mult))
                link(v.tensor_tensor(XN[:, :, 0:256], XN[:, :, 0:256], RNW[:].unsqueeze(1).to_broadcast([P, NT, 256]), ALU.mult))
                link(v.tensor_tensor(XN[:, :, 0:256], XN[:, :, 0:256], SG, ALU.mult))

                def biased(src):
                    def go(s, tt):
                        nk = (tt + 1) * P
                        link(v.scalar_tensor_tensor(SB[:, 0:nk], SC[:, 0:nk], SCALE, src(tt, nk), ALU.mult, ALU.add))
                    return go
                attend("head", 4, lambda tt: (tt + 1) * P, biased(lambda tt, nk: SEL[:, tt, 0:nk]),
                       lambda tt, c: XN[:, tt, bass.ds(c + 256, HD)])
                v.wait_ge(sems["xb_landed"], T.next("xb_landed", 16))
                attend("head", 8, lambda tt: (tt + 1) * P, biased(lambda tt, nk: XB[:, S - nk:S]),
                       lambda tt, c: XN[:, tt, bass.ds(c + 512, HD)])
                v.wait_ge(sems["head_oe"], T.at("head_oe", 0))
                v.sem_inc(sems["mix_ready"], 1)
                lo()
                v.sem_inc(sems["es_free"], 1)
                split("norm", NK, hH[:], hL[:], None)
                blk(add_x(0, False))
                blk(add_x(1, False))
                v.wait_ge(sems[BANKS[3]], T.at(BANKS[3], 0))
                v.sem_inc(sems["x5"], 1)
                link(v.tensor_copy(AF[:, 3, :], VT[:, bass.ds(l * 8 + V_MLP, 8)]))
                normed("norm", lambda i: X[:, i, :], XN, NT)
                split("norm", NK, hH[:], hL[:], lambda k: AF[:, 3, k:k + 1])

                def chunk(c, more=True):
                    def square():
                        for j in range(4):
                            v.wait_ge(sems[BANKS[j]], T.at(BANKS[j]))
                            v.tensor_tensor(F[:, j % 2, :], F[:, j % 2, :], F[:, j % 2, :], ALU.mult).then_inc(sems["mlp_sq"], 1)
                            v.wait_ge(sems["mlp_hi"], T.next("mlp_hi"))
                            v.tensor_tensor(aL[:, j, :], F[:, j % 2, :], aH[:, j, :].bitcast(F32), ALU.subtract).then_inc(
                                sems["mlp_lo"], 1)
                    blk(square)
                    for hf in range(2):
                        unit(add_x(hf, False), more or hf == 0)
                        skip_banks()
                v.sem_inc(sems["v_paused"], 1)
                T.loop(FF // UN - 1, chunk)
                chunk(FF // UN - 1, False)
                v.wait_ge(sems[BANKS[3]], T.at(BANKS[3], 0))
                v.sem_inc(sems["x4"], 1)
                v.sem_inc(sems["mlp_done"], 1)
            T.loop(2, layer)
            final("norm", lambda i: XN[:, i, :])
            v.sem_inc(sems["out_ready"], NT)


def tables():
    f = np.float32
    tok = np.arange(S)
    inv = 10000.0 ** (-np.arange(16) / 16.0)
    ang = np.concatenate([(tok // 64)[:, None] * inv, (tok % 64)[:, None] * inv], -1)
    tiles = lambda a: np.ascontiguousarray(a.reshape(NT, P, -1).transpose(1, 0, 2).astype(f))
    sign = np.where(np.arange(HD) % 2 == 0, -1.0, 1.0)
    inv2 = 10000.0 ** (-np.arange(32) / 32.0)
    ang2 = tok[:, None] * inv2
    col = np.arange(64)
    start = np.clip(col - 8, 0, 48)
    ok = (col[None, :] >= start[:, None]) & (col[None, :] < start[:, None] + 16)
    mask = np.where(ok, 0.0, NEG)
    diff = np.arange(P)[:, None] - np.arange(S)[None, :] + (S - P)
    count = ((diff >= 0) & (diff <= 128)).astype(int) + ((diff >= 0) & (diff % 4 == 0)) + ((diff >= 0) & (diff % 16 == 0))
    dil = np.where(count > 0, np.log(np.maximum(count, 1)), NEG)
    m = np.arange(S)[None, :] - np.arange(P)[:, None]
    lg = np.log(1.0 - 2.0 ** (-5.0 - np.arange(4)))
    decay = np.exp(np.maximum(m, 0)[None] * lg[:, None, None]) * (m >= 0)[None] * SCALE
    al = 2 * np.pi * ((tok[:, None] * tok[None, :]) % S) / S
    g = np.arange(P)
    ag = 2 * np.pi * ((g[:, None] * g[None, :]) % P) / P
    return {
        "k_ident": np.eye(P, dtype=f),
        "k_ropec": tiles(np.repeat(np.cos(ang), 2, -1)),
        "k_ropes": tiles(np.repeat(np.sin(ang), 2, -1) * sign),
        "k_colmask": np.concatenate([mask, mask], 0).astype(f),
        "k_causal": np.where(g[None, :] <= g[:, None], 0.0, NEG).astype(f),
        "k_dilbias": dil.astype(f),
        "k_decay": decay.astype(f),
        "k_retc": tiles(np.cos(ang2)),
        "k_rets": tiles(np.sin(ang2)),
        "k_dftc": (np.cos(al) / np.sqrt(S)).astype(f),
        "k_dfts": (np.sin(al) / np.sqrt(S)).astype(f),
        "k_dftg": (np.concatenate([np.cos(ag), -np.sin(ag)], 1) / np.sqrt(P)).astype(f),
    }


_INS = ["x", "c", "ctx", "c_ctx", "w_mod", "b_mod", "norm1_g", "norm2_g", "w_in", "q_norm_g", "k_norm_g", "na_rpb",
        "conv_w", "conv_b", "conv_norm_g", "w_branch", "w_out", "w_router", "router_bias", "w_expert_gu",
        "w_expert_down", "final_norm_g", "attn_norm_w_2", "w_in_2", "ret_norm_w_2", "dsa_kv_norm_w_2", "dsa_w_uk_2",
        "dsa_w_uv_2", "w_out_2", "mlp_norm_w_2", "w_up_2", "w_down_2", "final_norm_w_2"]
ONLY_FIRST = False


def kernel(**inputs):
    import numpy as _np
    import concourse.bacc as _bacc
    from concourse import mybir as _mybir
    from concourse.bass_utils import run_bass_kernel_spmd as _run

    arrays = {f"in_{n}_dram": _np.ascontiguousarray(inputs[n]) for n in _INS}
    arrays.update({f"in_{n}_dram": a for n, a in tables().items()})
    turns = {}
    for _ in range(2):
        nc = _bacc.Bacc("TRN2", target_bir_lowering=False, num_devices=1)
        t = {n[3:-5]: nc.dram_tensor(n, a.shape, _mybir.dt.from_np(a.dtype), kind="ExternalInput").ap()
             for n, a in arrays.items()}
        out = nc.dram_tensor("out_0_dram", (1, S, D), _mybir.dt.float32, kind="ExternalOutput").ap()
        program(nc, t, out, turns, ONLY_FIRST)
    r = _run(nc, [arrays], core_ids=[0])
    return r.results[0]["out_0_dram"]
```

```python
from contextlib import ExitStack

import concourse.bass as bass
from concourse import mybir
import numpy as np

F32 = mybir.dt.float32
F32R = mybir.dt.float32r
I32 = mybir.dt.int32
ALU = mybir.AluOpType
ACT = mybir.ActivationFunctionType
AX = mybir.AxisListType

P = 128
D = 1024
S = 512
C = 256
HD = 64
NK = D // P
NT = S // P
NC = C // P
UN = 512
UK = UN // P
SCALE = HD ** -0.5
EPS = 1e-6
NEG = -1.0e30
NTAP = 31
PADT = NTAP // 2
NEXP = 16
FF = 4096
NHEADS = 16
KEYS = S + C
NSEL = 128
TAKEN = -3.0e38
BIG_E = 1.0e30
WIN = 127
V_BMOD, V_N1, V_N2, V_ATT, V_MLP, V_CB, V_CG, V_C, V_CC, V_ALL = 0, 48, 56, 64, 80, 96, 100, 104, 112, 120


class Tally:

    def __init__(self, eng, turns, key, start):
        self.eng, self.turns, self.key = eng, turns, key
        self.n, self.frames, self.loops = dict(start), [], 0

    def at(self, name, k=1):
        v = self.n.get(name, 0) + k
        for i, adds in self.frames:
            if adds.get(name, 0):
                v = i * adds[name] + v
        return v

    def next(self, name, k=1):
        v = self.at(name, k)
        self.skip(name, k)
        return v

    def skip(self, name, k=1):
        self.n[name] = self.n.get(name, 0) + k

    def loop(self, count, body):
        key = (self.key, self.loops)
        self.loops += 1
        before = dict(self.n)
        with self.eng.Fori(0, count) as i:
            self.frames.append((i, self.turns.get(key, {})))
            body(i)
            self.frames.pop()
        got = {s: v - before.get(s, 0) for s, v in self.n.items() if v != before.get(s, 0)}
        self.turns[key] = got
        for s, v in got.items():
            self.n[s] += (count - 1) * v


class Sems(dict):
    def __init__(self, nc, ctx):
        super().__init__()
        self.nc, self.ctx = nc, ctx

    def __missing__(self, name):
        self[name] = self.ctx.enter_context(self.nc.semaphore(name))
        return self[name]


STORES_1 = [("ctx_kv", 0, 2 + 2 * NC), ("ctx_nk", 1, 4), ("ctx_nv", 0, NC), ("q", 1, 4), ("kv", 0, 2 + 2 * NT),
            ("nq", 1, 4), ("nk", 0, 4), ("nv", 1, NT), ("fourier", 0, 1), ("gqa", 1, 1), ("na", 0, 1)]
STORES_2 = [("rqk", 0, 4), ("rv", 1, NT), ("sqk", 0, 4), ("sv", 1, NT), ("dq", 0, 4), ("dk", 1, 4), ("dv", 0, NT)]


def stored(seq, s, upto=None):
    n = 0
    for name, b, k in seq:
        n += 16 * k if b == s else 0
        if name == upto:
            break
    return n


def program(nc, t, out, turns, only_first=False):
    ctx = ExitStack()
    with ctx:
        def sb(name, shape, dt=F32):
            return ctx.enter_context(nc.sbuf_tensor(name, shape, dt))

        def flat(ap):
            return ap.rearrange("p a b -> p (a b)")

        sems = Sems(nc, ctx)

        X = sb("X", [P, NT, D])
        BIG = sb("BIG", [P, NT * D])
        hH, hL = sb("hH", [P, NK, S], F32R), sb("hL", [P, NK, S], F32R)
        aH, aL = sb("aH", [P, UK, S], F32R), sb("aL", [P, UK, S], F32R)
        W = [sb(f"W{i}", [P, UK, UN]) for i in range(2)]
        WH = [sb(f"WH{i}", [P, UK, UN], F32R) for i in range(2)]
        WL = [sb(f"WL{i}", [P, UK, UN], F32R) for i in range(2)]
        ST = [sb(f"ST{i}", [P, UK, S]) for i in range(2)]
        G = sb("G", [P, NK, S])
        Z = sb("Z", [P, 4, S + 2 * PADT])
        F = sb("F", [P, 2, 512])
        AT = sb("AT", [P, 3 * KEYS])
        QS = [sb(f"QS{i}", [P, S]) for i in range(2)]
        KS = [sb(f"KS{i}", [P, KEYS]) for i in range(2)]
        VS = [sb(f"VS{i}", [P, KEYS // P, HD]) for i in range(2)]
        ES = [sb(f"ES{i}", [P, 14, 64]) for i in range(2)]
        VT = sb("VT", [P, V_ALL])
        MOD = sb("MOD", [P, 48, 2])
        CSH, CSL = sb("CSH", [P, NK, 2], F32R), sb("CSL", [P, NK, 2], F32R)
        CF = sb("CF", [P, 2, NK, 2])
        CW = sb("CW", [P, 4, 32])
        AF = sb("AF", [P, 4, NK])
        IDN = sb("IDN", [P, P])
        MSK = sb("MSK", [P, 64])
        CM = sb("CM", [P, P])
        RNW = sb("RNW", [P, 256])
        RB = sb("RB", [P, NEXP])
        WRH, WRL = sb("WRH", [P, NK, NEXP], F32R), sb("WRL", [P, NK, NEXP], F32R)
        GATE = sb("GATE", [P, NT, NEXP])
        SM = sb("SM", [P, 4, 32])
        MX, NM, DEN, RD = (sb(n, [P, 2]) for n in ("MX", "NM", "DEN", "RD"))
        TOP = sb("TOP", [P, 8])
        WIX = sb("WIX", [P, NT, 8])

        BKP = ctx.enter_context(nc.psum_tensor("BKP", [P, 2048], F32))
        BK = [BKP[:, i * 512:(i + 1) * 512] for i in range(4)]
        SC = ctx.enter_context(nc.psum_tensor("SCP", [P, 1024], F32))
        TP = ctx.enter_context(nc.psum_tensor("TPP", [P, 1024], F32))
        OB = [BK[0][:, 0:HD], BK[1][:, 0:HD]]
        OT = [BK[s][s * HD:(s + 1) * HD, :] for s in range(2)]
        SCS = [SC[:, :], BKP[:, 1024:2048]]

        qT_d = nc.dram_tensor("qT_scratch", (NHEADS, HD, S), F32).ap()
        kT_d = nc.dram_tensor("kT_scratch", (NHEADS, HD, KEYS), F32).ap()
        v_d = nc.dram_tensor("v_scratch", (NHEADS, KEYS, HD), F32).ap()
        yT_d = nc.dram_tensor("yT_scratch", (4, 512, S), F32).ap()
        rpb_d = nc.dram_tensor("rpb_scratch", (8 * 15, 64, WIN), F32).ap()

        XN = BIG[:].rearrange("p (t d) -> p t d", t=NT)
        BV = BIG[:].rearrange("p (k s) -> p k s", k=NK)
        cH = flat(aH[:]).rearrange("p (k s) -> p k s", k=NK)
        cL = flat(aL[:]).rearrange("p (k s) -> p k s", k=NK)
        CTX = [flat(ST[i][:])[:, 0:D] for i in range(2)]
        CTN = flat(G[:])[:, 0:2 * D].rearrange("p (t d) -> p t d", t=2)
        TM = AT[:, 0:NT * 512].rearrange("p (t c) -> p t c", t=NT)
        T1, T2 = G[:, 0:4, :], G[:, 4:8, :]
        PR = [AT[:, b * KEYS:(b + 1) * KEYS] for b in range(2)]
        SB = [AT[:, 2 * KEYS:3 * KEYS], flat(W[1][:, 2:4, :])[:, 0:KEYS]]
        PTB_1 = [(W[0][:], W[1][:, 0:2, :]), (BV[:, 0:4, :], BV[:, 4:6, :])]
        PTB_2 = [(W[0][:],), (XN[:, :, 256:768],)]
        QX = [flat(WH[s][:])[:, 0:S] for s in range(2)]
        KX = [flat(WH[s][:])[:, S:S + KEYS] for s in range(2)]
        KL = [flat(WH[s][:])[0:HD, S + KEYS:S + 2 * KEYS] for s in range(2)]
        GB = AT[:, 0:D]
        DG = AT[:, 2048:2304]
        VR = F[0:V_ALL, 0, 0:P]
        CWR = F[0:NTAP, 1, :]
        WR = Z[:, 0, 0:NK * NEXP].rearrange("p (k e) -> p k e", k=NK)
        RPB = Z[0:120, 1, 0:WIN]
        RC = flat(ES[1][:])[:, 0:256].rearrange("p (t d) -> p t d", t=NT)
        RS = flat(ES[1][:])[:, 256:512].rearrange("p (t d) -> p t d", t=NT)
        GQ, GK = flat(ES[1][:])[:, 512:576], flat(ES[1][:])[:, 576:640]
        KNW = flat(ES[1][:])[:, 512:640]
        ONE = AT[:, 1024:1152]
        TC = flat(ES[1][:])[:, 0:128].rearrange("p (t d) -> p t d", t=NT)
        TS = flat(ES[1][:])[:, 128:256].rearrange("p (t d) -> p t d", t=NT)
        XB = flat(ES[0][:])[:, 0:S]
        UKW, UVW = flat(ES[0][:])[:, 0:256], flat(ES[0][:])[:, 256:512]
        CU, CT = G[:, 0:4, :], G[:, 4:8, :]
        ZF = flat(Z[:])
        CKT, KIT = ZF[:, 0:512], ZF[:, 512:1024]
        SG = ZF[:, 1024:2048].rearrange("p (t c) -> p t c", t=NT)
        SEL, QI = G[:, 0:4, :], G[:, 4:8, :]
        IXA, IXW = AT[:, 0:512], AT[:, 512:1024]
        RP = TM
        RT = lambda n: F[:, 0, n * 64:(n + 1) * 64].rearrange("p (t e) -> p t e", t=NT)
        RT2 = lambda n, w: F[:, 1, n * 64:n * 64 + NT * w].rearrange("p (t e) -> p t e", t=NT)

        block = ctx.enter_context(nc.Block())
        BANKS = [f"bank_free{j}" for j in range(4)]

        @block.sync
        def _(sp):
            T = Tally(sp, turns, "sp", {})
            slot = [0]

            def unit(src, n=UN):
                s = slot[0]
                slot[0] ^= 1
                sp.wait_ge(sems["w_lo"], T.next("w_lo"))
                sp.dma_start(W[s][:, :, 0:n], src.rearrange("(k p) n -> p k n", p=P)).then_inc(sems[f"w_landed{s}"], 16)

            def blk(w, col, n=UN):
                for r in range(2):
                    unit(w[r * UN:(r + 1) * UN, bass.ds(col, n)], n)

            def load(dst, src, name):
                sp.dma_start(dst, src).then_inc(sems[name], 16)

            def row(ap, n):
                return ap.rearrange("(o n) -> o n", o=1).to_broadcast([P, n])

            def pick(ap, l):
                return ap[bass.ds(l, 1)].rearrange("a k n -> (a k) n")

            rows = lambda ap: ap.rearrange("(r p) -> r p", p=P)
            load(VR[V_BMOD:V_N1, :], rows(t["b_mod"][0]), "vec_landed")
            load(VR[V_N1:V_N2, :], rows(t["norm1_g"][0]), "vec_landed")
            load(VR[V_N2:V_ATT, :], rows(t["norm2_g"][0]), "vec_landed")
            load(VR[V_ATT:V_MLP, :], t["attn_norm_w_2"].rearrange("l (r p) -> (l r) p", p=P), "vec_landed")
            load(VR[V_MLP:V_CB, :], t["mlp_norm_w_2"].rearrange("l (r p) -> (l r) p", p=P), "vec_landed")
            load(VR[V_CB:V_CG, :], rows(t["conv_b"][0]), "vec_landed")
            load(VR[V_CG:V_C, :], rows(t["conv_norm_g"][0]), "vec_landed")
            load(VR[V_C:V_CC, :], rows(t["c"][0]), "vec_landed")
            load(VR[V_CC:V_ALL, :], rows(t["c_ctx"]), "vec_landed")
            load(CWR, t["conv_w"][0], "vec_landed")
            load(IDN[:], t["k_ident"], "vec_landed")
            load(WR, t["w_router"].rearrange("(k p) e -> p k e", p=P), "wr_landed")
            for i in range(NT):
                load(X[:, i, :], t["x"][0, i * P:(i + 1) * P, :], "x_landed")
            for i in range(NC):
                load(CTX[i], t["ctx"][0, i * P:(i + 1) * P, :], "x_landed")
            sp.wait_ge(sems["rpb_zero"], T.next("rpb_zero"))
            load(RPB[:, 48:79], t["na_rpb"][0].rearrange("h m c -> (h m) c"), "rpb_landed")
            load(RC, t["k_ropec"], "tab_landed")
            load(RS, t["k_ropes"], "tab_landed")
            load(GQ, row(t["q_norm_g"][0], HD), "tab_landed")
            load(GK, row(t["k_norm_g"][0], HD), "tab_landed")
            load(MSK[:], t["k_colmask"], "tab_landed")
            load(CM[:], t["k_causal"], "tab_landed")
            load(RB[:], row(t["router_bias"], NEXP), "tab_landed")

            T.loop(12, lambda i: blk(t["w_mod"][0], i * UN))
            w = t["w_in"][0]
            sp.wait_ge(sems["rpb_landed"], T.next("rpb_landed", 16))
            for h, (col, n) in enumerate(((512, 256), (1280, UN), (1792, UN), (0, UN), (512, 256), (768, UN), (1280, UN),
                                          (1792, UN))):
                blk(w, col, n)
                load(rpb_d[h * 15:(h + 1) * 15], RPB[h * 15:(h + 1) * 15, :].unsqueeze(1).to_broadcast([15, 64, WIN]),
                     "rpb_stored")
            blk(w, 2304)
            sp.wait_ge(sems["norm_tr"], T.next("norm_tr", NK))
            load(BV[:, 0:4, :], t["k_dftc"].rearrange("(k p) s -> p k s", p=P), "fou_landed")
            load(BV[:, 4:8, :], t["k_dfts"].rearrange("(k p) s -> p k s", p=P), "fou_landed")
            sp.wait_ge(sems["nv_out"], T.next("nv_out"))
            load(DG, t["k_dftg"], "fou_landed")
            blk(w, 3328)
            blk(w, 2816)

            def heads(count, base, nk, bias=None):
                def qk(h, s):
                    for r in range(2):
                        load(QS[s][r * HD:(r + 1) * HD, :], pick(qT_d, h), f"qk_landed{s}")
                        load(KS[s][r * HD:(r + 1) * HD, 0:nk], pick(kT_d, h)[:, 0:nk], f"qk_landed{s}")

                def vb(h, s):
                    load(VS[s][:, 0:nk // P, :], pick(v_d, h)[0:nk, :].rearrange("(t p) d -> p t d", p=P), f"head_landed{s}")
                    if bias is not None:
                        bias(h - base, s, f"head_landed{s}")
                for s in range(2):
                    qk(base + s, s)
                for s in range(2):
                    vb(base + s, s)
                T.skip("head_oe", 2)

                def later(i):
                    for s in range(2):
                        sp.wait_ge(sems["head_lo"], T.next("head_lo"))
                        qk(i * 2 + (base + 2 + s), s)
                    for s in range(2):
                        sp.wait_ge(sems["head_oe"], T.next("head_oe"))
                        vb(i * 2 + (base + 2 + s), s)
                T.loop(count // 2 - 1, later)
                T.skip("head_lo", 2)
                sp.wait_ge(sems["head_oe"], T.next("head_oe", 2))
                sp.sem_inc(sems["sp_paused"], 1)

            def retention_heads():
                def head(h, s):
                    load(QS[s][0:HD, :], pick(qT_d, h), f"head_landed{s}")
                    load(KS[s][0:HD, 0:S], pick(kT_d, h)[:, 0:S], f"head_landed{s}")
                    load(VS[s][:, 0:NT, :], pick(v_d, h)[0:S, :].rearrange("(t p) d -> p t d", p=P), f"head_landed{s}")
                    load(flat(ES[s][:])[:, 0:S], pick(t["k_decay"], h), f"head_landed{s}")
                for s in range(2):
                    head(s, s)
                for s in range(2):
                    sp.wait_ge(sems["ret_oe"], T.next("ret_oe", NT))
                    head(2 + s, s)
                sp.wait_ge(sems["ret_oe"], T.next("ret_oe", 2 * NT))
                sp.sem_inc(sems["sp_paused"], 1)

            for s in range(2):
                sp.wait_ge(sems[f"st_written{s}"], T.at(f"st_written{s}", stored(STORES_1, s, "nv" if s else "nk")))

            heads(8, 0, KEYS)
            sp.wait_ge(sems["rpb_stored"], T.at("rpb_stored", 16 * 8))

            def na_bias(h, s, sem):
                for rr in range(2):
                    src = bass.AP(rpb_d.tensor, h * (15 * 64 * WIN) + ((1 - rr) * 64 * WIN + 63),
                                  [[WIN - 1, 64], [64 * WIN, 14], [1, 64]])
                    load(ES[s][rr * 64:(rr + 1) * 64, :, :], src, sem)
            heads(8, 8, KEYS, na_bias)

            for s in range(2):
                sp.wait_ge(sems[f"st_written{s}"], T.next(f"st_written{s}", stored(STORES_1, s)))
            sp.wait_ge(sems["cv_written"], T.next("cv_written", 16))

            def branch(i):
                sp.wait_ge(sems["yb_used"], T.next("yb_used"))
                load(ST[1][:], pick(yT_d, i).rearrange("(k p) s -> p k s", p=P), "yb_landed")
                blk(w, i * D + 3840)
                blk(w, i * D + (3840 + UN))
                for hf in range(2):
                    unit(pick(t["w_branch"][0], i)[:, hf * UN:(hf + 1) * UN])
            T.loop(4, branch)
            blk(t["w_out"][0], 0)
            blk(t["w_out"][0], UN)

            def expert(e):
                gu = pick(t["w_expert_gu"][0], e)
                blk(gu, 0)
                blk(gu, UN)
                for hf in range(2):
                    unit(pick(t["w_expert_down"][0], e)[:, hf * UN:(hf + 1) * UN])
            T.loop(NEXP, expert)
            sp.wait_ge(sems["moe_done"], T.next("moe_done"))
            load(flat(G[:])[:, 0:D], row(t["final_norm_g"], D), "gf_landed")

            def layer(l):
                w2 = pick(t["w_in_2"], l)
                sp.wait_ge(sems["es_free"], T.next("es_free"))
                load(TC, t["k_retc"], "lay_landed")
                load(TS, t["k_rets"], "lay_landed")
                load(UKW, pick(t["dsa_w_uk_2"], l), "lay_landed")
                load(UVW, pick(t["dsa_w_uv_2"], l), "lay_landed")
                load(KNW, t["dsa_kv_norm_w_2"][bass.ds(l, 1), :].to_broadcast([P, P]), "lay_landed")
                load(RNW[:], t["ret_norm_w_2"].rearrange("l h d -> l (h d)")[bass.ds(l, 1), :].to_broadcast([P, 256]), "lay_landed")
                blk(w2, 0)
                blk(w2, UN)
                blk(w2, 1024, 384)
                blk(w2, 1408)
                blk(w2, 1920, 72)
                for b in range(3):
                    blk(w2, 1992 + b * UN)
                for s in range(2):
                    sp.wait_ge(sems[f"st_written{s}"], T.next(f"st_written{s}", stored(STORES_2, s)))
                retention_heads()
                load(XB, t["k_dilbias"], "xb_landed")
                heads(4, 4, S)
                heads(8, 8, S)
                wo = pick(t["w_out_2"], l)
                blk(wo, 0)
                blk(wo, UN)

                def chunk(c):
                    blk(pick(t["w_up_2"], l), c * UN)
                    for hf in range(2):
                        unit(t["w_down_2"][bass.ds(l, 1), bass.ds(c * UN, UN), hf * UN:(hf + 1) * UN]
                             .rearrange("a k n -> (a k) n"))
                sp.sem_inc(sems["sp_paused"], 1)
                T.loop(FF // UN, chunk)
            if not only_first:
                T.loop(2, layer)
                sp.wait_ge(sems["mlp_done"], T.next("mlp_done", 2))
                load(flat(G[:])[:, 0:D], row(t["final_norm_w_2"], D), "gf_landed")
            for i in range(NT):
                sp.wait_ge(sems["out_ready"], T.next("out_ready"))
                sp.dma_start(out[0, i * P:(i + 1) * P, :], XN[:, i, :]).then_inc(sems["out_written"], 16)
            sp.wait_ge(sems["out_written"], T.next("out_written", 16 * NT))

        @block.gpsimd
        def _(pool):
            T = Tally(pool, turns, "pool", {})
            pool.memset(RPB, 0.0).then_inc(sems["rpb_zero"], 1)

            def store(seq, name, dmas):
                s = [b for n, b, _ in seq if n == name][0]
                assert len(dmas) == [k for n, _, k in seq if n == name][0], name
                pool.wait_ge(sems[name + "_out"], T.next(name + "_out"))
                pool.sem_inc(sems["pool_paused"], 1)
                for dst, src in dmas:
                    pool.dma_start(dst, src).then_inc(sems[f"st_written{s}"], 16)

            def qk(dst, s, b0=0, nb=4):
                return [(dst[2 * b:2 * b + 2].rearrange("h d s -> (h d) s"), ST[s][:, b0 + b, 0:dst.shape[2]])
                        for b in range(nb)]

            def vv(dst, s, nt):
                nh = dst.shape[0]
                return [(dst[:, i * P:(i + 1) * P, :].rearrange("h p d -> p h d"),
                         ST[s][:, i, 0:nh * HD].rearrange("p (h d) -> p h d", h=nh)) for i in range(nt)]

            def kv(s, c0, nt):
                dm = []
                vt = flat(ST[s][:, 2:4, :]).rearrange("p (t c) -> p t c", t=8)
                for g in range(2):
                    dm.append((kT_d[4 * g:4 * g + 4, :, c0:c0 + nt * P].rearrange("r d s -> d r s"),
                               ST[s][g * HD:(g + 1) * HD, 0, 0:nt * P].unsqueeze(1).to_broadcast([HD, 4, nt * P])))
                    for i in range(nt):
                        dm.append((v_d[4 * g:4 * g + 4, c0 + i * P:c0 + (i + 1) * P, :].rearrange("r p d -> p r d"),
                                   vt[:, i, g * HD:(g + 1) * HD].unsqueeze(1).to_broadcast([P, 4, HD])))
                return dm

            store(STORES_1, "ctx_kv", kv(0, S, NC))
            store(STORES_1, "ctx_nk", qk(kT_d[8:16, :, S:KEYS], 1))
            store(STORES_1, "ctx_nv", vv(v_d[8:16, S:KEYS, :], 0, NC))
            store(STORES_1, "q", qk(qT_d[0:8], 1))
            store(STORES_1, "kv", kv(0, 0, NT))
            store(STORES_1, "nq", qk(qT_d[8:16], 1))
            store(STORES_1, "nk", qk(kT_d[8:16, :, 0:S], 0))
            store(STORES_1, "nv", vv(v_d[8:16, 0:S, :], 1, NT))
            store(STORES_1, "fourier", [(yT_d[2].rearrange("(k p) s -> p k s", p=P), ST[0][:])])

            pool.wait_ge(sems["z_ready"], T.next("z_ready"))
            pool.memset(CU, 0.0).then_inc(sems["pool_self"], 1)
            pool.wait_ge(sems["pool_self"], T.next("pool_self"))

            def tap(k):
                pool.tensor_tensor(CT, Z[:, :, bass.ds(k, S)], CW[:, :, bass.ds(k, 1)].to_broadcast([P, 4, S]),
                                   ALU.mult).then_inc(sems["pool_self"], 1)
                pool.wait_ge(sems["pool_self"], T.next("pool_self"))
                pool.tensor_tensor(CU, CU, CT, ALU.add).then_inc(sems["pool_self"], 1)
                pool.wait_ge(sems["pool_self"], T.next("pool_self"))
            T.loop(NTAP, tap)
            pool.sem_inc(sems["conv_done"], 1)
            store(STORES_1, "gqa", [(yT_d[0].rearrange("(k p) s -> p k s", p=P), ST[1][:])])
            store(STORES_1, "na", [(yT_d[1].rearrange("(k p) s -> p k s", p=P), ST[0][:])])
            pool.wait_ge(sems["cv_out"], T.next("cv_out"))
            pool.dma_start(yT_d[3].rearrange("(k p) s -> p k s", p=P), CU).then_inc(sems["cv_written"], 16)

            def layer(l):
                store(STORES_2, "rqk", qk(qT_d[0:4], 0, 0, 2) + qk(kT_d[0:4, :, 0:S], 0, 2, 2))
                store(STORES_2, "rv", vv(v_d[0:4, 0:S, :], 1, NT))
                store(STORES_2, "sqk", qk(qT_d[4:8], 0, 0, 2) + qk(kT_d[4:8, :, 0:S], 0, 2, 2))
                store(STORES_2, "sv", vv(v_d[4:8, 0:S, :], 1, NT))
                store(STORES_2, "dq", qk(qT_d[8:16], 0))
                store(STORES_2, "dk", qk(kT_d[8:16, :, 0:S], 1))
                store(STORES_2, "dv", vv(v_d[8:16, 0:S, :], 0, NT))
            if not only_first:
                T.loop(2, layer)
            for s in range(2):
                pool.wait_ge(sems[f"st_written{s}"],
                             stored(STORES_1, s) + (0 if only_first else 2 * stored(STORES_2, s)))
            pool.wait_ge(sems["cv_written"], 16)

        @block.tensor
        def _(pe):
            T = Tally(pe, turns, "pe", {"w_lo": 2, "yb_used": 1})
            slot = [0]
            h, cx, aa, cs = (hH[:], hL[:]), (cH, cL), (aH[:], aL[:]), (CSH[:], CSL[:])

            def unit(act, k0, form, n, start, stop, nj=4):
                s = slot[0]
                slot[0] ^= 1
                pe.wait_ge(sems["w_lo"], T.next("w_lo"))
                ah, al = act
                cols = n if form == "T" else ah.shape[2]
                for j in range(nj):
                    if start:
                        pe.wait_ge(sems[BANKS[j]], T.at(BANKS[j]))
                    q = []
                    for k in range(UK):
                        for wp, ap in ((WH, ah), (WL, ah), (WH, al)):
                            if form == "F":
                                q.append((wp[s][:, k, j * P:(j + 1) * P], ap[:, k0 + k, :]))
                            else:
                                q.append((ap[:, k0 + k, j * P:(j + 1) * P], wp[s][:, k, 0:n]))
                    for a, (lt, rh) in enumerate(q):
                        mm = pe.matmul(BK[j][:, 0:cols], lt, rh, start=start and a == 0,
                                       stop=stop and a == len(q) - 1, skip_group_check=True)
                    mm.then_inc(sems["gemm_done"], 4 // nj)
                if start:
                    for b in BANKS:
                        T.skip(b)

            def blk(act, form, n=UN, nj=4):
                unit(act, 0, form, n, True, False, nj)
                unit(act, 4, form, n, False, True, nj)

            def turn(name, src, nt, nk):
                for k in range(nk):
                    if k >= 2:
                        pe.wait_ge(sems[name + "_free"], T.next(name + "_free"))
                    for i in range(nt):
                        c0 = (k % 2) * 512 + i * P
                        mm = pe.transpose(TP[:, c0:c0 + P], src(i, k), IDN[:])
                    mm.then_inc(sems[name + "_tr"], 1)
                pe.wait_ge(sems[name + "_free"], T.next(name + "_free", min(2, nk)))

            cols_of = lambda v: (lambda i, k: v[:, i, k * P:(k + 1) * P])

            pe.wait_ge(sems["vec_landed"], T.next("vec_landed", 16 * 11))
            pe.transpose(TP[:, 0:V_ALL], VR, IDN[0:V_ALL, 0:V_ALL])
            for j in range(4):
                mm = pe.transpose(TP[:, 128 + j * 32:128 + j * 32 + NTAP], CWR[:, j * P:(j + 1) * P],
                                  IDN[0:NTAP, 0:NTAP])
            mm.then_inc(sems["vec_tr"], 1)
            pe.wait_ge(sems["cs_lo"], T.next("cs_lo"))

            def mod(i):
                for half in range(2):
                    s = slot[0]
                    slot[0] ^= 1
                    pe.wait_ge(sems["w_lo"], T.next("w_lo"))
                    if half == 0:
                        pe.wait_ge(sems["bank_free0"], T.next("bank_free0"))
                    q = [(a, w[s][:, k, :], half * 4 + k) for k in range(UK) for a, w in ((CSH, WH), (CSH, WL), (CSL, WH))]
                    for n, (a, w, k) in enumerate(q):
                        mm = pe.matmul(BK[0][0:2, :], a[:, k, :], w, start=half == 0 and n == 0,
                                       stop=half == 1 and n == len(q) - 1, skip_group_check=True)
                    mm.then_inc(sems["gemm_done"], 4)
                pe.wait_ge(sems["mod_row"], T.next("mod_row"))
                pe.wait_ge(sems["mod_out"], T.next("mod_out"))
                pe.sem_inc(sems["pe_paused"], 1)
                for j in range(4):
                    mm = pe.transpose(TP[:, j * 2:j * 2 + 2], F[0:2, 0, j * P:(j + 1) * P], IDN[0:2, 0:2])
                mm.then_inc(sems["mod_col"], 1)
            T.loop(12, mod)
            pe.wait_ge(sems["mod_out"], T.next("mod_out"))
            pe.wait_ge(sems["norm_xn"], T.next("norm_xn", NC))
            turn("norm", cols_of(CTN), NC, NK)
            pe.wait_ge(sems["norm_xn"], T.next("norm_xn", NT))
            turn("norm", cols_of(XN), NT, NK)
            pe.wait_ge(sems["norm_lo"], T.next("norm_lo", NK))
            blk(cx, "T", 256, 2)
            blk(cx, "F")
            pe.wait_ge(sems["ck_rms"], T.next("ck_rms"))
            turn("sink", cols_of(TM), NC, 1)
            blk(cx, "T", UN, 2)
            pe.wait_ge(sems["norm_lo"], T.next("norm_lo", NK))
            blk(h, "T")
            pe.wait_ge(sems["q_rope"], T.next("q_rope"))
            turn("sink", cols_of(TM), NT, 4)
            blk(h, "T", 256)
            blk(h, "F")
            pe.wait_ge(sems["k_rope"], T.next("k_rope"))
            turn("sink", cols_of(TM), NT, 1)
            blk(h, "F")
            blk(h, "T")
            blk(h, "T")
            pe.wait_ge(sems["fou_landed"], T.next("fou_landed", 48))
            pe.wait_ge(sems["fou_in"], T.next("fou_in"))
            for g in range(4):
                for part in range(2):
                    for k in range(4):
                        mm = pe.matmul(SC[:, part * 512:(part + 1) * 512], TM[:, k, g * P:(g + 1) * P],
                                       BV[:, part * 4 + k, :], start=k == 0, stop=k == 3)
                mm.then_inc(sems["fo_a"], 1)
                pe.wait_ge(sems["fo_cp"], T.next("fo_cp"))
                if g:
                    pe.wait_ge(sems["fo_o"], T.next("fo_o"))
                for part in range(2):
                    mm = pe.matmul(TP[:, 0:512], DG[:, part * P:(part + 1) * P], F[:, part, :],
                                   start=part == 0, stop=part == 1)
                mm.then_inc(sems["fo_b"], 1)
            pe.wait_ge(sems["fo_o"], T.next("fo_o"))
            blk(h, "F")
            blk(h, "F")

            def attend(count, loads, keys, PTB):
                chunks = lambda n: range(0, keys(n % NT), 512)

                def scores(n):
                    s, tt = (n // NT) % 2, n % NT
                    if tt == 0:
                        pe.wait_ge(sems["head_lo"], T.next("head_lo"))
                    nk = keys(tt)
                    for c0 in range(0, nk, 512):
                        c1 = min(nk, c0 + 512)
                        dst = SCS[n % 2][:, c0:c1]
                        pe.matmul(dst, QX[s][:, tt * P:(tt + 1) * P], KX[s][:, c0:c1], start=True, stop=False,
                                  skip_group_check=True)
                        mm = pe.matmul(dst, QX[s][0:HD, tt * P:(tt + 1) * P], KL[s][:, c0:c1], start=False, stop=True,
                                       skip_group_check=True)
                    mm.then_inc(sems["head_s"], 1)

                def turned(n):
                    pe.wait_ge(sems["head_pn"], T.next("head_pn"))
                    for c, c0 in enumerate(chunks(n)):
                        pe.wait_ge(sems["head_ptc"], T.next("head_ptc:free"))
                        bank = (n if len(chunks(n)) == 1 else c) % 2 * 512
                        for k0 in range(c0, min(c0 + 512, keys(n % NT)), P):
                            mm = pe.transpose(TP[:, bank + k0 - c0:bank + k0 - c0 + P], PR[n % 2][:, k0:k0 + P], IDN[:])
                        mm.then_inc(sems["head_pt"], 1)

                def values(s):
                    done = sum(len(chunks(tt)) for tt in range(NT))
                    pe.wait_ge(sems["head_ptc"], T.next("head_ptc:full", done))
                    pe.wait_ge(sems["head_oe"], T.next("head_oe"))
                    pe.wait_ge(sems[f"head_landed{s}"], T.next(f"head_landed{s}", 16 * loads))
                    nk = keys(NT - 1) // P
                    for kt in range(nk):
                        q0 = kt * P if keys(0) == P else 0
                        mm = pe.matmul(OT[s][:, q0:S], VS[s][:, kt, :], PTB[s][kt // 4][:, kt % 4, q0:S], start=kt == 0,
                                       stop=kt == nk - 1, skip_group_check=True)
                    mm.then_inc(sems["head_o"], 1)

                def body(first, last):
                    for n in range(2 * NT):
                        turned(n)
                        if n + 2 < 2 * NT or not last:
                            scores(n + 2)
                        if n % NT == 0 and not (first and n == 0):
                            values(1 if n == 0 else 0)
                for b in BANKS:
                    pe.wait_ge(sems[b], T.at(b))
                pe.sem_inc(sems["head_o"], 2)
                T.skip("head_ptc:full", 2)
                scores(0)
                scores(1)
                body(True, False)
                pe.sem_inc(sems["pe_paused"], 1)
                if count > 4:
                    T.loop(count // 2 - 2, lambda i: body(False, False))
                body(False, True)
                values(1)
                T.skip("head_ptc:free", 2)
                pe.wait_ge(sems["head_oe"], T.next("head_oe", 2))

            attend(8, 1, lambda tt: KEYS, PTB_1)
            attend(8, 3, lambda tt: KEYS, PTB_1)
            pe.wait_ge(sems["cv_sq"], T.next("cv_sq"))
            for j in range(4):
                mm = pe.matmul(SC[:, 0:512], ONE, CT[:, j, :], start=j == 0, stop=j == 3)
            mm.then_inc(sems["cv_pe"], 1)
            pe.wait_ge(sems["cv_r"], T.next("cv_r"))

            def branch(i):
                blk(h, "F")
                blk(h, "F")
                pe.wait_ge(sems["yb_used"], T.next("yb_used"))
                unit(aa, 0, "F", UN, True, True)
                unit(aa, 0, "F", UN, True, True)
            T.loop(4, branch)

            def spread(name):
                pe.wait_ge(sems[name + "_in"], T.next(name + "_in"))
                for k in range(NK):
                    mm = pe.matmul(SC[:, k * P:(k + 1) * P], flat(ST[0][:])[:, k * P:(k + 1) * P], IDN[:],
                                   start=True, stop=True, skip_group_check=True)
                mm.then_inc(sems[name + "_pe"], 1)
                pe.wait_ge(sems[name + "_gb"], T.next(name + "_gb"))
            spread("g1")
            pe.wait_ge(sems["norm_lo"], T.next("norm_lo", NK))
            blk(h, "T")
            blk(h, "T")
            pe.wait_ge(sems["norm_xn"], T.next("norm_xn", NT))
            turn("norm", cols_of(XN), NT, NK)
            pe.wait_ge(sems["norm_lo"], T.next("norm_lo", NK))
            pe.wait_ge(sems["wr_lo"], T.next("wr_lo"))
            for i in range(NT):
                q = [(a, b, k) for k in range(NK) for a, b in ((hH, WRH), (hH, WRL), (hL, WRH), (hL, WRL))]
                for n, (a, b, k) in enumerate(q):
                    mm = pe.matmul(TP[:, i * NEXP:(i + 1) * NEXP], a[:, k, i * P:(i + 1) * P], b[:, k, :],
                                   start=n == 0, stop=n == len(q) - 1, skip_group_check=True)
            mm.then_inc(sems["rt_pe"], 1)

            def expert(e):
                blk(h, "F")
                blk(h, "F")
                pe.wait_ge(sems["hid_lo"], T.next("hid_lo", 4))
                unit(aa, 0, "T", UN, True, True)
                unit(aa, 0, "T", UN, True, True)
            T.loop(NEXP, expert)
            spread("g2")

            def layer(l):
                pe.wait_ge(sems["norm_xn"], T.next("norm_xn", NT))
                turn("norm", cols_of(XN), NT, NK)
                pe.wait_ge(sems["norm_lo"], T.next("norm_lo", NK))
                blk(h, "T")
                blk(h, "T")
                pe.wait_ge(sems["rqk_rope"], T.next("rqk_rope"))
                turn("sink", cols_of(TM), NT, 4)
                blk(h, "T", 384)
                blk(h, "F")
                pe.wait_ge(sems["lat_rms"], T.next("lat_rms"))
                turn("sink", cols_of(TM), NT, 3)
                blk(h, "T", 72)
                pe.wait_ge(sems["lay_landed"], T.next("lay_landed", 16 * 6))
                for b in range(2):
                    mm = pe.matmul(SC[:, b * 512:(b + 1) * 512], UKW[:, b * P:(b + 1) * P], CKT, start=True, stop=True)
                for i in range(NT):
                    mm = pe.matmul(TP[:, i * 256:(i + 1) * 256], CKT[:, i * P:(i + 1) * P], UVW,
                                   start=True, stop=True, skip_group_check=True)
                mm.then_inc(sems["uk_pe"], 1)
                pe.wait_ge(sems["uk_cp"], T.next("uk_cp"))
                pe.wait_ge(sems["ki_out"], T.next("ki_out"))
                turn("sink", cols_of(TM), NT, 1)
                blk(h, "F")
                blk(h, "F")
                blk(h, "T")
                n = 0
                for tt in range(1, NT):
                    nk = (tt + 1) * P
                    for ih in range(8):
                        if n >= 2:
                            pe.wait_ge(sems["ix_act"], T.next("ix_act"))
                        p0 = (ih % 2) * HD
                        pe.matmul(SC[:, (n % 2) * 512:(n % 2) * 512 + nk],
                                  QI[p0:p0 + HD, ih // 2, tt * P:(tt + 1) * P], KIT[p0:p0 + HD, 0:nk],
                                  start=True, stop=True).then_inc(sems["ix_pe"], 1)
                        n += 1
                pe.wait_ge(sems["ix_act"], T.next("ix_act", 2))
                pe.wait_ge(sems["sel_done"], T.next("sel_done"))

                def ret(i):
                    for s in range(2):
                        pe.wait_ge(sems[f"head_landed{s}"], T.next(f"head_landed{s}", 64))
                        for kt in range(NT):
                            if kt >= 2:
                                pe.wait_ge(sems["ret_d"], T.next("ret_d"))
                            bank = SC if kt % 2 == 0 else TP
                            pe.matmul(bank[:, 0:S - kt * P], KS[s][0:HD, kt * P:(kt + 1) * P], QS[s][0:HD, kt * P:S],
                                      start=True, stop=True, skip_group_check=True).then_inc(sems["ret_s"], 1)
                        pe.wait_ge(sems["ret_d"], T.next("ret_d", 2))
                        for tt in range(NT):
                            if tt:
                                pe.wait_ge(sems["ret_oe"], T.next("ret_oe"))
                            for kt in range(tt + 1):
                                mm = pe.matmul(OB[tt % 2], RP[:, kt, (tt - kt) * P:(tt - kt + 1) * P],
                                               VS[s][:, kt, :], start=kt == 0, stop=kt == tt, skip_group_check=True)
                            mm.then_inc(sems["ret_o"], 1)
                        pe.wait_ge(sems["ret_oe"], T.next("ret_oe"))
                for b in BANKS[:2]:
                    pe.wait_ge(sems[b], T.at(b))
                pe.sem_inc(sems["pe_paused"], 1)
                T.loop(2, ret)
                attend(4, 1, lambda tt: (tt + 1) * P, PTB_2)
                attend(8, 1, lambda tt: (tt + 1) * P, PTB_2)
                pe.wait_ge(sems["mix_ready"], T.next("mix_ready"))
                turn("norm", cols_of(XN), NT, 2)
                pe.wait_ge(sems["norm_lo"], T.next("norm_lo", 2))
                blk(h, "T")
                blk(h, "T")
                pe.wait_ge(sems["norm_xn"], T.next("norm_xn", NT))
                turn("norm", cols_of(XN), NT, NK)
                pe.wait_ge(sems["norm_lo"], T.next("norm_lo", NK))

                def chunk(c):
                    blk(h, "F")
                    pe.wait_ge(sems["mlp_lo"], T.next("mlp_lo", 4))
                    unit(aa, 0, "T", UN, True, True)
                    unit(aa, 0, "T", UN, True, True)
                pe.sem_inc(sems["pe_paused"], 1)
                T.loop(FF // UN, chunk)
            if not only_first:
                T.loop(2, layer)

        @block.scalar
        def _(act):
            T = Tally(act, turns, "act", {b: 1 for b in BANKS})
            T.n["gemm_done:out"] = 8
            slot = [0]

            def hi():
                s = slot[0]
                slot[0] ^= 1
                act.wait_ge(sems[f"w_landed{s}"], T.next(f"w_landed{s}", 16))
                act.wait_ge(sems["gemm_done"], T.next("gemm_done:w", 4))
                act.activation(WH[s][:], W[s][:], ACT.Copy).then_inc(sems["w_hi"], 1)

            def unit(evac=None, more=True):
                if more:
                    hi()
                T.skip("gemm_done:out", 4)
                if evac is not None:
                    T.skip("gemm_done:out", -4)
                    evac()
                    T.skip("gemm_done:out", 4)

            def blk(evac=None, more=True):
                unit()
                unit(evac, more)
                for b in BANKS:
                    T.skip(b)

            def out(j, nj=4):
                act.wait_ge(sems["gemm_done"], T.at("gemm_done:out", (j + 1) * (4 // nj)))

            def copies(dst, cols=UN, nj=4, ready=None):
                def go():
                    for j in range(nj):
                        out(j, nj)
                        act.activation(dst(j), BK[j][:, 0:cols], ACT.Copy).then_inc(sems[BANKS[j]], 1)
                    for j in range(nj, 4):
                        act.sem_inc(sems[BANKS[j]], 1)
                    if ready:
                        act.wait_ge(sems[BANKS[nj - 1]], T.at(BANKS[nj - 1]))
                        act.sem_inc(sems[ready], 1)
                return go

            held = {0: 0, 1: 0}

            def begin(seq, name):
                s = [b for n, b, _ in seq if n == name][0]
                if held[s]:
                    act.wait_ge(sems[f"st_written{s}"], T.next(f"st_written{s}", held[s]))
                held[s] = 16 * [k for n, _, k in seq if n == name][0]
                return s

            def sink(name, nk, dst, w=S):
                for k in range(nk):
                    act.wait_ge(sems[name + "_tr"], T.next(name + "_tr"))
                    act.activation(dst(k), TP[:, (k % 2) * 512:(k % 2) * 512 + w], ACT.Copy).then_inc(
                        sems[name + "_free"], 1)
                act.wait_ge(sems[name + "_free"], T.next(name + "_free", nk))

            def split(name, nk, dst, w=S):
                for k in range(nk):
                    act.wait_ge(sems[name + "_free"], T.next(name + "_free"))
                    act.activation(dst[:, k, :], F[:, k % 2, 0:w], ACT.Copy).then_inc(sems[name + "_hi"], 1)

            def squares(name, src, nt):
                for i in range(nt):
                    act.activation(flat(F[:]), src(i), ACT.Square, accum_out=SM[:, 0, i:i + 1]).then_inc(
                        sems[name + "_ss"], 1)
                    act.wait_ge(sems[name + "_ss"], T.next(name + "_ss"))


            def mod(i):
                hi()
                T.skip("gemm_done:out", 4)
                hi()
                out(3)
                if True:
                    act.activation(F[0:2, 0, :], BK[0][0:2, :], ACT.Copy).then_inc(sems["mod_row"], 1)
                T.skip("gemm_done:out", 4)
                T.skip("bank_free0")

            hi()
            act.wait_ge(sems["vec_cp"], T.next("vec_cp"))
            act.activation(CF[:, 0, :, :], CF[:, 1, :, :], ACT.Sigmoid).then_inc(sems["cs_sig"], 1)
            act.wait_ge(sems["cs_val"], T.next("cs_val"))
            act.activation(CSH[:], CF[:, 0, :, :], ACT.Copy).then_inc(sems["cs_hi"], 1)
            act.wait_ge(sems["wr_landed"], T.next("wr_landed", 16))
            act.activation(WRH[:], WR, ACT.Copy).then_inc(sems["wr_hi"], 1)
            act.wait_ge(sems["x_landed"], T.next("x_landed", 16 * (NT + NC)))
            squares("norm", lambda i: CTX[i], NC)
            act.wait_ge(sems["norm_rd"], T.next("norm_rd"))
            squares("norm", lambda i: X[:, i, :], NT)
            act.wait_ge(sems["norm_rd"], T.next("norm_rd"))
            T.loop(12, mod)
            act.wait_ge(sems["mod_row"], T.at("mod_row", 12))
            split("norm", NK, cH, C)
            split("norm", NK, hH[:])
            s = begin(STORES_1, "ctx_kv")
            blk(copies(lambda j: TM[:, j, 0:256], 256, 2, "ck_in"))
            s1 = begin(STORES_1, "ctx_nk")
            blk(copies(lambda j: ST[s1][:, j, 0:C], C, 4, "ctx_nk_out"))

            def kv_sink(nt, ready):
                vt = flat(ST[0][:, 2:4, :]).rearrange("p (t c) -> p t c", t=8)
                sink("sink", 1, lambda k: ST[0][:, 0, 0:nt * P], nt * P)
                act.activation(vt[:, 0:nt, :], TM[:, 0:nt, P:256], ACT.Copy).then_inc(sems["act_self"], 1)
                act.wait_ge(sems["act_self"], T.next("act_self"))
                act.sem_inc(sems[ready], 1)
            kv_sink(NC, "ctx_kv_out")
            s = begin(STORES_1, "ctx_nv")
            blk(copies(lambda j: ST[0][:, j, :], UN, 2, "ctx_nv_out"))
            blk(copies(lambda j: TM[:, j, :], UN, 4, "q_in"))
            s = begin(STORES_1, "q")
            sink("sink", 4, lambda k: ST[1][:, k, :])
            act.sem_inc(sems["q_out"], 1)
            blk(copies(lambda j: TM[:, j, 0:256], 256, 4, "k_in"))
            begin(STORES_1, "kv")
            nq = lambda: begin(STORES_1, "nq")
            nq()
            blk(copies(lambda j: ST[1][:, j, :], UN, 4, "nq_out"))
            kv_sink(NT, "kv_out")
            begin(STORES_1, "nk")
            blk(copies(lambda j: ST[0][:, j, :], UN, 4, "nk_out"))
            begin(STORES_1, "nv")
            blk(copies(lambda j: ST[1][:, j, :], UN, 4, "nv_out"))
            blk(copies(lambda j: TM[:, j, :], UN, 4, "fou_in"))
            begin(STORES_1, "fourier")
            for g in range(4):
                act.wait_ge(sems["fo_a"], T.next("fo_a"))
                act.activation(flat(F[:]), SC[:], ACT.Copy).then_inc(sems["fo_cp"], 1)
                act.wait_ge(sems["fo_b"], T.next("fo_b"))
                act.activation(ST[0][:, g, :], TP[:, 0:512], ACT.Copy).then_inc(sems["fo_o"], 1)
            act.wait_ge(sems["fo_o"], T.next("fo_o", 4))
            act.sem_inc(sems["fourier_out"], 1)

            def conv_gate():
                for j in range(4):
                    out(j)
                    act.activation(CT[:, j, :], BK[j], ACT.Sigmoid).then_inc(sems[BANKS[j]], 1)
            blk(conv_gate)
            blk(None, False)

            def attend(count, keys, biased, PTB):
                def rounded(s):
                    act.wait_ge(sems[f"qk_landed{s}"], T.next(f"qk_landed{s}", 64))
                    act.activation(QX[s], QS[s][:], ACT.Copy)
                    act.activation(KX[s][:, 0:keys(NT - 1)], KS[s][:, 0:keys(NT - 1)], ACT.Copy).then_inc(sems["head_hi"], 1)

                def exponential(n):
                    nk = keys(n % NT)
                    act.wait_ge(sems["head_nm"], T.next("head_nm"))
                    src = SB[n % 2] if biased else SCS[n % 2]
                    act.activation(PR[n % 2][:, 0:nk], src[:, 0:nk], ACT.Exp, bias=NM[:, n % 2:n % 2 + 1],
                                   scale=1.0 if biased else SCALE,
                                   accum_out=DEN[:, n % 2:n % 2 + 1]).then_inc(sems["head_exp"], 1)

                def body(last):
                    for n in range(2 * NT):
                        s, tt = n // NT, n % NT
                        if n + 1 < 2 * NT or not last:
                            exponential((n + 1) % (2 * NT))
                        if tt == 1 and not (last and s == 1):
                            rounded(1 - s)
                        if tt == 0:
                            act.wait_ge(sems["head_o"], T.next("head_o:free"))
                        for c, c0 in enumerate(range(0, keys(tt), 512)):
                            c1 = min(c0 + 512, keys(tt))
                            bank = (n if keys(tt) <= 512 else c) % 2 * 512
                            act.wait_ge(sems["head_pt"], T.next("head_pt"))
                            act.activation(PTB[s][c][:, 0:(c1 - c0) // P, tt * P:(tt + 1) * P],
                                           TP[:, bank:bank + c1 - c0].rearrange("p (k q) -> p k q", q=P),
                                           ACT.Copy).then_inc(sems["head_ptc"], 1)
                act.wait_ge(sems["head_go"], T.next("head_go"))
                act.sem_inc(sems["head_ptc"], 2)
                rounded(0)
                exponential(0)
                act.sem_inc(sems["act_paused"], 1)
                T.loop(count // 2 - 1, lambda i: body(False))
                body(True)
                T.skip("head_o:free", 2)

            attend(8, lambda tt: KEYS, False, PTB_1)
            attend(8, lambda tt: KEYS, True, PTB_1)
            begin(STORES_1, "gqa")
            begin(STORES_1, "na")
            act.wait_ge(sems["cv_n"], T.next("cv_n"))
            act.activation(CT, CU, ACT.Sigmoid).then_inc(sems["cv_sig"], 1)

            def gates(hb):
                def go():
                    for j in range(4):
                        out(j)
                        act.activation(G[:, hb * 4 + j, :], BK[j], ACT.Sigmoid).then_inc(sems[BANKS[j]], 1)
                return go

            def skip_banks():
                for b in BANKS:
                    T.skip(b)

            act.wait_ge(sems["g_free"], T.next("g_free"))
            hi()

            def branch(i):
                blk(gates(0))
                act.wait_ge(sems["yb_landed"], T.next("yb_landed", 16))
                act.activation(aH[:], ST[1][:], ACT.Copy).then_inc(sems["yb_hi"], 1)
                blk(gates(1))
                for _ in range(2):
                    unit()
                    skip_banks()
            T.loop(4, branch)

            def spread(name):
                act.wait_ge(sems[name + "_pe"], T.next(name + "_pe"))
                act.activation(GB, SC[:], ACT.Copy).then_inc(sems[name + "_gb"], 1)
            spread("g1")
            for k in range(NK):
                act.wait_ge(sems["m_go"], T.next("m_go")) if k == 0 else None
                act.activation(hH[:, k, :], BV[:, k, :], ACT.Copy).then_inc(sems["norm_hi"], 1)
            blk()
            blk()
            act.wait_ge(sems["x2"], T.next("x2"))
            squares("norm", lambda i: X[:, i, :], NT)
            act.wait_ge(sems["norm_rd"], T.next("norm_rd"))
            split("norm", NK, hH[:])
            act.wait_ge(sems["rt_pe"], T.next("rt_pe"))
            act.activation(RT(0), TP[:, 0:64].rearrange("p (t e) -> p t e", t=NT), ACT.Sigmoid).then_inc(sems["rt_sig"], 1)
            act.wait_ge(sems["rt_done"], T.next("rt_done"))

            def hid_hi(name):
                def go():
                    for j in range(4):
                        act.wait_ge(sems[BANKS[j]], T.at(BANKS[j]))
                        act.activation(aH[:, j, :], F[:, j % 2, :], ACT.Copy).then_inc(sems[name], 1)
                return go

            def expert(e, more=True):
                def sig():
                    for j in range(4):
                        out(j)
                        act.activation(G[:, j, :], BK[j], ACT.Sigmoid).then_inc(sems["e_sig"], 1)
                blk(sig)
                blk(hid_hi("hid_hi"))
                unit()
                skip_banks()
                unit(None, more)
                skip_banks()
            T.loop(NEXP - 1, expert)
            expert(NEXP - 1, False)
            spread("g2")
            act.wait_ge(sems["x3"], T.next("x3"))
            squares("norm", lambda i: X[:, i, :], NT)
            act.wait_ge(sems["norm_rd"], T.next("norm_rd"))

            def layer(l):
                hi()
                act.wait_ge(sems["x4"], T.next("x4"))
                squares("norm", lambda i: X[:, i, :], NT)
                act.wait_ge(sems["norm_rd"], T.next("norm_rd"))
                split("norm", NK, hH[:])
                blk(copies(lambda j: TM[:, j, :], UN, 4, "rqk_in"))
                begin2("rv")

                def ret_vg():
                    for j in range(4):
                        out(j)
                        act.activation(ST[1][:, j, 0:256], BK[j][:, 0:256], ACT.Copy)
                        act.activation(SG[:, j, :], BK[j][:, 256:512], ACT.Sigmoid).then_inc(sems["sg_sig"], 1)
                    act.wait_ge(sems["sg_sig"], T.next("sg_sig", 4))
                    act.sem_inc(sems["rv_out"], 1)
                blk(ret_vg)
                begin2("rqk")
                sink("sink", 4, lambda k: ST[0][:, k, :])
                act.sem_inc(sems["rqk_out"], 1)
                blk(copies(lambda j: TM[:, j, 0:384], 384, 4, "lat_in"))
                blk(copies(lambda j: QI[:, j, :]))
                begin2("sqk")
                sink("sink", 3, lambda k: ST[0][:, k, :] if k < 2 else CKT)

                def index_kw():
                    for j in range(4):
                        out(j)
                        act.activation(TM[:, j, 0:64], BK[j][:, 0:64], ACT.Copy)
                        act.activation(TM[:, j, 64:128], BK[j][:, 0:64], ACT.Copy)
                        act.activation(WIX[:, j, :], BK[j][:, 64:72], ACT.Copy,
                                       scale=8 ** -0.5 * 64 ** -0.5).then_inc(sems[BANKS[j]], 1)
                    act.wait_ge(sems[BANKS[3]], T.at(BANKS[3]))
                    act.sem_inc(sems["ki_out"], 1)
                blk(index_kw)
                begin2("sv")
                act.wait_ge(sems["uk_pe"], T.next("uk_pe"))
                act.activation(ST[0][:, 2:4, :], SC[:].rearrange("p (k s) -> p k s", k=2), ACT.Copy)
                act.activation(ST[1][:, :, 0:256], TP[:].rearrange("p (t c) -> p t c", t=NT), ACT.Copy).then_inc(
                    sems["uk_cp"], 1)
                act.wait_ge(sems["uk_cp"], T.next("uk_cp"))
                act.sem_inc(sems["sqk_out"], 1)
                act.sem_inc(sems["sv_out"], 1)
                sink("sink", 1, lambda k: KIT)
                begin2("dq")
                blk(copies(lambda j: ST[0][:, j, :], UN, 4, "dq_out"))
                begin2("dk")
                blk(copies(lambda j: ST[1][:, j, :], UN, 4, "dk_out"))
                begin2("dv")
                blk(copies(lambda j: ST[0][:, j, :], UN, 4, "dv_out"), False)
                n = 0
                for tt in range(1, NT):
                    nk = (tt + 1) * P
                    for ih in range(8):
                        act.wait_ge(sems["ix_pe"], T.next("ix_pe"))
                        if n >= 2:
                            act.wait_ge(sems["ix_dve"], T.next("ix_dve"))
                        act.activation(F[:, n % 2, 0:nk], SC[:, (n % 2) * 512:(n % 2) * 512 + nk], ACT.Relu).then_inc(
                            sems["ix_act"], 1)
                        n += 1
                act.wait_ge(sems["ix_dve"], T.next("ix_dve", 2))
                act.wait_ge(sems["sel_done"], T.next("sel_done"))
                attend(4, lambda tt: (tt + 1) * P, True, PTB_2)
                attend(8, lambda tt: (tt + 1) * P, True, PTB_2)
                act.wait_ge(sems["mix_ready"], T.next("mix_ready"))
                hi()
                split("norm", 2, hH[:])
                blk()
                blk()
                act.wait_ge(sems["x5"], T.next("x5"))
                squares("norm", lambda i: X[:, i, :], NT)
                act.wait_ge(sems["norm_rd"], T.next("norm_rd"))
                split("norm", NK, hH[:])

                def chunk(c, more=True):
                    def relu():
                        for j in range(4):
                            out(j)
                            if j >= 2:
                                act.wait_ge(sems["mlp_lo"], T.next("mlp_lo"))
                            act.activation(F[:, j % 2, :], BK[j], ACT.Relu).then_inc(sems[BANKS[j]], 1)
                            act.wait_ge(sems["mlp_sq"], T.next("mlp_sq"))
                            act.activation(aH[:, j, :], F[:, j % 2, :], ACT.Copy).then_inc(sems["mlp_hi"], 1)
                        act.wait_ge(sems["mlp_lo"], T.next("mlp_lo", 2))
                    blk(relu)
                    unit()
                    skip_banks()
                    unit(None, more)
                    skip_banks()
                act.sem_inc(sems["act_paused"], 1)
                T.loop(FF // UN - 1, chunk)
                chunk(FF // UN - 1, False)
            ring2 = {}

            def begin2(name):
                s = [b for n, b, _ in STORES_2 if n == name][0]
                act.wait_ge(sems[f"st_written{s}"], T.next(f"st_written{s}", held[s]))
                held[s] = 16 * [k for n, _, k in STORES_2 if n == name][0]
            if not only_first:
                for s in range(2):
                    act.wait_ge(sems[f"st_written{s}"], T.next(f"st_written{s}", held[s]))
                    T.skip(f"st_written{s}", -16 * [k for n, b, k in STORES_2 if b == s][-1])
                    held[s] = 16 * [k for n, b, k in STORES_2 if b == s][-1]
                T.loop(2, layer)
                act.wait_ge(sems["x4"], T.next("x4"))
                squares("norm", lambda i: X[:, i, :], NT)

        @block.vector
        def _(v):
            T = Tally(v, turns, "dve", {b: 1 for b in BANKS})
            T.n["w_lo"] = 2
            T.n["gemm_done:out"] = 8
            slot = [0]
            link_sem = "dve_self"

            def link(ins):
                ins.then_inc(sems[link_sem], 1)
                v.wait_ge(sems[link_sem], T.next(link_sem))

            def lo():
                s = slot[0]
                slot[0] ^= 1
                v.wait_ge(sems["w_hi"], T.next("w_hi"))
                v.tensor_tensor(WL[s][:], W[s][:], WH[s][:].bitcast(F32), ALU.subtract).then_inc(sems["w_lo"], 1)
                T.skip("w_lo")

            def unit(evac=None, more=True):
                if more:
                    lo()
                if evac is not None:
                    evac()
                T.skip("gemm_done:out", 4)

            def blk(evac=None, more=True):
                unit()
                unit(evac, more)
                skip_banks()

            def skip_banks():
                for b in BANKS:
                    T.skip(b)

            def out(j):
                v.wait_ge(sems["gemm_done"], T.at("gemm_done:out", j + 1))

            def rsqrt(y, m, work):
                link(v.tensor_scalar(y.bitcast(I32), m.bitcast(I32), -0.5, float(0x5F3759DF), ALU.mult, ALU.add))
                for _ in range(3):
                    link(v.scalar_tensor_tensor(work, m, -0.5, y, ALU.mult, ALU.mult))
                    link(v.tensor_tensor(work, work, y, ALU.mult))
                    link(v.scalar_tensor_tensor(y, work, 1.5, y, ALU.add, ALU.mult))

            def stats(src_n, name, nt, dim):
                v.wait_ge(sems[name + "_ss"], T.next(name + "_ss", nt))
                link(v.tensor_scalar(SM[:, 1, 0:nt], SM[:, 0, 0:nt], 1.0 / dim, EPS, ALU.mult, ALU.add))
                rsqrt(SM[:, 2, 0:nt], SM[:, 1, 0:nt], SM[:, 3, 0:nt])
                v.sem_inc(sems[name + "_rd"], 1)

            def normed(name, src, dst, nt):
                stats(src, name, nt, D)
                for i in range(nt):
                    v.tensor_scalar(dst[:, i, :], src(i), SM[:, 2, i:i + 1], None, ALU.mult).then_inc(sems[name + "_xn"], 1)
                v.wait_ge(sems[name + "_xn"], T.next(name + "_xn", nt))

            def split(name, nk, H, L, scale, bias=None, w=S):
                def rest(k):
                    v.wait_ge(sems[name + "_hi"], T.next(name + "_hi"))
                    v.tensor_tensor(L[:, k, :], F[:, k % 2, 0:w], H[:, k, :].bitcast(F32), ALU.subtract).then_inc(
                        sems[name + "_lo"], 1)
                for k in range(nk):
                    v.wait_ge(sems[name + "_tr"], T.next(name + "_tr"))
                    if k >= 2:
                        v.wait_ge(sems[name + "_lo"], T.next(name + "_lo"))
                    src = TP[:, (k % 2) * 512:(k % 2) * 512 + w]
                    if scale is None:
                        ins = v.tensor_copy(F[:, k % 2, 0:w], src)
                    elif bias is None:
                        ins = v.tensor_scalar(F[:, k % 2, 0:w], src, scale(k), None, ALU.mult)
                    else:
                        ins = v.tensor_scalar(F[:, k % 2, 0:w], src, scale(k), bias(k), ALU.mult, ALU.add)
                    ins.then_inc(sems[name + "_free"], 1)
                    if k:
                        rest(k - 1)
                rest(nk - 1)
                v.wait_ge(sems[name + "_lo"], T.next(name + "_lo", 2))

            def rms(x4, nt, nh, gain, hd=HD):
                n = nt * nh
                sq = flat(T1)[:, 0:n * hd].rearrange("p (t h d) -> p t h d", t=nt, h=nh)
                ss = lambda r: SM[:, r, 0:n].rearrange("p (t h) -> p t h", t=nt)
                link(v.tensor_tensor(sq, x4, x4, ALU.mult))
                link(v.tensor_reduce(ss(0), sq, AX.X, ALU.add))
                link(v.tensor_scalar(SM[:, 1, 0:n], SM[:, 0, 0:n], 1.0 / hd, EPS, ALU.mult, ALU.add))
                rsqrt(SM[:, 2, 0:n], SM[:, 1, 0:n], SM[:, 3, 0:n])
                link(v.tensor_tensor(x4, x4, ss(2).unsqueeze(3).to_broadcast([P, nt, nh, hd]), ALU.mult))
                link(v.tensor_tensor(x4, x4, gain.unsqueeze(1).unsqueeze(1).to_broadcast([P, nt, nh, hd]), ALU.mult))

            def rope(x4, nt, nh):
                shp = [P, nt, nh, HD // 2]
                a = flat(T1)[:, 0:nt * nh * HD].rearrange("p (t h d) -> p t h d", t=nt, h=nh)
                b = flat(T2)[:, 0:nt * nh * HD].rearrange("p (t h d) -> p t h d", t=nt, h=nh)
                v.tensor_tensor(a, x4, RC.unsqueeze(2).to_broadcast([P, nt, nh, HD]), ALU.mult)
                v.tensor_tensor(b[:, :, :, 0:HD:2], x4[:, :, :, 1:HD:2], RS[:, :, 0:HD:2].unsqueeze(2).to_broadcast(shp), ALU.mult)
                link(v.tensor_tensor(b[:, :, :, 1:HD:2], x4[:, :, :, 0:HD:2], RS[:, :, 1:HD:2].unsqueeze(2).to_broadcast(shp), ALU.mult))
                link(v.tensor_tensor(x4, a, b, ALU.add))

            heads4 = lambda ap: ap.rearrange("p t (h d) -> p t h d", d=HD)

            v.sem_inc(sems["w_lo"], 2)
            v.sem_inc(sems["gemm_done"], 8)
            for b in BANKS:
                v.sem_inc(sems[b], 1)
            v.sem_inc(sems["yb_used"], 1)
            T.n["yb_used"] = 1
            v.wait_ge(sems["vec_tr"], T.next("vec_tr"))
            v.tensor_copy(VT[:], TP[:, 0:V_ALL])
            v.tensor_copy(CW[:, :, 0:NTAP], TP[:, 128:256].rearrange("p (j k) -> p j k", j=4)[:, :, 0:NTAP])
            for m in range(2):
                ins = v.tensor_copy(CF[:, 1, :, m], TP[:, V_C + 8 * m:V_C + 8 * m + 8])
            link(ins)
            v.sem_inc(sems["vec_cp"], 1)
            v.wait_ge(sems["cs_sig"], T.next("cs_sig"))
            link(v.tensor_tensor(CF[:, 0, :, :], CF[:, 0, :, :], CF[:, 1, :, :], ALU.mult))
            v.sem_inc(sems["cs_val"], 1)
            v.wait_ge(sems["cs_hi"], T.next("cs_hi"))
            v.tensor_tensor(CSL[:], CF[:, 0, :, :], CSH[:].bitcast(F32), ALU.subtract).then_inc(sems["cs_lo"], 1)
            v.wait_ge(sems["wr_hi"], T.next("wr_hi"))
            v.tensor_tensor(WRL[:], WR, WRH[:].bitcast(F32), ALU.subtract).then_inc(sems["wr_lo"], 1)
            lo()

            normed("norm", lambda i: CTX[i], CTN, NC)
            normed("norm", lambda i: X[:, i, :], XN, NT)
            v.sem_inc(sems["mod_out"], 1)

            def mod(i):
                for _ in range(2):
                    lo()
                    T.skip("gemm_done:out", 4)
                v.wait_ge(sems["mod_col"], T.next("mod_col"))
                v.tensor_copy(MOD[:, bass.ds(i * 4, 4), :].rearrange("p a b -> p (a b)"), TP[:, 0:8]).then_inc(
                    sems["mod_out"], 1)
                v.sem_inc(sems["bank_free0"], 1)
                T.skip("bank_free0")
            T.loop(12, mod)
            v.wait_ge(sems["mod_out"], T.next("mod_out", 13))
            link(v.tensor_tensor(MOD[:], MOD[:], VT[:, V_BMOD:V_N1].unsqueeze(2).to_broadcast([P, 48, 2]), ALU.add))
            for r, c0, m, g in ((0, 8, 0, V_N1), (1, 8, 1, V_N1), (2, 32, 0, V_N2)):
                ins = v.scalar_tensor_tensor(AF[:, r, :], MOD[:, c0:c0 + 8, m], 1.0, VT[:, g:g + 8], ALU.add, ALU.mult)
            link(ins)
            split("norm", NK, cH, cL, lambda k: AF[:, 1, k:k + 1], lambda k: MOD[:, k, 1:2], C)
            split("norm", NK, hH[:], hL[:], lambda k: AF[:, 0, k:k + 1], lambda k: MOD[:, k, 0:1])
            v.wait_ge(sems["tab_landed"], T.next("tab_landed", 16 * 7))
            blk()
            v.wait_ge(sems["ck_in"], T.next("ck_in"))
            rms(heads4(TM[:, 0:NC, 0:P]), NC, 2, GK)
            v.sem_inc(sems["ck_rms"], 1)
            blk()
            blk()
            blk()
            v.wait_ge(sems["q_in"], T.next("q_in"))
            rms(heads4(TM), NT, 8, GQ)
            rope(heads4(TM), NT, 8)
            v.sem_inc(sems["q_rope"], 1)
            blk()
            v.wait_ge(sems["k_in"], T.next("k_in"))
            rms(heads4(TM[:, :, 0:P]), NT, 2, GK)
            rope(heads4(TM[:, :, 0:P]), NT, 2)
            v.sem_inc(sems["k_rope"], 1)
            for _ in range(5):
                blk()

            def conv_in():
                for j in range(4):
                    out(j)
                    v.tensor_tensor(Z[:, j, PADT:PADT + S], BK[j], CT[:, j, :], ALU.mult).then_inc(sems[BANKS[j]], 1)
                v.wait_ge(sems[BANKS[3]], T.at(BANKS[3]))
                v.sem_inc(sems["z_ready"], 1)
            v.wait_ge(sems["rpb_stored"], T.at("rpb_stored", 16 * 8))
            link(v.memset(Z[:], 0.0))
            blk(conv_in, False)

            def attend(count, keys, bias, put_out, load_incs):
                def remainders(s):
                    nk = keys(NT - 1)
                    v.wait_ge(sems["head_hi"], T.next("head_hi"))
                    v.tensor_tensor(QX[s][HD:P, :], QS[s][HD:P, :], QX[s][HD:P, :].bitcast(F32), ALU.subtract)
                    v.tensor_tensor(KL[s][:, 0:nk], KS[s][0:HD, 0:nk], KX[s][0:HD, 0:nk].bitcast(F32),
                                    ALU.subtract).then_inc(sems["head_lo"], 1)

                def top(n):
                    nk = keys(n % NT)
                    if n % NT == 0 and load_incs:
                        v.wait_ge(sems[f"head_landed{n // NT}"], T.next(f"head_landed{n // NT}", load_incs))
                    v.wait_ge(sems["head_s"], T.next("head_s"))
                    src = SCS[n % 2][:, 0:nk]
                    if bias is not None:
                        bias(n // NT, n % NT, SCS[n % 2], SB[n % 2])
                        src = SB[n % 2][:, 0:nk]
                    c = n % 2
                    link(v.tensor_reduce(MX[:, c:c + 1], src, AX.X, ALU.max))
                    v.tensor_scalar(NM[:, c:c + 1], MX[:, c:c + 1], -1.0 if bias is not None else -SCALE, None,
                                    ALU.mult).then_inc(sems["head_nm"], 1)

                def normalise(n):
                    c, nk = n % 2, keys(n % NT)
                    v.wait_ge(sems["head_exp"], T.next("head_exp"))
                    link(v.reciprocal(RD[:, c:c + 1], DEN[:, c:c + 1]))
                    v.tensor_scalar(PR[c][:, 0:nk], PR[c][:, 0:nk], RD[:, c:c + 1], None, ALU.mult).then_inc(
                        sems["head_pn"], 1)

                def put(i, s):
                    v.wait_ge(sems["head_o"], T.next("head_o"))
                    put_out(i, s)

                def body(i, first, last):
                    for n in range(2 * NT):
                        s, tt = n // NT, n % NT
                        if n + 1 < 2 * NT or not last:
                            top((n + 1) % (2 * NT))
                        normalise(n)
                        if tt == 1:
                            if not (last and s == 1):
                                remainders(1 - s)
                            if s == 1:
                                put(i, 0)
                            elif not first:
                                put(i - 1, 1)
                v.wait_ge(sems["w_lo"], T.at("w_lo", 0))
                v.sem_inc(sems["head_go"], 1)
                v.sem_inc(sems["head_oe"], 2)
                T.skip("head_o", 2)
                remainders(0)
                top(0)
                body(0, True, False)
                v.sem_inc(sems["v_paused"], 1)
                if count > 4:
                    T.loop(count // 2 - 2, lambda i: body(i + 1, False, False))
                body(count // 2 - 1, False, True)
                put(count // 2 - 1, 1)
                T.skip("head_oe", count + 2)
                v.wait_ge(sems["head_oe"], T.at("head_oe", 0))

            def settle(name):
                v.wait_ge(sems[name], T.next(name))

            def to_stage(b):
                def go(i, s):
                    v.tensor_copy(ST[b][s * HD:(s + 1) * HD, bass.ds(i, 1), :].rearrange("p a q -> p (a q)"),
                                  OT[s]).then_inc(sems["head_oe"], 1)
                return go

            v.wait_ge(sems["fo_b"], T.next("fo_b", 4))
            v.wait_ge(sems["st_written1"], T.at("st_written1", stored(STORES_1, 1, "nv")))
            attend(8, lambda tt: KEYS, None, to_stage(1), 0)
            v.sem_inc(sems["gqa_out"], 1)
            T.skip("head_landed0", 16 * 4)
            T.skip("head_landed1", 16 * 4)

            def na_bias(s, tt, sc, sb):
                if tt == 0:
                    link(v.tensor_tensor(ES[s][:], ES[s][:], MSK[:].unsqueeze(1).to_broadcast([P, 14, 64]), ALU.add))
                j0 = 2 * (NT - 1 - tt)
                v.scalar_tensor_tensor(sb[:, 0:S], sc[:, 0:S], SCALE, flat(ES[s][:, j0:j0 + 8, :]), ALU.mult, ALU.add)
                link(v.tensor_scalar(sb[:, S:KEYS], sc[:, S:KEYS], SCALE, None, ALU.mult))
            v.wait_ge(sems["st_written0"], T.at("st_written0", stored(STORES_1, 0, "fourier")))
            attend(8, lambda tt: KEYS, na_bias, to_stage(0), 16 * 3)
            v.sem_inc(sems["na_out"], 1)
            v.memset(BIG[:], 0.0)
            v.memset(ONE, 1.0)
            v.wait_ge(sems["conv_done"], T.next("conv_done"))
            for j in range(4):
                ins = v.tensor_scalar(CU[:, j, :], CU[:, j, :], VT[:, V_CB + j:V_CB + j + 1], None, ALU.add)
            link(ins)
            v.tensor_tensor(CT, CU, CU, ALU.mult).then_inc(sems["cv_sq"], 1)
            v.wait_ge(sems["cv_pe"], T.next("cv_pe"))
            link(v.tensor_scalar(F[:, 0, :], SC[:, 0:512], 1.0 / 512, EPS, ALU.mult, ALU.add))
            v.sem_inc(sems["cv_r"], 1)
            rsqrt(F[:, 1, :], F[:, 0, :], AT[:, 0:512])
            for j in range(4):
                ins = v.scalar_tensor_tensor(CU[:, j, :], CU[:, j, :], VT[:, V_CG + j:V_CG + j + 1], F[:, 1, :],
                                             ALU.mult, ALU.mult)
            link(ins)
            v.sem_inc(sems["cv_n"], 1)
            v.wait_ge(sems["cv_sig"], T.next("cv_sig"))
            link(v.tensor_tensor(CU, CU, CT, ALU.mult))
            v.sem_inc(sems["cv_out"], 1)
            v.wait_ge(sems["cv_written"], T.next("cv_written", 16))
            v.sem_inc(sems["g_free"], 1)
            lo()

            def branch(i):
                blk()
                v.wait_ge(sems["yb_hi"], T.next("yb_hi"))
                v.tensor_tensor(aL[:], ST[1][:], aH[:].bitcast(F32), ALU.subtract).then_inc(sems["yb_used"], 1)
                blk()
                for hb in range(2):
                    def go():
                        for j in range(4):
                            out(j)
                            v.tensor_tensor(F[:, j % 2, :], BK[j], G[:, hb * 4 + j, :], ALU.mult).then_inc(
                                sems[BANKS[j]], 1)
                            v.wait_ge(sems[BANKS[j]], T.at(BANKS[j]))
                            link(v.tensor_tensor(BV[:, hb * 4 + j, :], BV[:, hb * 4 + j, :], F[:, j % 2, :], ALU.add))
                    unit(go)
                    skip_banks()
            T.loop(4, branch)
            v.sem_inc(sems["m_go"], 1)

            def spread(name, c0):
                link(v.tensor_copy(flat(ST[0][:])[:, 0:D].rearrange("p (k c) -> p k c", k=NK),
                                   MOD[:, c0:c0 + NK, 0].unsqueeze(2).to_broadcast([P, NK, P])))
                v.sem_inc(sems[name + "_in"], 1)
            spread("g1", 16)
            for k in range(NK):
                v.wait_ge(sems["norm_hi"], T.next("norm_hi"))
                v.tensor_tensor(hL[:, k, :], BV[:, k, :], hH[:, k, :].bitcast(F32), ALU.subtract).then_inc(sems["norm_lo"], 1)
            v.wait_ge(sems["g1_gb"], T.next("g1_gb"))

            def add_x(hb, gain):
                def go():
                    for j in range(4):
                        xs = X[:, j, hb * UN:(hb + 1) * UN]
                        out(j)
                        if gain:
                            v.tensor_tensor(F[:, j % 2, :], BK[j], GB[:, hb * UN:(hb + 1) * UN], ALU.mult).then_inc(
                                sems[BANKS[j]], 1)
                            v.wait_ge(sems[BANKS[j]], T.at(BANKS[j]))
                            link(v.tensor_tensor(xs, xs, F[:, j % 2, :], ALU.add))
                        else:
                            v.tensor_tensor(xs, xs, BK[j], ALU.add).then_inc(sems[BANKS[j]], 1)
                return go
            blk(add_x(0, True))
            blk(add_x(1, True))
            v.sem_inc(sems["x2"], 1)
            v.wait_ge(sems["norm_lo"], T.next("norm_lo", NK))
            normed("norm", lambda i: X[:, i, :], XN, NT)
            split("norm", NK, hH[:], hL[:], lambda k: AF[:, 2, k:k + 1], lambda k: MOD[:, 24 + k, 0:1])
            v.memset(BIG[:], 0.0)

            v.wait_ge(sems["rt_sig"], T.next("rt_sig"))
            s_, sel, tmp, eq, onehot, ing = RT(0), RT(1), RT(2), RT(3), RT(4), RT(5)
            link(v.tensor_tensor(sel, s_, RB[:].unsqueeze(1).to_broadcast([P, NT, NEXP]), ALU.add))
            g5 = sel.rearrange("p t (g x y) -> p (t g) x y", g=4, x=2)
            mx2, mn2 = RT2(0, 8).rearrange("p t (g x) -> p (t g) x", x=2), RT2(1, 8).rearrange("p t (g x) -> p (t g) x", x=2)
            v.tensor_tensor(mx2, g5[:, :, :, 0], g5[:, :, :, 1], ALU.max)
            link(v.tensor_tensor(mn2, g5[:, :, :, 0], g5[:, :, :, 1], ALU.min))
            ga, gb2, gs = (RT2(n, 4).rearrange("p t g -> p (t g)") for n in (2, 3, 4))
            v.tensor_tensor(ga, mx2[:, :, 0], mx2[:, :, 1], ALU.max)
            link(v.tensor_tensor(gb2, mx2[:, :, 0], mx2[:, :, 1], ALU.min))
            link(v.tensor_tensor(gs, mn2[:, :, 0], mn2[:, :, 1], ALU.max))
            link(v.tensor_tensor(gb2, gb2, gs, ALU.max))
            link(v.tensor_tensor(ga, ga, gb2, ALU.add))

            def first_max(vals, n, hot, work, mxt):
                bc = mxt.unsqueeze(2).to_broadcast([P, NT, n])
                link(v.tensor_reduce(mxt, vals, AX.X, ALU.max))
                link(v.tensor_tensor(work, vals, bc, ALU.is_ge))
                link(v.tensor_tensor(work, work, DESC[:, 0:n].unsqueeze(1).to_broadcast([P, NT, n]), ALU.mult))
                link(v.tensor_reduce(mxt, work, AX.X, ALU.max))
                link(v.tensor_tensor(hot, work, bc, ALU.is_ge))
            DESC = SM[:, 3, 0:NEXP]
            for e in range(NEXP):
                ins = v.memset(SM[:, 3, e:e + 1], float(NEXP - e))
            link(ins)
            mxt = SM[:, 3, NEXP:NEXP + NT]
            gv = RT2(2, 4)
            first_max(gv, 4, RT2(4, 4), RT2(3, 4), mxt)
            link(v.tensor_copy(ing.rearrange("p t (g x) -> p (t g) x", x=4),
                               RT2(4, 4).rearrange("p t g -> p (t g)").unsqueeze(2).to_broadcast([P, 16, 4])))
            link(v.tensor_tensor(sel, sel, ing, ALU.mult))
            link(v.tensor_scalar(ing, ing, -1.0, BIG_E, ALU.add, ALU.mult))
            link(v.tensor_tensor(sel, sel, ing, ALU.add))
            first_max(sel, NEXP, onehot, tmp, mxt)
            link(v.scalar_tensor_tensor(sel, onehot, -3.0e30, sel, ALU.mult, ALU.add))
            first_max(sel, NEXP, eq, tmp, mxt)
            link(v.tensor_tensor(onehot, onehot, eq, ALU.add))
            link(v.tensor_tensor(s_, s_, onehot, ALU.mult))
            link(v.tensor_reduce(mxt, s_, AX.X, ALU.add))
            link(v.reciprocal(SM[:, 3, 20:24], mxt))
            link(v.tensor_tensor(GATE[:], s_, SM[:, 3, 20:24].unsqueeze(2).to_broadcast([P, NT, NEXP]), ALU.mult))
            v.sem_inc(sems["rt_done"], 1)

            def expert(e, more=True):
                def gate_half():
                    for j in range(4):
                        v.wait_ge(sems["e_sig"], T.next("e_sig"))
                        v.tensor_tensor(G[:, 4 + j, :], BK[j], G[:, j, :], ALU.mult).then_inc(sems[BANKS[j]], 1)
                blk(gate_half)

                def hidden():
                    def rest(j):
                        v.wait_ge(sems["hid_hi"], T.next("hid_hi"))
                        v.tensor_tensor(aL[:, j, :], F[:, j % 2, :], aH[:, j, :].bitcast(F32), ALU.subtract).then_inc(
                            sems["hid_lo"], 1)
                    for j in range(4):
                        out(j)
                        if j >= 2:
                            v.wait_ge(sems["hid_lo"], T.next("hid_lo"))
                        v.tensor_tensor(F[:, j % 2, :], BK[j], G[:, 4 + j, :], ALU.mult).then_inc(sems[BANKS[j]], 1)
                        if j:
                            rest(j - 1)
                    rest(3)
                    v.wait_ge(sems["hid_lo"], T.next("hid_lo", 2))
                blk(hidden)
                for hf in range(2):
                    def down():
                        for j in range(4):
                            out(j)
                            acc = XN[:, j, hf * UN:(hf + 1) * UN]
                            v.scalar_tensor_tensor(acc, BK[j], GATE[:, j, bass.ds(e, 1)], acc, ALU.mult,
                                                   ALU.add).then_inc(sems[BANKS[j]], 1)
                    unit(down, more or hf == 0)
                    skip_banks()
            T.loop(NEXP - 1, expert)
            expert(NEXP - 1, False)
            for b in BANKS:
                v.wait_ge(sems[b], T.at(b, 0))
            v.sem_inc(sems["moe_done"], 1)
            spread("g2", 40)
            v.wait_ge(sems["g2_gb"], T.next("g2_gb"))
            for i in range(NT):
                link(v.tensor_tensor(XN[:, i, :], XN[:, i, :], GB, ALU.mult))
                link(v.tensor_tensor(X[:, i, :], X[:, i, :], XN[:, i, :], ALU.add))
            v.sem_inc(sems["x3"], 1)

            def final(name, dst):
                stats(None, name, NT, D)
                v.wait_ge(sems["gf_landed"], T.next("gf_landed", 16))
                for i in range(NT):
                    ins = v.scalar_tensor_tensor(dst(i), X[:, i, :], SM[:, 2, i:i + 1], flat(G[:])[:, 0:D], ALU.mult,
                                                 ALU.mult)
                    link(ins)

            final("norm", (lambda i: XN[:, i, :]) if only_first else (lambda i: X[:, i, :]))
            if only_first:
                v.sem_inc(sems["out_ready"], NT)
                return
            v.sem_inc(sems["x4"], 1)
            v.sem_inc(sems["es_free"], 1)

            def layer(l):
                lo()
                link(v.tensor_copy(AF[:, 3, :], VT[:, bass.ds(l * 8 + V_ATT, 8)]))
                normed("norm", lambda i: X[:, i, :], XN, NT)
                split("norm", NK, hH[:], hL[:], lambda k: AF[:, 3, k:k + 1])
                v.wait_ge(sems["lay_landed"], T.next("lay_landed", 16 * 6))
                blk()
                v.wait_ge(sems["rqk_in"], T.next("rqk_in"))
                x16 = TM.rearrange("p t (h d) -> p t h d", d=32)
                a16 = T1.rearrange("p t (h d) -> p t h d", d=32)
                x4, a4, b4 = (q.rearrange("p t (h x d) -> p t h x d", x=2, d=32) for q in (TM, T1, T2))
                shp = [P, NT, 8, 32]
                ts = TS.unsqueeze(2).to_broadcast(shp)
                v.tensor_tensor(a16, x16, TC.unsqueeze(2).to_broadcast([P, NT, 16, 32]), ALU.mult)
                v.tensor_tensor(b4[:, :, :, 0, :], x4[:, :, :, 1, :], ts, ALU.mult)
                link(v.tensor_tensor(b4[:, :, :, 1, :], x4[:, :, :, 0, :], ts, ALU.mult))
                v.tensor_tensor(x4[:, :, :, 0, :], a4[:, :, :, 0, :], b4[:, :, :, 0, :], ALU.subtract)
                link(v.tensor_tensor(x4[:, :, :, 1, :], a4[:, :, :, 1, :], b4[:, :, :, 1, :], ALU.add))
                v.sem_inc(sems["rqk_rope"], 1)

                def ret_gate():
                    for j in range(4):
                        v.wait_ge(sems["sg_sig"], T.next("sg_sig"))
                        v.tensor_tensor(SG[:, j, :], BK[j][:, 256:512], SG[:, j, :], ALU.mult).then_inc(sems[BANKS[j]], 1)
                blk(ret_gate)
                blk()
                v.wait_ge(sems["lat_in"], T.next("lat_in"))
                rms(TM[:, :, 256:384].unsqueeze(2), NT, 1, KNW, P)
                v.sem_inc(sems["lat_rms"], 1)
                for n in range(5):
                    blk(None, n < 4)
                n = 0
                for tt in range(NT):
                    nk = (tt + 1) * P
                    if tt == 0:
                        v.tensor_copy(SEL[:, 0, 0:P], CM[:])
                        continue
                    for ih in range(8):
                        v.wait_ge(sems["ix_act"], T.next("ix_act"))
                        w = WIX[:, tt, ih:ih + 1]
                        if ih == 0:
                            ins = v.tensor_scalar(IXA[:, 0:nk], F[:, n % 2, 0:nk], w, None, ALU.mult)
                        else:
                            ins = v.scalar_tensor_tensor(IXA[:, 0:nk], F[:, n % 2, 0:nk], w, IXA[:, 0:nk], ALU.mult, ALU.add)
                        ins.then_inc(sems["ix_dve"], 1)
                        v.wait_ge(sems["ix_dve"], T.next("ix_dve"))
                        n += 1
                    link(v.tensor_tensor(IXA[:, nk - P:nk], IXA[:, nk - P:nk], CM[:], ALU.add))
                    for r in range(NSEL // 8):
                        src = IXA if r == 0 else IXW
                        v.sem_inc(sems["v_paused"], 1)
                        link(v.max(TOP[:], src[:, 0:nk]))
                        v.sem_inc(sems["v_paused"], 1)
                        link(v.match_replace(IXW[:, 0:nk], TOP[:], src[:, 0:nk], TAKEN))
                    link(v.tensor_scalar(SEL[:, tt, 0:nk], IXW[:, 0:nk], 0.5 * TAKEN, NEG, ALU.is_gt, ALU.mult))
                v.sem_inc(sems["sel_done"], 1)

                def ret(i):
                    for s in range(2):
                        for kt in range(NT):
                            n = S - kt * P
                            v.wait_ge(sems["ret_s"], T.next("ret_s"))
                            bank = SC if kt % 2 == 0 else TP
                            v.tensor_tensor(RP[:, kt, 0:n], bank[:, 0:n], flat(ES[s][:])[:, 0:n], ALU.mult).then_inc(
                                sems["ret_d"], 1)
                        for tt in range(NT):
                            v.wait_ge(sems["ret_o"], T.next("ret_o"))
                            v.tensor_copy(XN[:, tt, bass.ds(i * (2 * HD) + s * HD, HD)], OB[tt % 2]).then_inc(
                                sems["ret_oe"], 1)
                v.sem_inc(sems["v_paused"], 1)
                T.loop(2, ret)
                T.skip("ret_oe", 4 * NT)
                v.wait_ge(sems["ret_oe"], T.at("ret_oe", 0))
                o4 = XN[:, :, 0:256].rearrange("p t (h d) -> p t h d", h=4)
                sq = flat(T2)[:, 0:NT * 256].rearrange("p (t h d) -> p t h d", t=NT, h=4)
                st = lambda r: SM[:, r, 0:16].rearrange("p (t h) -> p t h", t=NT)
                bc = lambda r: st(r).unsqueeze(3).to_broadcast([P, NT, 4, HD])
                link(v.tensor_reduce(st(0), o4, AX.X, ALU.add))
                link(v.tensor_scalar(SM[:, 1, 0:16], SM[:, 0, 0:16], 1.0 / HD, None, ALU.mult))
                link(v.tensor_tensor(o4, o4, bc(1), ALU.subtract))
                link(v.tensor_tensor(sq, o4, o4, ALU.mult))
                link(v.tensor_reduce(st(0), sq, AX.X, ALU.add))
                link(v.tensor_scalar(SM[:, 1, 0:16], SM[:, 0, 0:16], 1.0 / HD, EPS, ALU.mult, ALU.add))
                rsqrt(SM[:, 2, 0:16], SM[:, 1, 0:16], SM[:, 3, 0:16])
                link(v.tensor_tensor(o4, o4, bc(2), ALU.mult))
                link(v.tensor_tensor(XN[:, :, 0:256], XN[:, :, 0:256], RNW[:].unsqueeze(1).to_broadcast([P, NT, 256]), ALU.mult))
                link(v.tensor_tensor(XN[:, :, 0:256], XN[:, :, 0:256], SG, ALU.mult))

                def biased(src):
                    def go(s, tt, sc, sb):
                        nk = (tt + 1) * P
                        link(v.scalar_tensor_tensor(sb[:, 0:nk], sc[:, 0:nk], SCALE, src(tt, nk), ALU.mult, ALU.add))
                    return go

                def to_split(k0):
                    def go(i, s):
                        part = lambda ap: ap[s * HD:(s + 1) * HD, bass.ds(i + k0, 1), :].rearrange("p a q -> p (a q)")
                        link(v.tensor_copy(part(hH), OT[s]))
                        v.tensor_tensor(part(hL), OT[s], part(hH).bitcast(F32), ALU.subtract).then_inc(sems["head_oe"], 1)
                    return go
                attend(4, lambda tt: (tt + 1) * P, biased(lambda tt, nk: SEL[:, tt, 0:nk]), to_split(2), 0)
                v.wait_ge(sems["xb_landed"], T.next("xb_landed", 16))
                attend(8, lambda tt: (tt + 1) * P, biased(lambda tt, nk: XB[:, S - nk:S]), to_split(4), 0)
                v.sem_inc(sems["mix_ready"], 1)
                lo()
                v.sem_inc(sems["es_free"], 1)
                split("norm", 2, hH[:], hL[:], None)
                blk(add_x(0, False))
                blk(add_x(1, False))
                v.wait_ge(sems[BANKS[3]], T.at(BANKS[3], 0))
                v.sem_inc(sems["x5"], 1)
                link(v.tensor_copy(AF[:, 3, :], VT[:, bass.ds(l * 8 + V_MLP, 8)]))
                normed("norm", lambda i: X[:, i, :], XN, NT)
                split("norm", NK, hH[:], hL[:], lambda k: AF[:, 3, k:k + 1])

                def chunk(c, more=True):
                    def square():
                        for j in range(4):
                            v.wait_ge(sems[BANKS[j]], T.at(BANKS[j]))
                            v.tensor_tensor(F[:, j % 2, :], F[:, j % 2, :], F[:, j % 2, :], ALU.mult).then_inc(sems["mlp_sq"], 1)
                            v.wait_ge(sems["mlp_hi"], T.next("mlp_hi"))
                            v.tensor_tensor(aL[:, j, :], F[:, j % 2, :], aH[:, j, :].bitcast(F32), ALU.subtract).then_inc(
                                sems["mlp_lo"], 1)
                    blk(square)
                    for hf in range(2):
                        unit(add_x(hf, False), more or hf == 0)
                        skip_banks()
                v.sem_inc(sems["v_paused"], 1)
                T.loop(FF // UN - 1, chunk)
                chunk(FF // UN - 1, False)
                v.wait_ge(sems[BANKS[3]], T.at(BANKS[3], 0))
                v.sem_inc(sems["x4"], 1)
                v.sem_inc(sems["mlp_done"], 1)
            T.loop(2, layer)
            final("norm", lambda i: XN[:, i, :])
            v.sem_inc(sems["out_ready"], NT)


def tables():
    f = np.float32
    tok = np.arange(S)
    inv = 10000.0 ** (-np.arange(16) / 16.0)
    ang = np.concatenate([(tok // 64)[:, None] * inv, (tok % 64)[:, None] * inv], -1)
    tiles = lambda a: np.ascontiguousarray(a.reshape(NT, P, -1).transpose(1, 0, 2).astype(f))
    sign = np.where(np.arange(HD) % 2 == 0, -1.0, 1.0)
    inv2 = 10000.0 ** (-np.arange(32) / 32.0)
    ang2 = tok[:, None] * inv2
    col = np.arange(64)
    start = np.clip(col - 8, 0, 48)
    ok = (col[None, :] >= start[:, None]) & (col[None, :] < start[:, None] + 16)
    mask = np.where(ok, 0.0, NEG)
    diff = np.arange(P)[:, None] - np.arange(S)[None, :] + (S - P)
    count = ((diff >= 0) & (diff <= 128)).astype(int) + ((diff >= 0) & (diff % 4 == 0)) + ((diff >= 0) & (diff % 16 == 0))
    dil = np.where(count > 0, np.log(np.maximum(count, 1)), NEG)
    m = np.arange(S)[None, :] - np.arange(P)[:, None]
    lg = np.log(1.0 - 2.0 ** (-5.0 - np.arange(4)))
    decay = np.exp(np.maximum(m, 0)[None] * lg[:, None, None]) * (m >= 0)[None] * SCALE
    al = 2 * np.pi * ((tok[:, None] * tok[None, :]) % S) / S
    g = np.arange(P)
    ag = 2 * np.pi * ((g[:, None] * g[None, :]) % P) / P
    return {
        "k_ident": np.eye(P, dtype=f),
        "k_ropec": tiles(np.repeat(np.cos(ang), 2, -1)),
        "k_ropes": tiles(np.repeat(np.sin(ang), 2, -1) * sign),
        "k_colmask": np.concatenate([mask, mask], 0).astype(f),
        "k_causal": np.where(g[None, :] <= g[:, None], 0.0, NEG).astype(f),
        "k_dilbias": dil.astype(f),
        "k_decay": decay.astype(f),
        "k_retc": tiles(np.cos(ang2)),
        "k_rets": tiles(np.sin(ang2)),
        "k_dftc": (np.cos(al) / np.sqrt(S)).astype(f),
        "k_dfts": (np.sin(al) / np.sqrt(S)).astype(f),
        "k_dftg": (np.concatenate([np.cos(ag), -np.sin(ag)], 1) / np.sqrt(P)).astype(f),
    }


_INS = ["x", "c", "ctx", "c_ctx", "w_mod", "b_mod", "norm1_g", "norm2_g", "w_in", "q_norm_g", "k_norm_g", "na_rpb",
        "conv_w", "conv_b", "conv_norm_g", "w_branch", "w_out", "w_router", "router_bias", "w_expert_gu",
        "w_expert_down", "final_norm_g", "attn_norm_w_2", "w_in_2", "ret_norm_w_2", "dsa_kv_norm_w_2", "dsa_w_uk_2",
        "dsa_w_uv_2", "w_out_2", "mlp_norm_w_2", "w_up_2", "w_down_2", "final_norm_w_2"]
ONLY_FIRST = False


def kernel(**inputs):
    import numpy as _np
    import concourse.bacc as _bacc
    from concourse import mybir as _mybir
    from concourse.bass_utils import run_bass_kernel_spmd as _run

    arrays = {f"in_{n}_dram": _np.ascontiguousarray(inputs[n]) for n in _INS}
    arrays.update({f"in_{n}_dram": a for n, a in tables().items()})
    turns = {}
    for _ in range(2):
        nc = _bacc.Bacc("TRN2", target_bir_lowering=False, num_devices=1)
        t = {n[3:-5]: nc.dram_tensor(n, a.shape, _mybir.dt.from_np(a.dtype), kind="ExternalInput").ap()
             for n, a in arrays.items()}
        out = nc.dram_tensor("out_0_dram", (1, S, D), _mybir.dt.float32, kind="ExternalOutput").ap()
        program(nc, t, out, turns, ONLY_FIRST)
    r = _run(nc, [arrays], core_ids=[0])
    return r.results[0]["out_0_dram"]
```

```python
from contextlib import ExitStack

import concourse.bass as bass
from concourse import mybir
import numpy as np

F32 = mybir.dt.float32
F32R = mybir.dt.float32r
I32 = mybir.dt.int32
ALU = mybir.AluOpType
ACT = mybir.ActivationFunctionType
AX = mybir.AxisListType

P = 128
D = 1024
S = 512
C = 256
HD = 64
NK = D // P
NT = S // P
NC = C // P
UN = 512
UK = UN // P
SCALE = HD ** -0.5
EPS = 1e-6
NEG = -1.0e30
NTAP = 31
PADT = NTAP // 2
DTAP = 16
NEXP = 16
FF = 4096
NHEADS = 16
KEYS = S + C
NSEL = 128
TAKEN = -3.0e38
BIG_E = 1.0e30
WIN = 127
V_BMOD, V_N1, V_N2, V_ATT, V_MLP, V_CB, V_CG, V_C, V_CC, V_ALL = 0, 48, 56, 64, 80, 96, 100, 104, 112, 120


class Tally:

    def __init__(self, eng, turns, key, start):
        self.eng, self.turns, self.key = eng, turns, key
        self.n, self.frames, self.loops = dict(start), [], 0

    def at(self, name, k=1):
        v = self.n.get(name, 0) + k
        for i, adds in self.frames:
            if adds.get(name, 0):
                v = i * adds[name] + v
        return v

    def next(self, name, k=1):
        v = self.at(name, k)
        self.skip(name, k)
        return v

    def skip(self, name, k=1):
        self.n[name] = self.n.get(name, 0) + k

    def loop(self, count, body):
        key = (self.key, self.loops)
        self.loops += 1
        before = dict(self.n)
        with self.eng.Fori(0, count) as i:
            self.frames.append((i, self.turns.get(key, {})))
            body(i)
            self.frames.pop()
        got = {s: v - before.get(s, 0) for s, v in self.n.items() if v != before.get(s, 0)}
        self.turns[key] = got
        for s, v in got.items():
            self.n[s] += (count - 1) * v


class Sems(dict):
    def __init__(self, nc, ctx):
        super().__init__()
        self.nc, self.ctx = nc, ctx

    def __missing__(self, name):
        self[name] = self.ctx.enter_context(self.nc.semaphore(name))
        return self[name]


STORES_1 = [("ctx_kv", 0, 2 + 2 * NC), ("ctx_nk", 1, 4), ("ctx_nv", 0, NC), ("nk", 0, 4), ("q", 1, 4),
            ("nq", 1, 4), ("kv", 0, 2 + 2 * NT), ("nv", 1, NT), ("fourier", 0, 1), ("gqa", 1, 1), ("na", 0, 1)]
STORES_2 = [("rqk", 0, 4), ("rv", 1, NT), ("sqk", 0, 4), ("sv", 1, NT), ("dq", 0, 4), ("dk", 1, 4), ("dv", 0, NT)]


def stored(seq, s, upto=None):
    n = 0
    for name, b, k in seq:
        n += 16 * k if b == s else 0
        if name == upto:
            break
    return n


def program(nc, t, out, turns, only_first=False):
    ctx = ExitStack()
    with ctx:
        def sb(name, shape, dt=F32):
            return ctx.enter_context(nc.sbuf_tensor(name, shape, dt))

        def flat(ap):
            return ap.rearrange("p a b -> p (a b)")

        sems = Sems(nc, ctx)

        X = sb("X", [P, NT, D])
        BIG = sb("BIG", [P, NT * D])
        hH, hL = sb("hH", [P, NK, S], F32R), sb("hL", [P, NK, S], F32R)
        aH, aL = sb("aH", [P, UK, S], F32R), sb("aL", [P, UK, S], F32R)
        W = [sb(f"W{i}", [P, UK, UN]) for i in range(2)]
        WH = [sb(f"WH{i}", [P, UK, UN], F32R) for i in range(2)]
        WL = [sb(f"WL{i}", [P, UK, UN], F32R) for i in range(2)]
        ST = [sb(f"ST{i}", [P, UK, S]) for i in range(2)]
        G = sb("G", [P, NK, S])
        Z = sb("Z", [P, 4, S + 2 * PADT])
        F = sb("F", [P, 2, 512])
        AT = sb("AT", [P, 3 * KEYS])
        QS = [sb(f"QS{i}", [P, S]) for i in range(2)]
        KS = [sb(f"KS{i}", [P, KEYS]) for i in range(2)]
        VS = [sb(f"VS{i}", [P, KEYS // P, HD]) for i in range(2)]
        ES = [sb(f"ES{i}", [P, 14, 64]) for i in range(2)]
        VT = sb("VT", [P, V_ALL])
        MODP = sb("MODP", [P, 52, 2])
        MOD = MODP[:, 4:52, :]
        CSH, CSL = sb("CSH", [P, NK, 2], F32R), sb("CSL", [P, NK, 2], F32R)
        CF = sb("CF", [P, 2, NK, 2])
        CW = sb("CW", [P, 4, 32])
        AF = sb("AF", [P, 4, NK])
        IDN = sb("IDN", [P, P])
        MSK = sb("MSK", [P, 64])
        CM = sb("CM", [P, P])
        RNW = sb("RNW", [P, 256])
        RB = sb("RB", [P, NEXP])
        WRH, WRL = sb("WRH", [P, NK, NEXP], F32R), sb("WRL", [P, NK, NEXP], F32R)
        GATE = sb("GATE", [P, NT, NEXP])
        SM = sb("SM", [P, 4, 32])
        MX, MXC, NM, DEN, RD = (sb(n, [P, 2]) for n in ("MX", "MXC", "NM", "DEN", "RD"))
        TOP = sb("TOP", [P, 8])
        WIX = sb("WIX", [P, NT, 8])

        BKP = ctx.enter_context(nc.psum_tensor("BKP", [P, 2048], F32))
        BK = [BKP[:, i * 512:(i + 1) * 512] for i in range(4)]
        SC = ctx.enter_context(nc.psum_tensor("SCP", [P, 1024], F32))
        TP = ctx.enter_context(nc.psum_tensor("TPP", [P, 1024], F32))
        OB = [BK[0][:, 0:HD], BK[1][:, 0:HD]]
        OT = [BK[s][s * HD:(s + 1) * HD, :] for s in range(2)]
        SCS = [SC[:, :], BKP[:, 1024:2048]]

        qT_d = nc.dram_tensor("qT_scratch", (NHEADS, HD, S), F32).ap()
        kT_d = nc.dram_tensor("kT_scratch", (NHEADS, HD, KEYS), F32).ap()
        v_d = nc.dram_tensor("v_scratch", (NHEADS, KEYS, HD), F32).ap()
        yT_d = nc.dram_tensor("yT_scratch", (4, 512, S), F32).ap()
        rpb_d = nc.dram_tensor("rpb_scratch", (8 * 15, 64, WIN), F32).ap()

        XN = BIG[:].rearrange("p (t d) -> p t d", t=NT)
        BV = BIG[:].rearrange("p (k s) -> p k s", k=NK)
        cH = flat(aH[:]).rearrange("p (k s) -> p k s", k=NK)
        cL = flat(aL[:]).rearrange("p (k s) -> p k s", k=NK)
        CTX = [flat(ST[i][:])[:, 0:D] for i in range(2)]
        CTN = flat(G[:])[:, 0:2 * D].rearrange("p (t d) -> p t d", t=2)
        TM = AT[:, 0:NT * 512].rearrange("p (t c) -> p t c", t=NT)
        T1, T2 = G[:, 0:4, :], G[:, 4:8, :]
        PR = [AT[:, b * KEYS:(b + 1) * KEYS] for b in range(2)]
        SB = [AT[:, 2 * KEYS:3 * KEYS], flat(W[1][:, 2:4, :])[:, 0:KEYS]]
        PTB_1 = [(W[0][:], W[1][:, 0:2, :]), (BV[:, 0:4, :], BV[:, 4:6, :])]
        PTB_2 = [(W[0][:],), (XN[:, :, 256:768],)]
        QX = [flat(WH[s][:])[:, 0:S] for s in range(2)]
        KX = [flat(WH[s][:])[:, S:S + KEYS] for s in range(2)]
        KL = [flat(WH[s][:])[0:HD, S + KEYS:S + 2 * KEYS] for s in range(2)]
        GB, GF = AT[:, 0:D], AT[:, D:2 * D]
        DG = AT[:, 2048:2304]
        VR = F[0:V_ALL, 0, 0:P]
        CWR = F[0:NTAP, 1, :]
        WR = Z[:, 0, 0:NK * NEXP].rearrange("p (k e) -> p k e", k=NK)
        RPB = Z[0:120, 1, 0:WIN]
        RC = flat(ES[1][:])[:, 0:256].rearrange("p (t d) -> p t d", t=NT)
        RS = flat(ES[1][:])[:, 256:512].rearrange("p (t d) -> p t d", t=NT)
        GQ, GK = flat(ES[1][:])[:, 512:576], flat(ES[1][:])[:, 576:640]
        KNW = flat(ES[1][:])[:, 512:640]
        ONE = AT[:, 1024:1152]
        TC = flat(ES[1][:])[:, 0:128].rearrange("p (t d) -> p t d", t=NT)
        TS = flat(ES[1][:])[:, 128:256].rearrange("p (t d) -> p t d", t=NT)
        XB = flat(ES[0][:])[:, 0:S]
        UKW, UVW = flat(ES[0][:])[:, 0:256], flat(ES[0][:])[:, 256:512]
        CU, CT = G[:, 0:4, :], G[:, 4:8, :]
        CD = BV[:, 6:8, :]
        ZF = flat(Z[:])
        CY = ZF[:, 0:4 * S].rearrange("p (k s) -> p k s", k=4)
        CKT, KIT = ZF[:, 0:512], ZF[:, 512:1024]
        SG = ZF[:, 1024:2048].rearrange("p (t c) -> p t c", t=NT)
        SEL, QI = G[:, 0:4, :], G[:, 4:8, :]
        IX = [SEL[:, tt, 0:(tt + 1) * P] for tt in range(NT)]
        RP = TM
        RT = lambda n: F[:, 0, n * 64:(n + 1) * 64].rearrange("p (t e) -> p t e", t=NT)
        RT2 = lambda n, w: F[:, 1, n * 64:n * 64 + NT * w].rearrange("p (t e) -> p t e", t=NT)

        block = ctx.enter_context(nc.Block())
        BANKS = [f"bank_free{j}" for j in range(4)]

        @block.sync
        def _(sp):
            T = Tally(sp, turns, "sp", {})
            slot = [0]

            def unit(src, n=UN):
                s = slot[0]
                slot[0] ^= 1
                sp.wait_ge(sems["w_lo"], T.next("w_lo"))
                sp.dma_start(W[s][:, :, 0:n], src.rearrange("(k p) n -> p k n", p=P)).then_inc(sems[f"w_landed{s}"], 16)

            def blk(w, col, n=UN):
                for r in range(2):
                    unit(w[r * UN:(r + 1) * UN, bass.ds(col, n)], n)

            def load(dst, src, name):
                sp.dma_start(dst, src).then_inc(sems[name], 16)

            def row(ap, n):
                return ap.rearrange("(o n) -> o n", o=1).to_broadcast([P, n])

            def pick(ap, l):
                return ap[bass.ds(l, 1)].rearrange("a k n -> (a k) n")

            rows = lambda ap: ap.rearrange("(r p) -> r p", p=P)
            load(VR[V_BMOD:V_N1, :], rows(t["b_mod"][0]), "vec_landed")
            load(VR[V_N1:V_N2, :], rows(t["norm1_g"][0]), "vec_landed")
            load(VR[V_N2:V_ATT, :], rows(t["norm2_g"][0]), "vec_landed")
            load(VR[V_ATT:V_MLP, :], t["attn_norm_w_2"].rearrange("l (r p) -> (l r) p", p=P), "vec_landed")
            load(VR[V_MLP:V_CB, :], t["mlp_norm_w_2"].rearrange("l (r p) -> (l r) p", p=P), "vec_landed")
            load(VR[V_CB:V_CG, :], rows(t["conv_b"][0]), "vec_landed")
            load(VR[V_CG:V_C, :], rows(t["conv_norm_g"][0]), "vec_landed")
            load(VR[V_C:V_CC, :], rows(t["c"][0]), "vec_landed")
            load(VR[V_CC:V_ALL, :], rows(t["c_ctx"]), "vec_landed")
            load(CWR, t["conv_w"][0], "vec_landed")
            load(IDN[:], t["k_ident"], "vec_landed")
            load(WR, t["w_router"].rearrange("(k p) e -> p k e", p=P), "wr_landed")
            for i in range(NT):
                load(X[:, i, :], t["x"][0, i * P:(i + 1) * P, :], "x_landed")
            for i in range(NC):
                load(CTX[i], t["ctx"][0, i * P:(i + 1) * P, :], "x_landed")
            sp.wait_ge(sems["rpb_zero"], T.next("rpb_zero"))
            load(RPB[:, 48:79], t["na_rpb"][0].rearrange("h m c -> (h m) c"), "rpb_landed")
            load(RC, t["k_ropec"], "tab_landed")
            load(RS, t["k_ropes"], "tab_landed")
            load(GQ, row(t["q_norm_g"][0], HD), "tab_landed")
            load(GK, row(t["k_norm_g"][0], HD), "tab_landed")
            load(MSK[:], t["k_colmask"], "tab_landed")
            load(CM[:], t["k_causal"], "tab_landed")
            load(RB[:], row(t["router_bias"], NEXP), "tab_landed")

            T.loop(12, lambda i: blk(t["w_mod"][0], i * UN))
            w = t["w_in"][0]
            sp.wait_ge(sems["rpb_landed"], T.next("rpb_landed", 16))
            for h, (col, n) in enumerate(((512, 256), (1280, UN), (1792, UN), (0, UN), (1280, UN), (512, 256), (768, UN),
                                          (1792, UN))):
                blk(w, col, n)
                load(rpb_d[h * 15:(h + 1) * 15], RPB[h * 15:(h + 1) * 15, :].unsqueeze(1).to_broadcast([15, 64, WIN]),
                     "rpb_stored")
            blk(w, 2304)
            sp.wait_ge(sems["norm_tr"], T.next("norm_tr", NK))
            load(BV[:, 0:4, :], t["k_dftc"].rearrange("(k p) s -> p k s", p=P), "fou_landed")
            load(BV[:, 4:8, :], t["k_dfts"].rearrange("(k p) s -> p k s", p=P), "fou_landed")
            sp.wait_ge(sems["nv_out"], T.next("nv_out"))
            load(DG, t["k_dftg"], "fou_landed")
            blk(w, 3328)
            blk(w, 2816)

            def heads(count, base, nk, bias=None, before=None):
                def qk(h, s):
                    for r in range(2):
                        load(QS[s][r * HD:(r + 1) * HD, :], pick(qT_d, h), f"qk_landed{s}")
                        load(KS[s][r * HD:(r + 1) * HD, 0:nk], pick(kT_d, h)[:, 0:nk], f"qk_landed{s}")

                def values(h, s):
                    load(VS[s][:, 0:nk // P, :], pick(v_d, h)[0:nk, :].rearrange("(t p) d -> p t d", p=P), f"head_landed{s}")
                for s in range(2):
                    if before:
                        before(s)
                    qk(base + s, s)
                for s in range(2):
                    if bias is not None:
                        bias(s, s)
                    values(base + s, s)
                T.skip("head_oe", 2)

                def later(i):
                    for s in range(2):
                        sp.wait_ge(sems["head_lo"], T.next("head_lo"))
                        sp.sem_inc(sems["sp_paused"], 1)
                        qk(i * 2 + (base + 2 + s), s)
                    for s in range(2):
                        if bias is None:
                            T.skip("head_nm", NT)
                        else:
                            sp.wait_ge(sems["head_nm"], T.next("head_nm", NT))
                            sp.sem_inc(sems["sp_paused"], 1)
                            bias(i * 2 + (2 + s), s)
                        sp.wait_ge(sems["head_oe"], T.next("head_oe"))
                        sp.sem_inc(sems["sp_paused"], 1)
                        values(i * 2 + (base + 2 + s), s)
                T.loop(count // 2 - 1, later)
                T.skip("head_lo", 2)
                T.skip("head_nm", 2 * NT)
                sp.wait_ge(sems["head_oe"], T.next("head_oe", 2))
                sp.sem_inc(sems["sp_paused"], 1)

            def retention_heads():
                def head(h, s):
                    load(QS[s][0:HD, :], pick(qT_d, h), f"head_landed{s}")
                    load(KS[s][0:HD, 0:S], pick(kT_d, h)[:, 0:S], f"head_landed{s}")
                    load(VS[s][:, 0:NT, :], pick(v_d, h)[0:S, :].rearrange("(t p) d -> p t d", p=P), f"head_landed{s}")
                    load(flat(ES[s][:])[:, 0:S], pick(t["k_decay"], h), f"head_landed{s}")
                for s in range(2):
                    sp.wait_ge(sems[f"st_written{s}"], T.at(f"st_written{s}", stored(STORES_2, s, "sv" if s else "sqk")))
                    sp.sem_inc(sems["sp_paused"], 1)
                for s in range(2):
                    head(s, s)
                for s in range(2):
                    sp.wait_ge(sems["ret_oe"], T.next("ret_oe", NT))
                    sp.sem_inc(sems["sp_paused"], 1)
                    head(2 + s, s)

            def after_retention(s):
                if s == 0:
                    for b in range(2):
                        sp.wait_ge(sems[f"st_written{b}"], T.next(f"st_written{b}", stored(STORES_2, b)))
                        sp.sem_inc(sems["sp_paused"], 1)
                sp.wait_ge(sems["ret_oe"], T.next("ret_oe", NT))
                sp.sem_inc(sems["sp_paused"], 1)
                if s == 0:
                    load(XB, t["k_dilbias"], "xb_landed")

            for s in range(2):
                sp.wait_ge(sems[f"st_written{s}"], T.at(f"st_written{s}", stored(STORES_1, s, "nv" if s else "kv")))

            heads(8, 0, KEYS)
            sp.wait_ge(sems["rpb_stored"], T.at("rpb_stored", 16 * 8))

            def na_bias(h, s):
                for rr in range(2):
                    src = bass.AP(rpb_d.tensor, h * (15 * 64 * WIN) + ((1 - rr) * 64 * WIN + 63),
                                  [[WIN - 1, 64], [64 * WIN, 14], [1, 64]])
                    load(ES[s][rr * 64:(rr + 1) * 64, :, :], src, f"bias_landed{s}")
            heads(8, 8, KEYS, na_bias)

            def branch(i):
                blk(w, i * D + 3840)
                if isinstance(i, int) and i == 0:
                    for s in range(2):
                        sp.wait_ge(sems[f"st_written{s}"], T.next(f"st_written{s}", stored(STORES_1, s)))
                if isinstance(i, int) and i == 3:
                    sp.wait_ge(sems["cv_written"], T.next("cv_written", 16))
                sp.wait_ge(sems["yb_used"], T.next("yb_used"))
                sp.sem_inc(sems["sp_paused"], 1)
                load(ST[1][:], pick(yT_d, i).rearrange("(k p) s -> p k s", p=P), "yb_landed")
                blk(w, i * D + (3840 + UN))
                for hf in range(2):
                    unit(pick(t["w_branch"][0], i)[:, hf * UN:(hf + 1) * UN])
            branch(0)
            T.loop(2, lambda i: branch(i + 1))
            branch(3)
            blk(t["w_out"][0], 0)
            blk(t["w_out"][0], UN)

            def expert(e):
                gu = pick(t["w_expert_gu"][0], e)
                blk(gu, 0)
                blk(gu, UN)
                for hf in range(2):
                    unit(pick(t["w_expert_down"][0], e)[:, hf * UN:(hf + 1) * UN])
            T.loop(NEXP, expert)
            load(GF, row(t["final_norm_g"], D), "gf_landed")

            def layer(l):
                w2 = pick(t["w_in_2"], l)
                blk(w2, 0)
                sp.wait_ge(sems["es_free"], T.next("es_free"))
                sp.sem_inc(sems["sp_paused"], 1)
                load(TC, t["k_retc"], "lay_landed")
                load(TS, t["k_rets"], "lay_landed")
                load(UKW, pick(t["dsa_w_uk_2"], l), "lay_landed")
                load(UVW, pick(t["dsa_w_uv_2"], l), "lay_landed")
                load(KNW, t["dsa_kv_norm_w_2"][bass.ds(l, 1), :].to_broadcast([P, P]), "lay_landed")
                load(RNW[:], t["ret_norm_w_2"].rearrange("l h d -> l (h d)")[bass.ds(l, 1), :].to_broadcast([P, 256]), "lay_landed")
                blk(w2, UN)
                blk(w2, 1024, 384)
                blk(w2, 1408)
                blk(w2, 1920, 72)
                for b in range(3):
                    blk(w2, 1992 + b * UN)
                retention_heads()
                heads(12, 4, S, before=after_retention)
                wo = pick(t["w_out_2"], l)
                blk(wo, 0)
                blk(wo, UN)

                def chunk(c):
                    blk(pick(t["w_up_2"], l), c * UN)
                    for hf in range(2):
                        unit(t["w_down_2"][bass.ds(l, 1), bass.ds(c * UN, UN), hf * UN:(hf + 1) * UN]
                             .rearrange("a k n -> (a k) n"))
                sp.sem_inc(sems["sp_paused"], 1)
                T.loop(FF // UN, chunk)
            if not only_first:
                T.loop(2, layer)
                load(GF, row(t["final_norm_w_2"], D), "gf_landed")
            for i in range(NT):
                sp.wait_ge(sems["out_ready"], T.next("out_ready"))
                sp.dma_start(out[0, i * P:(i + 1) * P, :], XN[:, i, :]).then_inc(sems["out_written"], 16)
            sp.wait_ge(sems["out_written"], T.next("out_written", 16 * NT))

        @block.gpsimd
        def _(pool):
            T = Tally(pool, turns, "pool", {})
            pool.memset(RPB, 0.0).then_inc(sems["rpb_zero"], 1)

            def store(seq, name, dmas):
                s = [b for n, b, _ in seq if n == name][0]
                assert len(dmas) == [k for n, _, k in seq if n == name][0], name
                pool.wait_ge(sems[name + "_out"], T.next(name + "_out"))
                pool.sem_inc(sems["pool_paused"], 1)
                for dst, src in dmas:
                    pool.dma_start(dst, src).then_inc(sems[f"st_written{s}"], 16)

            def qk(dst, s, b0=0, nb=4):
                return [(dst[2 * b:2 * b + 2].rearrange("h d s -> (h d) s"), ST[s][:, b0 + b, 0:dst.shape[2]])
                        for b in range(nb)]

            def vv(dst, s, nt):
                nh = dst.shape[0]
                return [(dst[:, i * P:(i + 1) * P, :].rearrange("h p d -> p h d"),
                         ST[s][:, i, 0:nh * HD].rearrange("p (h d) -> p h d", h=nh)) for i in range(nt)]

            def kv(s, c0, nt):
                dm = []
                vt = flat(ST[s][:, 2:4, :]).rearrange("p (t c) -> p t c", t=8)
                for g in range(2):
                    dm.append((kT_d[4 * g:4 * g + 4, :, c0:c0 + nt * P].rearrange("r d s -> d r s"),
                               ST[s][g * HD:(g + 1) * HD, 0, 0:nt * P].unsqueeze(1).to_broadcast([HD, 4, nt * P])))
                    for i in range(nt):
                        dm.append((v_d[4 * g:4 * g + 4, c0 + i * P:c0 + (i + 1) * P, :].rearrange("r p d -> p r d"),
                                   vt[:, i, g * HD:(g + 1) * HD].unsqueeze(1).to_broadcast([P, 4, HD])))
                return dm

            store(STORES_1, "ctx_kv", kv(0, S, NC))
            store(STORES_1, "ctx_nk", qk(kT_d[8:16, :, S:KEYS], 1))
            store(STORES_1, "ctx_nv", vv(v_d[8:16, S:KEYS, :], 0, NC))
            store(STORES_1, "nk", qk(kT_d[8:16, :, 0:S], 0))
            store(STORES_1, "q", qk(qT_d[0:8], 1))
            store(STORES_1, "nq", qk(qT_d[8:16], 1))
            store(STORES_1, "kv", kv(0, 0, NT))
            store(STORES_1, "nv", vv(v_d[8:16, 0:S, :], 1, NT))
            store(STORES_1, "fourier", [(yT_d[2].rearrange("(k p) s -> p k s", p=P), ST[0][:])])

            pool.wait_ge(sems["z_ready"], T.next("z_ready"))
            pool.memset(CU, 0.0).then_inc(sems["pool_self"], 1)
            pool.wait_ge(sems["pool_self"], T.next("pool_self"))

            def tap(k, b0=0):
                pool.tensor_tensor(CT[:, b0:4, :], Z[:, b0:4, bass.ds(k, S)],
                                   CW[:, b0:4, bass.ds(k, 1)].to_broadcast([P, 4 - b0, S]),
                                   ALU.mult).then_inc(sems["pool_self"], 1)
                pool.wait_ge(sems["pool_self"], T.next("pool_self"))
                pool.tensor_tensor(CU[:, b0:4, :], CU[:, b0:4, :], CT[:, b0:4, :], ALU.add).then_inc(
                    sems["pool_self"], 1)
                pool.wait_ge(sems["pool_self"], T.next("pool_self"))
            T.loop(NTAP - DTAP, lambda k: tap(k + DTAP))
            T.loop(DTAP, lambda k: tap(k, 2))
            pool.sem_inc(sems["conv_done"], 1)
            store(STORES_1, "gqa", [(yT_d[0].rearrange("(k p) s -> p k s", p=P), ST[1][:])])
            store(STORES_1, "na", [(yT_d[1].rearrange("(k p) s -> p k s", p=P), ST[0][:])])
            pool.wait_ge(sems["cv_out"], T.next("cv_out"))
            pool.dma_start(yT_d[3].rearrange("(k p) s -> p k s", p=P), CY).then_inc(sems["cv_written"], 16)

            def layer(l):
                store(STORES_2, "rqk", qk(qT_d[0:4], 0, 0, 2) + qk(kT_d[0:4, :, 0:S], 0, 2, 2))
                store(STORES_2, "rv", vv(v_d[0:4, 0:S, :], 1, NT))
                store(STORES_2, "sqk", qk(qT_d[4:8], 0, 0, 2) + qk(kT_d[4:8, :, 0:S], 0, 2, 2))
                store(STORES_2, "sv", vv(v_d[4:8, 0:S, :], 1, NT))
                store(STORES_2, "dq", qk(qT_d[8:16], 0))
                store(STORES_2, "dk", qk(kT_d[8:16, :, 0:S], 1))
                store(STORES_2, "dv", vv(v_d[8:16, 0:S, :], 0, NT))
            if not only_first:
                T.loop(2, layer)
            for s in range(2):
                pool.wait_ge(sems[f"st_written{s}"],
                             stored(STORES_1, s) + (0 if only_first else 2 * stored(STORES_2, s)))
            pool.wait_ge(sems["cv_written"], 16)

        @block.tensor
        def _(pe):
            T = Tally(pe, turns, "pe", {"w_lo": 2, "yb_used": 1})
            slot = [0]
            h, cx, aa, cs = (hH[:], hL[:]), (cH, cL), (aH[:], aL[:]), (CSH[:], CSL[:])

            def unit(act, k0, form, n, start, stop, nj=4, ready=None):
                s = slot[0]
                slot[0] ^= 1
                pe.wait_ge(sems["w_lo"], T.next("w_lo"))
                ah, al = act
                cols = n if form == "T" else ah.shape[2]
                for j in range(nj):
                    if start:
                        pe.wait_ge(sems[BANKS[j]], T.at(BANKS[j]))
                    q = []
                    for k in range(UK):
                        for wp, ap in ((WH, ah), (WL, ah), (WH, al)):
                            if form == "F":
                                q.append((wp[s][:, k, j * P:(j + 1) * P], ap[:, k0 + k, :]))
                            else:
                                q.append((ap[:, k0 + k, j * P:(j + 1) * P], wp[s][:, k, 0:n]))
                    for a, (lt, rh) in enumerate(q):
                        if ready and j == 0 and a % 3 == 0:
                            pe.wait_ge(sems[ready], T.next(ready))
                        mm = pe.matmul(BK[j][:, 0:cols], lt, rh, start=start and a == 0,
                                       stop=stop and a == len(q) - 1, skip_group_check=True)
                    mm.then_inc(sems["gemm_done"], 4 // nj)
                if start:
                    for b in BANKS:
                        T.skip(b)

            def blk(act, form, n=UN, nj=4, ready=None):
                unit(act, 0, form, n, True, False, nj, ready)
                unit(act, 4, form, n, False, True, nj, ready)

            def turn(name, src, nt, nk):
                for k in range(nk):
                    if k >= 2:
                        pe.wait_ge(sems[name + "_free"], T.next(name + "_free"))
                    for i in range(nt):
                        c0 = (k % 2) * 512 + i * P
                        mm = pe.transpose(TP[:, c0:c0 + P], src(i, k), IDN[:])
                    mm.then_inc(sems[name + "_tr"], 1)
                pe.wait_ge(sems[name + "_free"], T.next(name + "_free", min(2, nk)))

            cols_of = lambda v: (lambda i, k: v[:, i, k * P:(k + 1) * P])

            pe.wait_ge(sems["vec_landed"], T.next("vec_landed", 16 * 11))
            pe.transpose(TP[:, 0:V_ALL], VR, IDN[0:V_ALL, 0:V_ALL])
            for j in range(4):
                mm = pe.transpose(TP[:, 128 + j * 32:128 + j * 32 + NTAP], CWR[:, j * P:(j + 1) * P],
                                  IDN[0:NTAP, 0:NTAP])
            mm.then_inc(sems["vec_tr"], 1)
            pe.wait_ge(sems["cs_lo"], T.next("cs_lo"))

            def mod_column():
                pe.wait_ge(sems["bank_free0"], T.next("bank_free0"))
                pe.sem_inc(sems["pe_paused"], 1)
                for j in range(4):
                    mm = pe.transpose(TP[:, j * 2:j * 2 + 2], F[0:2, 0, j * P:(j + 1) * P], IDN[0:2, 0:2])
                mm.then_inc(sems["mod_col"], 1)

            def mod(i):
                for half in range(2):
                    s = slot[0]
                    slot[0] ^= 1
                    pe.wait_ge(sems["w_lo"], T.next("w_lo"))
                    if half == 0:
                        pe.wait_ge(sems["bank_free0"], T.at("bank_free0"))
                    q = [(a, w[s][:, k, :], half * 4 + k) for k in range(UK) for a, w in ((CSH, WH), (CSH, WL), (CSL, WH))]
                    for n, (a, w, k) in enumerate(q):
                        mm = pe.matmul(BK[0][0:2, :], a[:, k, :], w, start=half == 0 and n == 0,
                                       stop=half == 1 and n == len(q) - 1, skip_group_check=True)
                    mm.then_inc(sems["gemm_done"], 4)
                    if half == 0:
                        pe.wait_ge(sems["mod_out"], T.next("mod_out"))
                        mod_column()
            T.loop(12, mod)
            pe.wait_ge(sems["mod_out"], T.next("mod_out"))
            mod_column()
            T.skip("bank_free0", -1)
            pe.wait_ge(sems["mod_out"], T.next("mod_out"))
            pe.wait_ge(sems["norm_xn"], T.next("norm_xn", NC))
            turn("norm", cols_of(CTN), NC, NK)
            pe.wait_ge(sems["norm_xn"], T.next("norm_xn", NT))
            turn("norm", cols_of(XN), NT, NK)
            blk(cx, "T", 256, 2, "norm_lo")
            blk(cx, "F")
            pe.wait_ge(sems["ck_rms"], T.next("ck_rms"))
            turn("sink", cols_of(TM), NC, 1)
            blk(cx, "T", UN, 2)
            blk(h, "T", ready="norm_lo")
            blk(h, "F")
            pe.wait_ge(sems["q_rope"], T.next("q_rope"))
            turn("sink", cols_of(TM), NT, 4)
            blk(h, "T", 256)
            blk(h, "F")
            pe.wait_ge(sems["k_rope"], T.next("k_rope"))
            turn("sink", cols_of(TM), NT, 1)
            blk(h, "T")
            blk(h, "T")
            pe.wait_ge(sems["fou_landed"], T.next("fou_landed", 48))
            pe.wait_ge(sems["fou_in"], T.next("fou_in"))
            for g in range(4):
                for part in range(2):
                    for k in range(4):
                        mm = pe.matmul(SC[:, part * 512:(part + 1) * 512], TM[:, k, g * P:(g + 1) * P],
                                       BV[:, part * 4 + k, :], start=k == 0, stop=k == 3)
                mm.then_inc(sems["fo_a"], 1)
                pe.wait_ge(sems["fo_cp"], T.next("fo_cp"))
                if g:
                    pe.wait_ge(sems["fo_o"], T.next("fo_o"))
                for part in range(2):
                    mm = pe.matmul(TP[:, 0:512], DG[:, part * P:(part + 1) * P], F[:, part, :],
                                   start=part == 0, stop=part == 1)
                mm.then_inc(sems["fo_b"], 1)
            pe.wait_ge(sems["fo_o"], T.next("fo_o"))
            blk(h, "F")
            blk(h, "F")

            def attend(count, loads, keys, PTB, read):
                chunks = lambda n: range(0, keys(n % NT), 512)

                def scores(n):
                    s, tt = (n // NT) % 2, n % NT
                    if tt == 0:
                        pe.wait_ge(sems["head_lo"], T.next("head_lo"))
                    nk = keys(tt)
                    for c0 in range(0, nk, 512):
                        c1 = min(nk, c0 + 512)
                        dst = SCS[n % 2][:, c0:c1]
                        pe.matmul(dst, QX[s][:, tt * P:(tt + 1) * P], KX[s][:, c0:c1], start=True, stop=False,
                                  skip_group_check=True)
                        mm = pe.matmul(dst, QX[s][0:HD, tt * P:(tt + 1) * P], KL[s][:, c0:c1], start=False, stop=True,
                                       skip_group_check=True)
                    mm.then_inc(sems["head_s"], 1)

                def turned(n):
                    pe.wait_ge(sems["head_pn"], T.next("head_pn"))
                    for c, c0 in enumerate(chunks(n)):
                        pe.wait_ge(sems["head_ptc"], T.next("head_ptc:free"))
                        bank = (n if len(chunks(n)) == 1 else c) % 2 * 512
                        for k0 in range(c0, min(c0 + 512, keys(n % NT)), P):
                            mm = pe.transpose(TP[:, bank + k0 - c0:bank + k0 - c0 + P], PR[n % 2][:, k0:k0 + P], IDN[:])
                        mm.then_inc(sems["head_pt"], 1)

                def values(s):
                    done = sum(len(chunks(tt)) for tt in range(NT))
                    pe.wait_ge(sems["head_ptc"], T.next("head_ptc:full", done))
                    pe.wait_ge(sems["head_oe"], T.next("head_oe"))
                    pe.wait_ge(sems[f"head_landed{s}"], T.next(f"head_landed{s}", 16 * loads))
                    nk = keys(NT - 1) // P
                    for kt in range(nk):
                        q0 = kt * P if keys(0) == P else 0
                        mm = pe.matmul(OT[s][:, q0:S], VS[s][:, kt, :], PTB[s][kt // 4][:, kt % 4, q0:S], start=kt == 0,
                                       stop=kt == nk - 1, skip_group_check=True)
                    mm.then_inc(sems["head_o"], 1)

                def body(first, last):
                    for n in range(2 * NT):
                        if n + 2 < 2 * NT or not last:
                            pe.wait_ge(sems[read], T.next(read))
                            scores(n + 2)
                        else:
                            T.skip(read)
                        turned(n)
                        if n % NT == 0 and not (first and n == 0):
                            values(1 if n == 0 else 0)
                for b in BANKS:
                    pe.wait_ge(sems[b], T.at(b))
                pe.sem_inc(sems["head_o"], 2)
                T.skip("head_ptc:full", 2)
                scores(0)
                scores(1)
                body(True, False)
                pe.sem_inc(sems["pe_paused"], 1)
                if count > 4:
                    T.loop(count // 2 - 2, lambda i: body(False, False))
                body(False, True)
                values(1)
                T.skip("head_ptc:free", 2)
                pe.wait_ge(sems["head_oe"], T.next("head_oe", 2))

            attend(8, 1, lambda tt: KEYS, PTB_1, "head_exp")
            T.skip("head_nm", 8 * NT)
            attend(8, 1, lambda tt: KEYS, PTB_1, "head_nm")
            pe.wait_ge(sems["cv_sq"], T.next("cv_sq"))
            for j in range(4):
                mm = pe.matmul(SC[:, 0:512], ONE, CT[:, j, :], start=j == 0, stop=j == 3)
            mm.then_inc(sems["cv_pe"], 1)
            pe.wait_ge(sems["cv_r"], T.next("cv_r"))

            def branch(i):
                blk(h, "F")
                blk(h, "F")
                pe.wait_ge(sems["yb_used"], T.next("yb_used"))
                unit(aa, 0, "F", UN, True, True)
                unit(aa, 0, "F", UN, True, True)
            T.loop(4, branch)

            def spread(name):
                pe.wait_ge(sems[name + "_in"], T.next(name + "_in"))
                for k in range(NK):
                    mm = pe.matmul(SC[:, k * P:(k + 1) * P], flat(ST[0][:])[:, k * P:(k + 1) * P], IDN[:],
                                   start=True, stop=True, skip_group_check=True)
                mm.then_inc(sems[name + "_pe"], 1)
                pe.wait_ge(sems[name + "_gb"], T.next(name + "_gb"))
            spread("g1")
            blk(h, "T", ready="norm_lo")
            blk(h, "T")
            pe.wait_ge(sems["norm_xn"], T.next("norm_xn", NT))
            turn("norm", cols_of(XN), NT, NK)
            pe.wait_ge(sems["norm_lo"], T.next("norm_lo", NK))
            pe.wait_ge(sems["wr_lo"], T.next("wr_lo"))
            for i in range(NT):
                q = [(a, b, k) for k in range(NK) for a, b in ((hH, WRH), (hH, WRL), (hL, WRH), (hL, WRL))]
                for n, (a, b, k) in enumerate(q):
                    mm = pe.matmul(TP[:, i * NEXP:(i + 1) * NEXP], a[:, k, i * P:(i + 1) * P], b[:, k, :],
                                   start=n == 0, stop=n == len(q) - 1, skip_group_check=True)
            mm.then_inc(sems["rt_pe"], 1)

            spread("g2")

            def expert(e):
                blk(h, "F")
                blk(h, "F")
                unit(aa, 0, "T", UN, True, True, ready="hid_lo")
                unit(aa, 0, "T", UN, True, True)
            T.loop(NEXP, expert)

            def layer(l):
                pe.wait_ge(sems["norm_xn"], T.next("norm_xn", NT))
                turn("norm", cols_of(XN), NT, NK)
                blk(h, "T", ready="norm_lo")
                blk(h, "T")
                pe.wait_ge(sems["rqk_rope"], T.next("rqk_rope"))
                turn("sink", cols_of(TM), NT, 4)
                blk(h, "T", 384)
                blk(h, "F")
                pe.wait_ge(sems["lat_rms"], T.next("lat_rms"))
                turn("sink", cols_of(TM), NT, 3)
                blk(h, "T", 72)
                pe.wait_ge(sems["lay_landed"], T.next("lay_landed", 16 * 6))
                for b in range(2):
                    mm = pe.matmul(SC[:, b * 512:(b + 1) * 512], UKW[:, b * P:(b + 1) * P], CKT, start=True, stop=True)
                for i in range(NT):
                    mm = pe.matmul(TP[:, i * 256:(i + 1) * 256], CKT[:, i * P:(i + 1) * P], UVW,
                                   start=True, stop=True, skip_group_check=True)
                mm.then_inc(sems["uk_pe"], 1)
                pe.wait_ge(sems["uk_cp"], T.next("uk_cp"))
                pe.wait_ge(sems["ki_out"], T.next("ki_out"))
                turn("sink", cols_of(TM), NT, 1)
                n = 0
                for tt in range(1, NT):
                    nk = (tt + 1) * P
                    for ih in range(8):
                        if n >= 2:
                            pe.wait_ge(sems["ix_act"], T.next("ix_act"))
                        p0 = (ih % 2) * HD
                        pe.matmul(SC[:, (n % 2) * 512:(n % 2) * 512 + nk],
                                  QI[p0:p0 + HD, ih // 2, tt * P:(tt + 1) * P], KIT[p0:p0 + HD, 0:nk],
                                  start=True, stop=True).then_inc(sems["ix_pe"], 1)
                        n += 1
                pe.wait_ge(sems["ix_act"], T.next("ix_act", 2))
                blk(h, "F")
                blk(h, "F")
                blk(h, "T")
                pe.wait_ge(sems["sel_done"], T.next("sel_done"))

                def ret(i):
                    for s in range(2):
                        pe.wait_ge(sems[f"head_landed{s}"], T.next(f"head_landed{s}", 64))
                        for kt in range(NT):
                            if kt >= 2:
                                pe.wait_ge(sems["ret_d"], T.next("ret_d"))
                            bank = SC if kt % 2 == 0 else TP
                            pe.matmul(bank[:, 0:S - kt * P], KS[s][0:HD, kt * P:(kt + 1) * P], QS[s][0:HD, kt * P:S],
                                      start=True, stop=True, skip_group_check=True).then_inc(sems["ret_s"], 1)
                        pe.wait_ge(sems["ret_d"], T.next("ret_d", 2))
                        for tt in range(NT):
                            if tt:
                                pe.wait_ge(sems["ret_oe"], T.next("ret_oe"))
                            for kt in range(tt + 1):
                                mm = pe.matmul(OB[tt % 2], RP[:, kt, (tt - kt) * P:(tt - kt + 1) * P],
                                               VS[s][:, kt, :], start=kt == 0, stop=kt == tt, skip_group_check=True)
                            mm.then_inc(sems["ret_o"], 1)
                        pe.wait_ge(sems["ret_oe"], T.next("ret_oe"))
                for b in BANKS[:2]:
                    pe.wait_ge(sems[b], T.at(b))
                pe.sem_inc(sems["pe_paused"], 1)
                T.loop(2, ret)
                attend(12, 1, lambda tt: (tt + 1) * P, PTB_2, "head_nm")
                pe.wait_ge(sems["mix_ready"], T.next("mix_ready"))
                turn("norm", cols_of(XN), NT, 2)
                pe.wait_ge(sems["norm_lo"], T.next("norm_lo", 2))
                blk(h, "T")
                blk(h, "T")
                pe.wait_ge(sems["norm_xn"], T.next("norm_xn", NT))
                turn("norm", cols_of(XN), NT, NK)

                def chunk(c, ready=None):
                    blk(h, "F", ready=ready)
                    unit(aa, 0, "T", UN, True, True, ready="hid_lo")
                    unit(aa, 0, "T", UN, True, True)
                chunk(0, "norm_lo")
                pe.sem_inc(sems["pe_paused"], 1)
                T.loop(FF // UN - 1, chunk)
            if not only_first:
                T.loop(2, layer)

        @block.scalar
        def _(act):
            T = Tally(act, turns, "act", {b: 1 for b in BANKS})
            T.n["gemm_done:out"] = 8
            slot = [0]

            def hi():
                s = slot[0]
                slot[0] ^= 1
                act.wait_ge(sems[f"w_landed{s}"], T.next(f"w_landed{s}", 16))
                act.wait_ge(sems["gemm_done"], T.next("gemm_done:w", 4))
                act.activation(WH[s][:], W[s][:], ACT.Copy).then_inc(sems["w_hi"], 1)

            def unit(evac=None, more=True):
                if more:
                    hi()
                T.skip("gemm_done:out", 4)
                if evac is not None:
                    T.skip("gemm_done:out", -4)
                    evac()
                    T.skip("gemm_done:out", 4)

            def blk(evac=None, more=True):
                unit()
                unit(evac, more)
                for b in BANKS:
                    T.skip(b)

            def out(j, nj=4):
                act.wait_ge(sems["gemm_done"], T.at("gemm_done:out", (j + 1) * (4 // nj)))

            def copies(dst, cols=UN, nj=4, ready=None):
                def go():
                    for j in range(nj):
                        out(j, nj)
                        act.activation(dst(j), BK[j][:, 0:cols], ACT.Copy).then_inc(sems[BANKS[j]], 1)
                    for j in range(nj, 4):
                        act.sem_inc(sems[BANKS[j]], 1)
                    if ready:
                        act.wait_ge(sems[BANKS[nj - 1]], T.at(BANKS[nj - 1]))
                        act.sem_inc(sems[ready], 1)
                return go

            held = {0: 0, 1: 0}

            def begin(seq, name):
                s = [b for n, b, _ in seq if n == name][0]
                if held[s]:
                    act.wait_ge(sems[f"st_written{s}"], T.next(f"st_written{s}", held[s]))
                held[s] = 16 * [k for n, _, k in seq if n == name][0]
                return s

            def sink(name, nk, dst, w=S):
                for k in range(nk):
                    act.wait_ge(sems[name + "_tr"], T.next(name + "_tr"))
                    act.activation(dst(k), TP[:, (k % 2) * 512:(k % 2) * 512 + w], ACT.Copy).then_inc(
                        sems[name + "_free"], 1)
                act.wait_ge(sems[name + "_free"], T.next(name + "_free", nk))

            def split(name, nk, dst, w=S):
                for k in range(nk):
                    act.wait_ge(sems[name + "_free"], T.next(name + "_free"))
                    act.activation(dst[:, k, :], F[:, k % 2, 0:w], ACT.Copy).then_inc(sems[name + "_hi"], 1)

            def squares(name, src, nt, ready=None):
                for i in range(nt):
                    if ready:
                        act.wait_ge(sems[ready], T.next(ready))
                    act.activation((CTN if nt == NC else XN)[:, i, :], src(i), ACT.Square, accum_out=SM[:, 0, i:i + 1]).then_inc(
                        sems[name + "_ss"], 1)
                    act.wait_ge(sems[name + "_ss"], T.next(name + "_ss"))


            def mod(i):
                hi()
                T.skip("gemm_done:out", 4)
                hi()
                out(3)
                act.activation(F[0:2, 0, :], BK[0][0:2, :], ACT.Copy).then_inc(sems["bank_free0"], 1)
                T.skip("gemm_done:out", 4)
                T.skip("bank_free0")

            hi()
            act.wait_ge(sems["vec_cp"], T.next("vec_cp"))
            act.activation(CF[:, 0, :, :], CF[:, 1, :, :], ACT.Sigmoid).then_inc(sems["cs_sig"], 1)
            act.wait_ge(sems["cs_val"], T.next("cs_val"))
            act.activation(CSH[:], CF[:, 0, :, :], ACT.Copy).then_inc(sems["cs_hi"], 1)
            act.wait_ge(sems["wr_landed"], T.next("wr_landed", 16))
            act.activation(WRH[:], WR, ACT.Copy).then_inc(sems["wr_hi"], 1)
            act.wait_ge(sems["x_landed"], T.next("x_landed", 16 * (NT + NC)))
            squares("norm", lambda i: CTX[i], NC)
            act.wait_ge(sems["norm_rd"], T.next("norm_rd"))
            squares("norm", lambda i: X[:, i, :], NT)
            act.wait_ge(sems["norm_rd"], T.next("norm_rd"))
            T.loop(12, mod)
            act.wait_ge(sems["mod_done"], T.next("mod_done"))
            split("norm", NK, cH, C)
            split("norm", NK, hH[:])
            s = begin(STORES_1, "ctx_kv")
            blk(copies(lambda j: TM[:, j, 0:256], 256, 2, "ck_in"))
            s1 = begin(STORES_1, "ctx_nk")
            blk(copies(lambda j: ST[s1][:, j, 0:C], C, 4, "ctx_nk_out"))

            def kv_sink(nt, ready):
                vt = flat(ST[0][:, 2:4, :]).rearrange("p (t c) -> p t c", t=8)
                sink("sink", 1, lambda k: ST[0][:, 0, 0:nt * P], nt * P)
                act.activation(vt[:, 0:nt, :], TM[:, 0:nt, P:256], ACT.Copy).then_inc(sems["act_self"], 1)
                act.wait_ge(sems["act_self"], T.next("act_self"))
                act.sem_inc(sems[ready], 1)
            kv_sink(NC, "ctx_kv_out")
            s = begin(STORES_1, "ctx_nv")
            blk(copies(lambda j: ST[0][:, j, :], UN, 2, "ctx_nv_out"))
            blk(copies(lambda j: TM[:, j, :], UN, 4, "q_in"))
            begin(STORES_1, "nk")
            blk(copies(lambda j: ST[0][:, j, :], UN, 4, "nk_out"))
            begin(STORES_1, "q")
            sink("sink", 4, lambda k: ST[1][:, k, :])
            act.sem_inc(sems["q_out"], 1)
            blk(copies(lambda j: TM[:, j, 0:256], 256, 4, "k_in"))
            begin(STORES_1, "nq")
            blk(copies(lambda j: ST[1][:, j, :], UN, 4, "nq_out"))
            begin(STORES_1, "kv")
            kv_sink(NT, "kv_out")
            begin(STORES_1, "nv")
            blk(copies(lambda j: ST[1][:, j, :], UN, 4, "nv_out"))
            blk(copies(lambda j: TM[:, j, :], UN, 4, "fou_in"))
            begin(STORES_1, "fourier")
            for g in range(4):
                act.wait_ge(sems["fo_a"], T.next("fo_a"))
                act.activation(flat(F[:]), SC[:], ACT.Copy).then_inc(sems["fo_cp"], 1)
                act.wait_ge(sems["fo_b"], T.next("fo_b"))
                act.activation(ST[0][:, g, :], TP[:, 0:512], ACT.Copy).then_inc(sems["fo_o"], 1)
            act.wait_ge(sems["fo_o"], T.next("fo_o", 4))
            act.sem_inc(sems["fourier_out"], 1)

            def conv_gate():
                for j in range(4):
                    out(j)
                    act.activation(CT[:, j, :], BK[j], ACT.Sigmoid).then_inc(sems[BANKS[j]], 1)
            blk(conv_gate)
            blk(None, False)

            def attend(count, keys, biased, PTB):
                def rounded(s):
                    act.wait_ge(sems[f"qk_landed{s}"], T.next(f"qk_landed{s}", 64))
                    act.activation(QX[s], QS[s][:], ACT.Copy)
                    act.activation(KX[s][:, 0:keys(NT - 1)], KS[s][:, 0:keys(NT - 1)], ACT.Copy).then_inc(sems["head_hi"], 1)

                def exponential(n):
                    nk = keys(n % NT)
                    act.wait_ge(sems["head_nm"], T.next("head_nm"))
                    src = SB[n % 2] if biased else SCS[n % 2]
                    act.activation(PR[n % 2][:, 0:nk], src[:, 0:nk], ACT.Exp, bias=NM[:, n % 2:n % 2 + 1],
                                   scale=SCALE,
                                   accum_out=DEN[:, n % 2:n % 2 + 1]).then_inc(sems["head_exp"], 1)

                def body(last):
                    for n in range(2 * NT):
                        s, tt = n // NT, n % NT
                        if n + 1 < 2 * NT or not last:
                            exponential((n + 1) % (2 * NT))
                        if tt == 1 and not (last and s == 1):
                            rounded(1 - s)
                        if tt == 0:
                            act.wait_ge(sems["head_o"], T.next("head_o:free"))
                        for c, c0 in enumerate(range(0, keys(tt), 512)):
                            c1 = min(c0 + 512, keys(tt))
                            bank = (n if keys(tt) <= 512 else c) % 2 * 512
                            act.wait_ge(sems["head_pt"], T.next("head_pt"))
                            act.activation(PTB[s][c][:, 0:(c1 - c0) // P, tt * P:(tt + 1) * P],
                                           TP[:, bank:bank + c1 - c0].rearrange("p (k q) -> p k q", q=P),
                                           ACT.Copy).then_inc(sems["head_ptc"], 1)
                act.wait_ge(sems["head_go"], T.next("head_go"))
                act.sem_inc(sems["head_ptc"], 2)
                rounded(0)
                exponential(0)
                act.sem_inc(sems["act_paused"], 1)
                T.loop(count // 2 - 1, lambda i: body(False))
                body(True)
                T.skip("head_o:free", 2)

            attend(8, lambda tt: KEYS, False, PTB_1)
            attend(8, lambda tt: KEYS, True, PTB_1)
            begin(STORES_1, "gqa")
            begin(STORES_1, "na")
            hi()
            act.wait_ge(sems["cv_n"], T.next("cv_n"))
            act.activation(CT, CU, ACT.Sigmoid).then_inc(sems["cv_sig"], 1)

            def gates(hb):
                def go():
                    for j in range(4):
                        out(j)
                        act.activation(G[:, hb * 4 + j, :], BK[j], ACT.Sigmoid).then_inc(sems[BANKS[j]], 1)
                return go

            def skip_banks():
                for b in BANKS:
                    T.skip(b)

            act.wait_ge(sems["g_free"], T.next("g_free"))

            def branch(i):
                blk(gates(0))
                act.wait_ge(sems["yb_landed"], T.next("yb_landed", 16))
                act.activation(aH[:], ST[1][:], ACT.Copy).then_inc(sems["yb_hi"], 1)
                blk(gates(1))
                for _ in range(2):
                    unit()
                    skip_banks()
            T.loop(4, branch)

            def spread(name):
                act.wait_ge(sems[name + "_pe"], T.next(name + "_pe"))
                act.activation(GB, SC[:], ACT.Copy).then_inc(sems[name + "_gb"], 1)
            spread("g1")
            for k in range(NK):
                act.wait_ge(sems["m_go"], T.next("m_go")) if k == 0 else None
                act.activation(hH[:, k, :], BV[:, k, :], ACT.Copy).then_inc(sems["norm_hi"], 1)
            blk()
            blk()
            squares("norm", lambda i: X[:, i, :], NT, "x2")
            act.wait_ge(sems["norm_rd"], T.next("norm_rd"))
            split("norm", NK, hH[:])
            act.wait_ge(sems["rt_pe"], T.next("rt_pe"))
            act.activation(RT(0), TP[:, 0:64].rearrange("p (t e) -> p t e", t=NT), ACT.Sigmoid).then_inc(sems["rt_sig"], 1)
            act.wait_ge(sems["rt_done"], T.next("rt_done"))
            spread("g2")

            def hid_hi(name):
                def go():
                    for j in range(4):
                        act.wait_ge(sems[BANKS[j]], T.at(BANKS[j]))
                        act.activation(aH[:, j, :], F[:, j % 2, :], ACT.Copy).then_inc(sems[name], 1)
                return go

            def expert(e, more=True):
                def sig():
                    for j in range(4):
                        out(j)
                        act.activation(G[:, j, :], BK[j], ACT.Sigmoid).then_inc(sems["e_sig"], 1)
                blk(sig)
                blk(hid_hi("hid_hi"))
                unit()
                skip_banks()
                unit(None, more)
                skip_banks()
            T.loop(NEXP - 1, expert)
            expert(NEXP - 1, False)
            squares("norm", lambda i: X[:, i, :], NT, "x3")
            act.wait_ge(sems["norm_rd"], T.next("norm_rd"))

            def layer(l):
                hi()
                squares("norm", lambda i: X[:, i, :], NT, "x4")
                act.wait_ge(sems["norm_rd"], T.next("norm_rd"))
                split("norm", NK, hH[:])
                blk(copies(lambda j: TM[:, j, :], UN, 4, "rqk_in"))
                begin2("rv")

                def ret_vg():
                    for j in range(4):
                        out(j)
                        act.activation(ST[1][:, j, 0:256], BK[j][:, 0:256], ACT.Copy)
                        act.activation(SG[:, j, :], BK[j][:, 256:512], ACT.Sigmoid).then_inc(sems["sg_sig"], 1)
                    act.wait_ge(sems["sg_sig"], T.next("sg_sig", 4))
                    act.sem_inc(sems["rv_out"], 1)
                blk(ret_vg)
                begin2("rqk")
                sink("sink", 4, lambda k: ST[0][:, k, :])
                act.sem_inc(sems["rqk_out"], 1)
                blk(copies(lambda j: TM[:, j, 0:384], 384, 4, "lat_in"))
                blk(copies(lambda j: QI[:, j, :]))
                begin2("sqk")
                sink("sink", 3, lambda k: ST[0][:, k, :] if k < 2 else CKT)

                def index_kw():
                    for j in range(4):
                        out(j)
                        act.activation(TM[:, j, 0:64], BK[j][:, 0:64], ACT.Copy)
                        act.activation(TM[:, j, 64:128], BK[j][:, 0:64], ACT.Copy)
                        act.activation(WIX[:, j, :], BK[j][:, 64:72], ACT.Copy,
                                       scale=8 ** -0.5 * 64 ** -0.5).then_inc(sems[BANKS[j]], 1)
                    act.wait_ge(sems[BANKS[3]], T.at(BANKS[3]))
                    act.sem_inc(sems["ki_out"], 1)
                blk(index_kw)
                begin2("sv")
                act.wait_ge(sems["uk_pe"], T.next("uk_pe"))
                act.activation(ST[0][:, 2:4, :], SC[:].rearrange("p (k s) -> p k s", k=2), ACT.Copy)
                act.activation(ST[1][:, :, 0:256], TP[:].rearrange("p (t c) -> p t c", t=NT), ACT.Copy).then_inc(
                    sems["uk_cp"], 1)
                act.wait_ge(sems["uk_cp"], T.next("uk_cp"))
                act.sem_inc(sems["sqk_out"], 1)
                act.sem_inc(sems["sv_out"], 1)
                sink("sink", 1, lambda k: KIT)
                n = 0
                for tt in range(1, NT):
                    nk = (tt + 1) * P
                    for ih in range(8):
                        act.wait_ge(sems["ix_pe"], T.next("ix_pe"))
                        if n >= 2:
                            act.wait_ge(sems["ix_dve"], T.next("ix_dve"))
                        act.activation(F[:, n % 2, 0:nk], SC[:, (n % 2) * 512:(n % 2) * 512 + nk], ACT.Relu).then_inc(
                            sems["ix_act"], 1)
                        n += 1
                act.wait_ge(sems["ix_dve"], T.next("ix_dve", 2))
                begin2("dq")
                blk(copies(lambda j: ST[0][:, j, :], UN, 4, "dq_out"))
                begin2("dk")
                blk(copies(lambda j: ST[1][:, j, :], UN, 4, "dk_out"))
                begin2("dv")
                blk(copies(lambda j: ST[0][:, j, :], UN, 4, "dv_out"), False)
                act.wait_ge(sems["sel_done"], T.next("sel_done"))
                attend(12, lambda tt: (tt + 1) * P, True, PTB_2)
                act.wait_ge(sems["mix_ready"], T.next("mix_ready"))
                hi()
                split("norm", 2, hH[:])
                blk()
                blk()
                squares("norm", lambda i: X[:, i, :], NT, "x5")
                act.wait_ge(sems["norm_rd"], T.next("norm_rd"))
                split("norm", NK, hH[:])

                def chunk(c, more=True):
                    def relu():
                        for j in range(5):
                            if j < 4:
                                out(j)
                                act.activation(G[:, j, :], BK[j], ACT.Relu).then_inc(sems["e_sig"], 1)
                            if j:
                                act.wait_ge(sems[BANKS[j - 1]], T.at(BANKS[j - 1]))
                                act.activation(aH[:, j - 1, :], F[:, (j - 1) % 2, :], ACT.Copy).then_inc(sems["hid_hi"], 1)
                    blk(relu)
                    unit()
                    skip_banks()
                    unit(None, more)
                    skip_banks()
                act.sem_inc(sems["act_paused"], 1)
                T.loop(FF // UN - 1, chunk)
                chunk(FF // UN - 1, False)

            def begin2(name):
                s = [b for n, b, _ in STORES_2 if n == name][0]
                act.wait_ge(sems[f"st_written{s}"], T.next(f"st_written{s}", held[s]))
                held[s] = 16 * [k for n, _, k in STORES_2 if n == name][0]
            if not only_first:
                for s in range(2):
                    act.wait_ge(sems[f"st_written{s}"], T.next(f"st_written{s}", held[s]))
                    T.skip(f"st_written{s}", -16 * [k for n, b, k in STORES_2 if b == s][-1])
                    held[s] = 16 * [k for n, b, k in STORES_2 if b == s][-1]
                T.loop(2, layer)
                squares("norm", lambda i: X[:, i, :], NT, "x4")

        @block.vector
        def _(v):
            T = Tally(v, turns, "dve", {b: 1 for b in BANKS})
            T.n["w_lo"] = 2
            T.n["gemm_done:out"] = 8
            slot = [0]
            link_sem = "dve_self"

            def link(ins):
                ins.then_inc(sems[link_sem], 1)
                v.wait_ge(sems[link_sem], T.next(link_sem))

            def lo():
                s = slot[0]
                slot[0] ^= 1
                v.wait_ge(sems["w_hi"], T.next("w_hi"))
                v.tensor_tensor(WL[s][:], W[s][:], WH[s][:].bitcast(F32), ALU.subtract).then_inc(sems["w_lo"], 1)
                T.skip("w_lo")

            def unit(evac=None, more=True):
                if more:
                    lo()
                if evac is not None:
                    evac()
                T.skip("gemm_done:out", 4)

            def blk(evac=None, more=True):
                unit()
                unit(evac, more)
                skip_banks()

            def skip_banks():
                for b in BANKS:
                    T.skip(b)

            def out(j):
                v.wait_ge(sems["gemm_done"], T.at("gemm_done:out", j + 1))

            def rsqrt(y, m, work):
                link(v.tensor_scalar(y.bitcast(I32), m.bitcast(I32), -0.5, float(0x5F3759DF), ALU.mult, ALU.add))
                for _ in range(3):
                    link(v.scalar_tensor_tensor(work, m, -0.5, y, ALU.mult, ALU.mult))
                    link(v.tensor_tensor(work, work, y, ALU.mult))
                    link(v.scalar_tensor_tensor(y, work, 1.5, y, ALU.add, ALU.mult))

            def stats(src_n, name, nt, dim):
                v.wait_ge(sems[name + "_ss"], T.next(name + "_ss", nt))
                link(v.tensor_scalar(SM[:, 1, 0:nt], SM[:, 0, 0:nt], 1.0 / dim, EPS, ALU.mult, ALU.add))
                rsqrt(SM[:, 2, 0:nt], SM[:, 1, 0:nt], SM[:, 3, 0:nt])
                v.sem_inc(sems[name + "_rd"], 1)

            def normed(name, src, dst, nt):
                stats(src, name, nt, D)
                for i in range(nt):
                    v.tensor_scalar(dst[:, i, :], src(i), SM[:, 2, i:i + 1], None, ALU.mult).then_inc(sems[name + "_xn"], 1)
                v.wait_ge(sems[name + "_xn"], T.next(name + "_xn", nt))

            def split(name, nk, H, L, scale, bias=None, w=S):
                def rest(k):
                    v.wait_ge(sems[name + "_hi"], T.next(name + "_hi"))
                    v.tensor_tensor(L[:, k, :], F[:, k % 2, 0:w], H[:, k, :].bitcast(F32), ALU.subtract).then_inc(
                        sems[name + "_lo"], 1)
                for k in range(nk):
                    v.wait_ge(sems[name + "_tr"], T.next(name + "_tr"))
                    if k >= 2:
                        v.wait_ge(sems[name + "_lo"], T.next(name + "_lo"))
                    src = TP[:, (k % 2) * 512:(k % 2) * 512 + w]
                    if scale is None:
                        ins = v.tensor_copy(F[:, k % 2, 0:w], src)
                    elif bias is None:
                        ins = v.tensor_scalar(F[:, k % 2, 0:w], src, scale(k), None, ALU.mult)
                    else:
                        ins = v.tensor_scalar(F[:, k % 2, 0:w], src, scale(k), bias(k), ALU.mult, ALU.add)
                    ins.then_inc(sems[name + "_free"], 1)
                    if k:
                        rest(k - 1)
                rest(nk - 1)
                v.wait_ge(sems[name + "_lo"], T.next(name + "_lo", 2))

            def rms(x4, nt, nh, gain, hd=HD):
                n = nt * nh
                sq = flat(T1)[:, 0:n * hd].rearrange("p (t h d) -> p t h d", t=nt, h=nh)
                ss = lambda r: SM[:, r, 0:n].rearrange("p (t h) -> p t h", t=nt)
                link(v.tensor_tensor(sq, x4, x4, ALU.mult))
                link(v.tensor_reduce(ss(0), sq, AX.X, ALU.add))
                link(v.tensor_scalar(SM[:, 1, 0:n], SM[:, 0, 0:n], 1.0 / hd, EPS, ALU.mult, ALU.add))
                rsqrt(SM[:, 2, 0:n], SM[:, 1, 0:n], SM[:, 3, 0:n])
                link(v.tensor_tensor(x4, x4, ss(2).unsqueeze(3).to_broadcast([P, nt, nh, hd]), ALU.mult))
                link(v.tensor_tensor(x4, x4, gain.unsqueeze(1).unsqueeze(1).to_broadcast([P, nt, nh, hd]), ALU.mult))

            def rope(x4, nt, nh):
                shp = [P, nt, nh, HD // 2]
                a = flat(T1)[:, 0:nt * nh * HD].rearrange("p (t h d) -> p t h d", t=nt, h=nh)
                b = flat(T2)[:, 0:nt * nh * HD].rearrange("p (t h d) -> p t h d", t=nt, h=nh)
                v.tensor_tensor(a, x4, RC.unsqueeze(2).to_broadcast([P, nt, nh, HD]), ALU.mult)
                v.tensor_tensor(b[:, :, :, 0:HD:2], x4[:, :, :, 1:HD:2], RS[:, :, 0:HD:2].unsqueeze(2).to_broadcast(shp), ALU.mult)
                link(v.tensor_tensor(b[:, :, :, 1:HD:2], x4[:, :, :, 0:HD:2], RS[:, :, 1:HD:2].unsqueeze(2).to_broadcast(shp), ALU.mult))
                link(v.tensor_tensor(x4, a, b, ALU.add))

            heads4 = lambda ap: ap.rearrange("p t (h d) -> p t h d", d=HD)

            v.sem_inc(sems["w_lo"], 2)
            v.sem_inc(sems["gemm_done"], 8)
            for b in BANKS:
                v.sem_inc(sems[b], 1)
            v.sem_inc(sems["yb_used"], 1)
            T.n["yb_used"] = 1
            v.wait_ge(sems["vec_tr"], T.next("vec_tr"))
            v.tensor_copy(VT[:], TP[:, 0:V_ALL])
            link(v.memset(F[0:2, 0, :], 0.0))
            v.tensor_copy(CW[:, :, 0:NTAP], TP[:, 128:256].rearrange("p (j k) -> p j k", j=4)[:, :, 0:NTAP])
            for m in range(2):
                ins = v.tensor_copy(CF[:, 1, :, m], TP[:, V_C + 8 * m:V_C + 8 * m + 8])
            link(ins)
            v.sem_inc(sems["vec_cp"], 1)
            v.wait_ge(sems["cs_sig"], T.next("cs_sig"))
            link(v.tensor_tensor(CF[:, 0, :, :], CF[:, 0, :, :], CF[:, 1, :, :], ALU.mult))
            v.sem_inc(sems["cs_val"], 1)
            v.wait_ge(sems["cs_hi"], T.next("cs_hi"))
            v.tensor_tensor(CSL[:], CF[:, 0, :, :], CSH[:].bitcast(F32), ALU.subtract).then_inc(sems["cs_lo"], 1)
            v.wait_ge(sems["wr_hi"], T.next("wr_hi"))
            v.tensor_tensor(WRL[:], WR, WRH[:].bitcast(F32), ALU.subtract).then_inc(sems["wr_lo"], 1)
            lo()

            normed("norm", lambda i: CTX[i], CTN, NC)
            normed("norm", lambda i: X[:, i, :], XN, NT)
            v.sem_inc(sems["mod_out"], 1)

            def mod_columns(at):
                v.wait_ge(sems["mod_col"], T.next("mod_col"))
                v.tensor_copy(at.rearrange("p a b -> p (a b)"), TP[:, 0:8]).then_inc(sems["mod_out"], 1)

            def mod(i):
                lo()
                mod_columns(MODP[:, bass.ds(i * 4, 4), :])
                lo()
                T.skip("gemm_done:out", 8)
                T.skip("bank_free0")
            T.loop(12, mod)
            mod_columns(MODP[:, 48:52, :])
            v.wait_ge(sems["mod_out"], T.next("mod_out", 14))
            v.sem_inc(sems["mod_done"], 1)
            link(v.tensor_tensor(MOD, MOD, VT[:, V_BMOD:V_N1].unsqueeze(2).to_broadcast([P, 48, 2]), ALU.add))
            for r, c0, m, g in ((0, 8, 0, V_N1), (1, 8, 1, V_N1), (2, 32, 0, V_N2)):
                ins = v.scalar_tensor_tensor(AF[:, r, :], MOD[:, c0:c0 + 8, m], 1.0, VT[:, g:g + 8], ALU.add, ALU.mult)
            link(ins)
            split("norm", NK, cH, cL, lambda k: AF[:, 1, k:k + 1], lambda k: MOD[:, k, 1:2], C)
            split("norm", NK, hH[:], hL[:], lambda k: AF[:, 0, k:k + 1], lambda k: MOD[:, k, 0:1])
            v.wait_ge(sems["tab_landed"], T.next("tab_landed", 16 * 7))
            blk()
            v.wait_ge(sems["ck_in"], T.next("ck_in"))
            rms(heads4(TM[:, 0:NC, 0:P]), NC, 2, GK)
            v.sem_inc(sems["ck_rms"], 1)
            blk()
            blk()
            blk()
            v.wait_ge(sems["q_in"], T.next("q_in"))
            unit()
            rms(heads4(TM), NT, 8, GQ)
            unit()
            skip_banks()
            rope(heads4(TM), NT, 8)
            v.sem_inc(sems["q_rope"], 1)
            blk()
            v.wait_ge(sems["k_in"], T.next("k_in"))
            rms(heads4(TM[:, :, 0:P]), NT, 2, GK)
            rope(heads4(TM[:, :, 0:P]), NT, 2)
            v.sem_inc(sems["k_rope"], 1)
            for _ in range(4):
                blk()

            def conv_in():
                for j in range(4):
                    out(j)
                    v.tensor_tensor(Z[:, j, PADT:PADT + S], BK[j], CT[:, j, :], ALU.mult).then_inc(sems[BANKS[j]], 1)
                v.wait_ge(sems[BANKS[3]], T.at(BANKS[3]))
                v.sem_inc(sems["z_ready"], 1)
            v.wait_ge(sems["rpb_stored"], T.at("rpb_stored", 16 * 8))
            link(v.memset(Z[:], 0.0))
            blk(conv_in, False)

            def attend(count, keys, bias, put_out, load_incs, other=None, beside=None):
                def remainders(s):
                    nk = keys(NT - 1)
                    v.wait_ge(sems["head_hi"], T.next("head_hi"))
                    v.tensor_tensor(QX[s][HD:P, :], QS[s][HD:P, :], QX[s][HD:P, :].bitcast(F32), ALU.subtract)
                    v.tensor_tensor(KL[s][:, 0:nk], KS[s][0:HD, 0:nk], KX[s][0:HD, 0:nk].bitcast(F32),
                                    ALU.subtract).then_inc(sems["head_lo"], 1)

                def top(n, bias):
                    nk = keys(n % NT)
                    if n % NT == 0 and load_incs:
                        v.wait_ge(sems[f"bias_landed{n // NT}"], T.next(f"bias_landed{n // NT}", load_incs))
                    v.wait_ge(sems["head_s"], T.next("head_s"))
                    c = n % 2
                    if bias is None:
                        link(v.tensor_reduce(MX[:, c:c + 1], SCS[c][:, 0:nk], AX.X, ALU.max))
                    else:
                        v.sem_inc(sems["v_paused"], 1)
                        bias(n // NT, n % NT, SCS[c], SB[c], MX[:, c:c + 1])
                    v.tensor_scalar(NM[:, c:c + 1], MX[:, c:c + 1], -SCALE, None, ALU.mult).then_inc(
                        sems["head_nm"], 1)


                def normalise(n):
                    c, nk = n % 2, keys(n % NT)
                    v.wait_ge(sems["head_exp"], T.next("head_exp"))
                    link(v.reciprocal(RD[:, c:c + 1], DEN[:, c:c + 1]))
                    v.tensor_scalar(PR[c][:, 0:nk], PR[c][:, 0:nk], RD[:, c:c + 1], None, ALU.mult).then_inc(
                        sems["head_pn"], 1)

                def put(i, s):
                    v.wait_ge(sems["head_o"], T.next("head_o"))
                    put_out(i, s)

                def body(i, first, last, bias, bias_next):
                    for n in range(2 * NT):
                        s, tt = n // NT, n % NT
                        if n + 1 < 2 * NT or not last:
                            top((n + 1) % (2 * NT), bias if n + 1 < 2 * NT else bias_next)
                        normalise(n)
                        if beside:
                            beside(i, n)
                        if tt == 1:
                            if not (last and s == 1):
                                remainders(1 - s)
                            if s == 1:
                                put(i, 0)
                            elif not first:
                                put(i - 1, 1)
                v.wait_ge(sems["w_lo"], T.at("w_lo", 0))
                v.sem_inc(sems["head_go"], 1)
                v.sem_inc(sems["head_oe"], 2)
                T.skip("head_o", 2)
                remainders(0)
                top(0, bias)
                if other is None:
                    body(0, True, False, bias, bias)
                else:
                    body(0, True, False, bias, bias)
                    body(1, False, False, bias, other)
                    bias = other
                done = 1 if other is None else 2
                v.sem_inc(sems["v_paused"], 1)
                T.loop(count // 2 - 1 - done, lambda i: body(i + done, False, False, bias, bias))
                body(count // 2 - 1, False, True, bias, bias)
                put(count // 2 - 1, 1)
                T.skip("head_oe", count + 2)
                v.wait_ge(sems["head_oe"], T.at("head_oe", 0))

            def to_stage(b):
                def go(i, s):
                    v.tensor_copy(ST[b][s * HD:(s + 1) * HD, bass.ds(i, 1), :].rearrange("p a q -> p (a q)"),
                                  OT[s]).then_inc(sems["head_oe"], 1)
                return go

            v.wait_ge(sems["fo_b"], T.next("fo_b", 4))
            v.wait_ge(sems["st_written1"], T.at("st_written1", stored(STORES_1, 1, "nv")))

            def conv_tap(i, n):
                j = n % 2
                x, w = Z[:, j, bass.ds(i * 4 + n // 2, S)], CW[:, j, bass.ds(i * 4 + n // 2, 1)]
                if isinstance(i, int) and i == 0 and n < 2:
                    link(v.tensor_scalar(CD[:, j, :], x, w, None, ALU.mult))
                else:
                    link(v.scalar_tensor_tensor(CD[:, j, :], x, w, CD[:, j, :], ALU.mult, ALU.add))
            attend(8, lambda tt: KEYS, None, to_stage(1), 0, beside=conv_tap)
            v.sem_inc(sems["gqa_out"], 1)

            def add_max(dst, sc, add, most):
                return v.tensor_tensor_reduce(dst, sc, add, 1.0, TAKEN, ALU.add, ALU.max, most)

            link(v.memset(RNW[:], 0.0))

            def na_bias(s, tt, sc, sb, most):
                if tt == 0:
                    link(v.scalar_tensor_tensor(ES[s][:], ES[s][:], 1 / SCALE,
                                                MSK[:].unsqueeze(1).to_broadcast([P, 14, 64]), ALU.mult, ALU.add))
                    v.sem_inc(sems["v_paused"], 1)
                j0 = 2 * (NT - 1 - tt)
                add_max(sb[:, 0:S], sc[:, 0:S], flat(ES[s][:, j0:j0 + 8, :]), MXC[:, 0:1])
                link(add_max(sb[:, S:KEYS], sc[:, S:KEYS], RNW[:], MXC[:, 1:2]))
                link(v.tensor_tensor(most, MXC[:, 0:1], MXC[:, 1:2], ALU.max))
            v.wait_ge(sems["st_written0"], T.at("st_written0", stored(STORES_1, 0, "fourier")))
            attend(8, lambda tt: KEYS, na_bias, to_stage(0), 16 * 2)
            v.sem_inc(sems["na_out"], 1)
            v.memset(BV[:, 0:6, :], 0.0)
            v.memset(ONE, 1.0)
            lo()
            v.wait_ge(sems["conv_done"], T.next("conv_done"))
            for j in range(4):
                b = VT[:, V_CB + j:V_CB + j + 1]
                if j < 2:
                    ins = v.scalar_tensor_tensor(CU[:, j, :], CU[:, j, :], b, CD[:, j, :], ALU.add, ALU.add)
                else:
                    ins = v.tensor_scalar(CU[:, j, :], CU[:, j, :], b, None, ALU.add)
            link(ins)
            v.tensor_tensor(CT, CU, CU, ALU.mult).then_inc(sems["cv_sq"], 1)
            v.wait_ge(sems["cv_pe"], T.next("cv_pe"))
            link(v.tensor_scalar(F[:, 0, :], SC[:, 0:512], 1.0 / 512, EPS, ALU.mult, ALU.add))
            v.sem_inc(sems["cv_r"], 1)
            rsqrt(F[:, 1, :], F[:, 0, :], AT[:, 0:512])
            for j in range(4):
                ins = v.scalar_tensor_tensor(CU[:, j, :], CU[:, j, :], VT[:, V_CG + j:V_CG + j + 1], F[:, 1, :],
                                             ALU.mult, ALU.mult)
            link(ins)
            v.sem_inc(sems["cv_n"], 1)
            v.memset(CD, 0.0)
            v.wait_ge(sems["cv_sig"], T.next("cv_sig"))
            link(v.tensor_tensor(CY, CU, CT, ALU.mult))
            v.sem_inc(sems["cv_out"], 1)
            v.sem_inc(sems["g_free"], 1)

            def branch(i):
                blk()
                v.wait_ge(sems["yb_hi"], T.next("yb_hi"))
                v.tensor_tensor(aL[:], ST[1][:], aH[:].bitcast(F32), ALU.subtract).then_inc(sems["yb_used"], 1)
                blk()
                for hb in range(2):
                    def go():
                        for j in range(4):
                            out(j)
                            v.tensor_tensor(F[:, j % 2, :], BK[j], G[:, hb * 4 + j, :], ALU.mult).then_inc(
                                sems[BANKS[j]], 1)
                            v.wait_ge(sems[BANKS[j]], T.at(BANKS[j]))
                            link(v.tensor_tensor(BV[:, hb * 4 + j, :], BV[:, hb * 4 + j, :], F[:, j % 2, :], ALU.add))
                    unit(go)
                    skip_banks()
            T.loop(4, branch)
            v.sem_inc(sems["m_go"], 1)

            def spread(name, c0):
                link(v.tensor_copy(flat(ST[0][:])[:, 0:D].rearrange("p (k c) -> p k c", k=NK),
                                   MOD[:, c0:c0 + NK, 0].unsqueeze(2).to_broadcast([P, NK, P])))
                v.sem_inc(sems[name + "_in"], 1)
            spread("g1", 16)
            for k in range(NK):
                v.wait_ge(sems["norm_hi"], T.next("norm_hi"))
                v.tensor_tensor(hL[:, k, :], BV[:, k, :], hH[:, k, :].bitcast(F32), ALU.subtract).then_inc(sems["norm_lo"], 1)
            v.wait_ge(sems["g1_gb"], T.next("g1_gb"))

            def add_x(hb, gain, ready=None):
                def go():
                    for j in range(4):
                        if ready and j:
                            v.sem_inc(sems[ready], 1)
                        xs = X[:, j, hb * UN:(hb + 1) * UN]
                        out(j)
                        if gain:
                            v.tensor_tensor(F[:, j % 2, :], BK[j], GB[:, hb * UN:(hb + 1) * UN], ALU.mult).then_inc(
                                sems[BANKS[j]], 1)
                            v.wait_ge(sems[BANKS[j]], T.at(BANKS[j]))
                            link(v.tensor_tensor(xs, xs, F[:, j % 2, :], ALU.add))
                        else:
                            v.tensor_tensor(xs, xs, BK[j], ALU.add).then_inc(sems[BANKS[j]], 1)
                            if ready:
                                v.wait_ge(sems[BANKS[j]], T.at(BANKS[j]))
                    if ready:
                        v.sem_inc(sems[ready], 1)
                return go
            blk(add_x(0, True))
            blk(add_x(1, True, "x2"))
            v.wait_ge(sems["norm_lo"], T.next("norm_lo", NK))
            normed("norm", lambda i: X[:, i, :], XN, NT)
            split("norm", NK, hH[:], hL[:], lambda k: AF[:, 2, k:k + 1], lambda k: MOD[:, 24 + k, 0:1])
            v.memset(BIG[:], 0.0)

            spread("g2", 40)

            v.wait_ge(sems["rt_sig"], T.next("rt_sig"))
            s_, sel, tmp, eq, onehot, ing = RT(0), RT(1), RT(2), RT(3), RT(4), RT(5)
            link(v.tensor_tensor(sel, s_, RB[:].unsqueeze(1).to_broadcast([P, NT, NEXP]), ALU.add))
            g5 = sel.rearrange("p t (g x y) -> p (t g) x y", g=4, x=2)
            mx2, mn2 = RT2(0, 8).rearrange("p t (g x) -> p (t g) x", x=2), RT2(1, 8).rearrange("p t (g x) -> p (t g) x", x=2)
            v.tensor_tensor(mx2, g5[:, :, :, 0], g5[:, :, :, 1], ALU.max)
            link(v.tensor_tensor(mn2, g5[:, :, :, 0], g5[:, :, :, 1], ALU.min))
            ga, gb2, gs = (RT2(n, 4).rearrange("p t g -> p (t g)") for n in (2, 3, 4))
            v.tensor_tensor(ga, mx2[:, :, 0], mx2[:, :, 1], ALU.max)
            link(v.tensor_tensor(gb2, mx2[:, :, 0], mx2[:, :, 1], ALU.min))
            link(v.tensor_tensor(gs, mn2[:, :, 0], mn2[:, :, 1], ALU.max))
            link(v.tensor_tensor(gb2, gb2, gs, ALU.max))
            link(v.tensor_tensor(ga, ga, gb2, ALU.add))

            def first_max(vals, n, hot, work, mxt):
                bc = mxt.unsqueeze(2).to_broadcast([P, NT, n])
                link(v.tensor_reduce(mxt, vals, AX.X, ALU.max))
                link(v.tensor_tensor(work, vals, bc, ALU.is_ge))
                link(v.tensor_tensor(work, work, DESC[:, 0:n].unsqueeze(1).to_broadcast([P, NT, n]), ALU.mult))
                link(v.tensor_reduce(mxt, work, AX.X, ALU.max))
                link(v.tensor_tensor(hot, work, bc, ALU.is_ge))
            DESC = SM[:, 3, 0:NEXP]
            for e in range(NEXP):
                ins = v.memset(SM[:, 3, e:e + 1], float(NEXP - e))
            link(ins)
            mxt = SM[:, 3, NEXP:NEXP + NT]
            gv = RT2(2, 4)
            first_max(gv, 4, RT2(4, 4), RT2(3, 4), mxt)
            link(v.tensor_copy(ing.rearrange("p t (g x) -> p (t g) x", x=4),
                               RT2(4, 4).rearrange("p t g -> p (t g)").unsqueeze(2).to_broadcast([P, 16, 4])))
            link(v.tensor_tensor(sel, sel, ing, ALU.mult))
            link(v.tensor_scalar(ing, ing, -1.0, BIG_E, ALU.add, ALU.mult))
            link(v.tensor_tensor(sel, sel, ing, ALU.add))
            first_max(sel, NEXP, onehot, tmp, mxt)
            link(v.scalar_tensor_tensor(sel, onehot, -3.0e30, sel, ALU.mult, ALU.add))
            first_max(sel, NEXP, eq, tmp, mxt)
            link(v.tensor_tensor(onehot, onehot, eq, ALU.add))
            link(v.tensor_tensor(s_, s_, onehot, ALU.mult))
            link(v.tensor_reduce(mxt, s_, AX.X, ALU.add))
            link(v.reciprocal(SM[:, 3, 20:24], mxt))
            link(v.tensor_tensor(GATE[:], s_, SM[:, 3, 20:24].unsqueeze(2).to_broadcast([P, NT, NEXP]), ALU.mult))
            v.sem_inc(sems["rt_done"], 1)
            v.wait_ge(sems["g2_gb"], T.next("g2_gb"))

            def hidden(make):
                def rest(j):
                    v.wait_ge(sems["hid_hi"], T.next("hid_hi"))
                    v.tensor_tensor(aL[:, j, :], F[:, j % 2, :], aH[:, j, :].bitcast(F32), ALU.subtract).then_inc(
                        sems["hid_lo"], 1)

                def go():
                    for j in range(4):
                        out(j)
                        if j >= 2:
                            v.wait_ge(sems["hid_lo"], T.next("hid_lo"))
                        make(F[:, j % 2, :], j).then_inc(sems[BANKS[j]], 1)
                        if j:
                            rest(j - 1)
                    rest(3)
                    v.wait_ge(sems["hid_lo"], T.next("hid_lo", 2))
                return go

            def expert(e, more=True):
                def gate_half():
                    for j in range(4):
                        v.wait_ge(sems["e_sig"], T.next("e_sig"))
                        v.tensor_tensor(G[:, 4 + j, :], BK[j], G[:, j, :], ALU.mult).then_inc(sems[BANKS[j]], 1)
                blk(gate_half)

                blk(hidden(lambda dst, j: v.tensor_tensor(dst, BK[j], G[:, 4 + j, :], ALU.mult)))
                for hf in range(2):
                    def down():
                        for j in range(4):
                            out(j)
                            acc = XN[:, j, hf * UN:(hf + 1) * UN]
                            v.scalar_tensor_tensor(acc, BK[j], GATE[:, j, bass.ds(e, 1)], acc, ALU.mult,
                                                   ALU.add).then_inc(sems[BANKS[j]], 1)
                    unit(down, more or hf == 0)
                    skip_banks()
            T.loop(NEXP - 1, expert)
            expert(NEXP - 1, False)
            for b in BANKS:
                v.wait_ge(sems[b], T.at(b, 0))
            for i in range(NT):
                link(v.tensor_tensor(XN[:, i, :], XN[:, i, :], GB, ALU.mult))
                link(v.tensor_tensor(X[:, i, :], X[:, i, :], XN[:, i, :], ALU.add))
                v.sem_inc(sems["x3"], 1)

            def final(name, dst, ready):
                stats(None, name, NT, D)
                v.wait_ge(sems["gf_landed"], T.next("gf_landed", 16))
                for i in range(NT):
                    ins = v.scalar_tensor_tensor(dst(i), X[:, i, :], SM[:, 2, i:i + 1], GF, ALU.mult, ALU.mult)
                    link(ins)
                    v.sem_inc(sems[ready], 1)

            if only_first:
                final("norm", lambda i: XN[:, i, :], "out_ready")
                return
            final("norm", lambda i: X[:, i, :], "x4")
            v.sem_inc(sems["es_free"], 1)

            def layer(l):
                lo()
                link(v.tensor_copy(AF[:, 3, :], VT[:, bass.ds(l * 8 + V_ATT, 8)]))
                normed("norm", lambda i: X[:, i, :], XN, NT)
                split("norm", NK, hH[:], hL[:], lambda k: AF[:, 3, k:k + 1])
                v.wait_ge(sems["lay_landed"], T.next("lay_landed", 16 * 6))
                blk()
                v.wait_ge(sems["rqk_in"], T.next("rqk_in"))
                x16 = TM.rearrange("p t (h d) -> p t h d", d=32)
                a16 = T1.rearrange("p t (h d) -> p t h d", d=32)
                x4, a4, b4 = (q.rearrange("p t (h x d) -> p t h x d", x=2, d=32) for q in (TM, T1, T2))
                shp = [P, NT, 8, 32]
                ts = TS.unsqueeze(2).to_broadcast(shp)
                v.tensor_tensor(a16, x16, TC.unsqueeze(2).to_broadcast([P, NT, 16, 32]), ALU.mult)
                v.tensor_tensor(b4[:, :, :, 0, :], x4[:, :, :, 1, :], ts, ALU.mult)
                link(v.tensor_tensor(b4[:, :, :, 1, :], x4[:, :, :, 0, :], ts, ALU.mult))
                v.tensor_tensor(x4[:, :, :, 0, :], a4[:, :, :, 0, :], b4[:, :, :, 0, :], ALU.subtract)
                link(v.tensor_tensor(x4[:, :, :, 1, :], a4[:, :, :, 1, :], b4[:, :, :, 1, :], ALU.add))
                v.sem_inc(sems["rqk_rope"], 1)

                def ret_gate():
                    for j in range(4):
                        v.wait_ge(sems["sg_sig"], T.next("sg_sig"))
                        v.tensor_tensor(SG[:, j, :], BK[j][:, 256:512], SG[:, j, :], ALU.mult).then_inc(sems[BANKS[j]], 1)
                blk(ret_gate)
                blk()
                v.wait_ge(sems["lat_in"], T.next("lat_in"))
                rms(TM[:, :, 256:384].unsqueeze(2), NT, 1, KNW, P)
                v.sem_inc(sems["lat_rms"], 1)
                blk()
                blk()
                v.tensor_copy(SEL[:, 0, 0:P], CM[:])
                n = 0
                for tt in range(1, NT):
                    nk = (tt + 1) * P
                    for ih in range(8):
                        v.wait_ge(sems["ix_act"], T.next("ix_act"))
                        w = WIX[:, tt, ih:ih + 1]
                        if ih == 0:
                            ins = v.tensor_scalar(IX[tt], F[:, n % 2, 0:nk], w, None, ALU.mult)
                        else:
                            ins = v.scalar_tensor_tensor(IX[tt], F[:, n % 2, 0:nk], w, IX[tt], ALU.mult, ALU.add)
                        ins.then_inc(sems["ix_dve"], 1)
                        v.wait_ge(sems["ix_dve"], T.next("ix_dve"))
                        n += 1
                    link(v.tensor_tensor(IX[tt][:, nk - P:nk], IX[tt][:, nk - P:nk], CM[:], ALU.add))

                def top_rounds(tt, n=NSEL // 16):
                    for r in range(n):
                        v.sem_inc(sems["v_paused"], 1)
                        link(v.max(TOP[:], IX[tt]))
                        v.sem_inc(sems["v_paused"], 1)
                        link(v.match_replace(IX[tt], TOP[:], IX[tt], TAKEN))

                def selected(tt):
                    link(v.tensor_scalar(IX[tt], IX[tt], 0.5 * TAKEN, NEG, ALU.is_gt, ALU.mult))
                for tt in range(1, NT):
                    for half in range(2):
                        unit(None, tt < NT - 1 or half == 0)
                        if tt < NT - 1 or half == 0:
                            top_rounds(tt)
                    skip_banks()
                    if tt < NT - 1:
                        selected(tt)
                v.sem_inc(sems["sel_done"], 1)

                def ret(i):
                    for s in range(2):
                        for kt in range(NT):
                            n = S - kt * P
                            v.wait_ge(sems["ret_s"], T.next("ret_s"))
                            bank = SC if kt % 2 == 0 else TP
                            v.tensor_tensor(RP[:, kt, 0:n], bank[:, 0:n], flat(ES[s][:])[:, 0:n], ALU.mult).then_inc(
                                sems["ret_d"], 1)
                        top_rounds(NT - 1, NSEL // 64)
                        for tt in range(NT):
                            v.wait_ge(sems["ret_o"], T.next("ret_o"))
                            v.tensor_copy(XN[:, tt, bass.ds(i * (2 * HD) + s * HD, HD)], OB[tt % 2]).then_inc(
                                sems["ret_oe"], 1)
                v.sem_inc(sems["v_paused"], 1)
                T.loop(2, ret)
                T.skip("ret_oe", 4 * NT)
                selected(NT - 1)
                v.wait_ge(sems["ret_oe"], T.at("ret_oe", 0))
                o4 = XN[:, :, 0:256].rearrange("p t (h d) -> p t h d", h=4)
                sq = flat(T2)[:, 0:NT * 256].rearrange("p (t h d) -> p t h d", t=NT, h=4)
                st = lambda r: SM[:, r, 0:16].rearrange("p (t h) -> p t h", t=NT)
                bc = lambda r: st(r).unsqueeze(3).to_broadcast([P, NT, 4, HD])
                link(v.tensor_reduce(st(0), o4, AX.X, ALU.add))
                link(v.tensor_scalar(SM[:, 1, 0:16], SM[:, 0, 0:16], 1.0 / HD, None, ALU.mult))
                link(v.tensor_tensor(o4, o4, bc(1), ALU.subtract))
                link(v.tensor_tensor(sq, o4, o4, ALU.mult))
                link(v.tensor_reduce(st(0), sq, AX.X, ALU.add))
                link(v.tensor_scalar(SM[:, 1, 0:16], SM[:, 0, 0:16], 1.0 / HD, EPS, ALU.mult, ALU.add))
                rsqrt(SM[:, 2, 0:16], SM[:, 1, 0:16], SM[:, 3, 0:16])
                link(v.tensor_tensor(o4, o4, bc(2), ALU.mult))
                link(v.tensor_tensor(XN[:, :, 0:256], XN[:, :, 0:256], RNW[:].unsqueeze(1).to_broadcast([P, NT, 256]), ALU.mult))
                link(v.tensor_tensor(XN[:, :, 0:256], XN[:, :, 0:256], SG, ALU.mult))

                def biased(src):
                    def go(s, tt, sc, sb, most):
                        nk = (tt + 1) * P
                        link(add_max(sb[:, 0:nk], sc[:, 0:nk], src(tt, nk), most))
                    return go

                def to_split(k0):
                    def go(i, s):
                        part = lambda ap: ap[s * HD:(s + 1) * HD, bass.ds(i + k0, 1), :].rearrange("p a q -> p (a q)")
                        link(v.tensor_copy(part(hH), OT[s]))
                        v.tensor_tensor(part(hL), OT[s], part(hH).bitcast(F32), ALU.subtract).then_inc(sems["head_oe"], 1)
                    return go
                v.wait_ge(sems["xb_landed"], T.next("xb_landed", 16))
                attend(12, lambda tt: (tt + 1) * P, biased(lambda tt, nk: SEL[:, tt, 0:nk]), to_split(2), 0,
                       biased(lambda tt, nk: XB[:, S - nk:S]))
                v.sem_inc(sems["mix_ready"], 1)
                lo()
                v.sem_inc(sems["es_free"], 1)
                split("norm", 2, hH[:], hL[:], None)
                blk(add_x(0, False))
                blk(add_x(1, False, "x5"))
                link(v.tensor_copy(AF[:, 3, :], VT[:, bass.ds(l * 8 + V_MLP, 8)]))
                normed("norm", lambda i: X[:, i, :], XN, NT)
                split("norm", NK, hH[:], hL[:], lambda k: AF[:, 3, k:k + 1])

                def chunk(c, more=True):
                    def relu_squared(dst, j):
                        v.wait_ge(sems["e_sig"], T.next("e_sig"))
                        return v.tensor_tensor(dst, BK[j], G[:, j, :], ALU.mult)
                    blk(hidden(relu_squared))
                    for hf in range(2):
                        unit(add_x(hf, False, None if more or hf == 0 else "x4"), more or hf == 0)
                        skip_banks()
                v.sem_inc(sems["v_paused"], 1)
                T.loop(FF // UN - 1, chunk)
                chunk(FF // UN - 1, False)
            T.loop(2, layer)
            final("norm", lambda i: XN[:, i, :], "out_ready")


def tables():
    f = np.float32
    tok = np.arange(S)
    inv = 10000.0 ** (-np.arange(16) / 16.0)
    ang = np.concatenate([(tok // 64)[:, None] * inv, (tok % 64)[:, None] * inv], -1)
    tiles = lambda a: np.ascontiguousarray(a.reshape(NT, P, -1).transpose(1, 0, 2).astype(f))
    sign = np.where(np.arange(HD) % 2 == 0, -1.0, 1.0)
    inv2 = 10000.0 ** (-np.arange(32) / 32.0)
    ang2 = tok[:, None] * inv2
    col = np.arange(64)
    start = np.clip(col - 8, 0, 48)
    ok = (col[None, :] >= start[:, None]) & (col[None, :] < start[:, None] + 16)
    mask = np.where(ok, 0.0, NEG)
    diff = np.arange(P)[:, None] - np.arange(S)[None, :] + (S - P)
    count = ((diff >= 0) & (diff <= 128)).astype(int) + ((diff >= 0) & (diff % 4 == 0)) + ((diff >= 0) & (diff % 16 == 0))
    dil = np.where(count > 0, np.log(np.maximum(count, 1)), NEG)
    m = np.arange(S)[None, :] - np.arange(P)[:, None]
    lg = np.log(1.0 - 2.0 ** (-5.0 - np.arange(4)))
    decay = np.exp(np.maximum(m, 0)[None] * lg[:, None, None]) * (m >= 0)[None] * SCALE
    al = 2 * np.pi * ((tok[:, None] * tok[None, :]) % S) / S
    g = np.arange(P)
    ag = 2 * np.pi * ((g[:, None] * g[None, :]) % P) / P
    return {
        "k_ident": np.eye(P, dtype=f),
        "k_ropec": tiles(np.repeat(np.cos(ang), 2, -1)),
        "k_ropes": tiles(np.repeat(np.sin(ang), 2, -1) * sign),
        "k_colmask": np.concatenate([mask, mask], 0).astype(f),
        "k_causal": np.where(g[None, :] <= g[:, None], 0.0, NEG).astype(f),
        "k_dilbias": (dil / SCALE).astype(f),
        "k_decay": decay.astype(f),
        "k_retc": tiles(np.cos(ang2)),
        "k_rets": tiles(np.sin(ang2)),
        "k_dftc": (np.cos(al) / np.sqrt(S)).astype(f),
        "k_dfts": (np.sin(al) / np.sqrt(S)).astype(f),
        "k_dftg": (np.concatenate([np.cos(ag), -np.sin(ag)], 1) / np.sqrt(P)).astype(f),
    }


_INS = ["x", "c", "ctx", "c_ctx", "w_mod", "b_mod", "norm1_g", "norm2_g", "w_in", "q_norm_g", "k_norm_g", "na_rpb",
        "conv_w", "conv_b", "conv_norm_g", "w_branch", "w_out", "w_router", "router_bias", "w_expert_gu",
        "w_expert_down", "final_norm_g", "attn_norm_w_2", "w_in_2", "ret_norm_w_2", "dsa_kv_norm_w_2", "dsa_w_uk_2",
        "dsa_w_uv_2", "w_out_2", "mlp_norm_w_2", "w_up_2", "w_down_2", "final_norm_w_2"]
ONLY_FIRST = False


def kernel(**inputs):
    import numpy as _np
    import concourse.bacc as _bacc
    from concourse import mybir as _mybir
    from concourse.bass_utils import run_bass_kernel_spmd as _run

    arrays = {f"in_{n}_dram": _np.ascontiguousarray(inputs[n]) for n in _INS}
    arrays.update({f"in_{n}_dram": a for n, a in tables().items()})
    turns = {}
    for _ in range(2):
        nc = _bacc.Bacc("TRN2", target_bir_lowering=False, num_devices=1)
        t = {n[3:-5]: nc.dram_tensor(n, a.shape, _mybir.dt.from_np(a.dtype), kind="ExternalInput").ap()
             for n, a in arrays.items()}
        out = nc.dram_tensor("out_0_dram", (1, S, D), _mybir.dt.float32, kind="ExternalOutput").ap()
        program(nc, t, out, turns, ONLY_FIRST)
    r = _run(nc, [arrays], core_ids=[0])
    return r.results[0]["out_0_dram"]
```
